# Optimizing a Trainium2 kernel written in Bass

```python
import jax, jax.numpy as jnp
from jax import lax
import numpy as np

D_MODEL = 1024
BATCH = 1
SEQ = 1024
DEPTH = 1

CTX_LEN = 256
GRID_W = 64
N_HEADS = 16
N_KV_HEADS = 4
HEAD_DIM = 64
Q_GROUP = N_HEADS // N_KV_HEADS
WINDOW = 128
BLOCK = 128
N_FOURIER_GROUPS = 4
FOURIER_GROUP_DIM = 128
FOURIER_WIDTH = N_FOURIER_GROUPS * FOURIER_GROUP_DIM
D_FF = 2816
ROPE_BASE = 10000.0
AXIS_ROT_DIM = HEAD_DIM // 2
N_MOD = 9
RMS_EPS = 1e-6
NEG_INF = -1e30

ATTN_Q_W = N_HEADS * HEAD_DIM
ATTN_KV_W = N_KV_HEADS * HEAD_DIM
Q_OFF = 0
K_OFF = Q_OFF + ATTN_Q_W
V_OFF = K_OFF + ATTN_KV_W
U_OFF = V_OFF + ATTN_KV_W
GA_OFF = U_OFF + FOURIER_WIDTH
GF_OFF = GA_OFF + D_MODEL
D_IN = GF_OFF + D_MODEL

kernel_name = "hybrid_dit_window_gqa_fnet_macaron"

def rms_norm(x, g):
    xf = x.astype(jnp.float32)
    y = xf * lax.rsqrt(jnp.mean(xf * xf, axis=-1, keepdims=True) + RMS_EPS)
    return (y * g.astype(jnp.float32)).astype(x.dtype)

def mod_vec(mod, idx):
    return mod[:, idx][:, None, :]

def adaln_norm(x, g, mod, base):
    h = rms_norm(x, g)
    return h * (1.0 + mod_vec(mod, base + 1)) + mod_vec(mod, base)

def swiglu(h, w_in, w_out):
    hu = h @ w_in
    a, u = hu[..., :D_FF], hu[..., D_FF:]
    return (jax.nn.silu(a) * u) @ w_out

def macaron_ffn(x, mod, base, g, w_in, w_out):
    h = adaln_norm(x, g, mod, base)
    return x + 0.5 * mod_vec(mod, base + 2) * swiglu(h, w_in, w_out)

def axial_rope_angles(n_tokens):
    rows = n_tokens // GRID_W
    row = jnp.repeat(jnp.arange(rows, dtype=jnp.float32), GRID_W)
    col = jnp.tile(jnp.arange(GRID_W, dtype=jnp.float32), rows)
    inv_freq = ROPE_BASE ** (-jnp.arange(0, AXIS_ROT_DIM, 2, dtype=jnp.float32) / AXIS_ROT_DIM)
    ang = jnp.concatenate([row[:, None] * inv_freq, col[:, None] * inv_freq], axis=-1)
    return jnp.cos(ang), jnp.sin(ang)

def apply_rope(x, cos, sin):
    xp = x.reshape(x.shape[:-1] + (HEAD_DIM // 2, 2))
    xe, xo = xp[..., 0], xp[..., 1]
    c = cos[None, :, None, :].astype(x.dtype)
    s = sin[None, :, None, :].astype(x.dtype)
    out = jnp.stack([xe * c - xo * s, xe * s + xo * c], axis=-1)
    return out.reshape(x.shape)

def split_projection(p):
    b, n = p.shape[:2]
    q = p[..., Q_OFF:K_OFF].reshape(b, n, N_HEADS, HEAD_DIM)
    k = p[..., K_OFF:V_OFF].reshape(b, n, N_KV_HEADS, HEAD_DIM)
    v = p[..., V_OFF:U_OFF].reshape(b, n, N_KV_HEADS, HEAD_DIM)
    u = p[..., U_OFF:GA_OFF]
    ga = p[..., GA_OFF:GF_OFF]
    gf = p[..., GF_OFF:D_IN]
    return q, k, v, u, ga, gf

def windowed_attention_with_context(q, k, v, k_ctx, v_ctx, sink):
    b, n = q.shape[:2]
    n_ctx = k_ctx.shape[1]
    nb = n // BLOCK
    scale = HEAD_DIM ** -0.5
    qb = (q * scale).reshape(b, nb, BLOCK, N_KV_HEADS, Q_GROUP, HEAD_DIM).transpose(1, 0, 2, 3, 4, 5)
    pad = ((0, 0), (BLOCK, BLOCK), (0, 0), (0, 0))
    k_pad = jnp.pad(k, pad)
    v_pad = jnp.pad(v, pad)
    sink_b = jnp.broadcast_to(sink.astype(jnp.float32).reshape(1, N_KV_HEADS, Q_GROUP, 1, 1),
                              (b, N_KV_HEADS, Q_GROUP, BLOCK, 1))

    def block(args):
        i, qi = args
        start = i * BLOCK
        kb = lax.dynamic_slice_in_dim(k_pad, start, 3 * BLOCK, axis=1)
        vb = lax.dynamic_slice_in_dim(v_pad, start, 3 * BLOCK, axis=1)
        qpos = start + jnp.arange(BLOCK)
        kpos = start - BLOCK + jnp.arange(3 * BLOCK)
        valid = (jnp.abs(qpos[:, None] - kpos[None, :]) <= WINDOW) & (kpos[None, :] >= 0) & (kpos[None, :] < n)
        s_loc = jnp.einsum('bqkgd,bskd->bkgqs', qi, kb).astype(jnp.float32)
        s_loc = jnp.where(valid, s_loc, NEG_INF)
        s_ctx = jnp.einsum('bqkgd,bskd->bkgqs', qi, k_ctx).astype(jnp.float32)
        logits = jnp.concatenate([s_loc, s_ctx, sink_b], axis=-1)
        p = jax.nn.softmax(logits, axis=-1).astype(v.dtype)
        o = (jnp.einsum('bkgqs,bskd->bqkgd', p[..., :3 * BLOCK], vb)
             + jnp.einsum('bkgqs,bskd->bqkgd', p[..., 3 * BLOCK:3 * BLOCK + n_ctx], v_ctx))
        return o.reshape(b, BLOCK, ATTN_Q_W)

    out = lax.map(block, (jnp.arange(nb), qb))
    return out.transpose(1, 0, 2, 3).reshape(b, n, ATTN_Q_W)

def context_attention(q, k, v, sink):
    b, L = q.shape[:2]
    qg = (q * HEAD_DIM ** -0.5).reshape(b, L, N_KV_HEADS, Q_GROUP, HEAD_DIM)
    s = jnp.einsum('bqkgd,bskd->bkgqs', qg, k).astype(jnp.float32)
    sink_b = jnp.broadcast_to(sink.astype(jnp.float32).reshape(1, N_KV_HEADS, Q_GROUP, 1, 1),
                              (b, N_KV_HEADS, Q_GROUP, L, 1))
    p = jax.nn.softmax(jnp.concatenate([s, sink_b], axis=-1), axis=-1).astype(v.dtype)
    o = jnp.einsum('bkgqs,bskd->bqkgd', p[..., :L], v)
    return o.reshape(b, L, ATTN_Q_W)

def fourier_mix(u):
    b, n = u.shape[:2]
    ug = u.astype(jnp.float32).reshape(b, n, N_FOURIER_GROUPS, FOURIER_GROUP_DIM)
    f = jnp.fft.fft2(ug, axes=(1, 3), norm="ortho")
    return jnp.real(f).astype(u.dtype).reshape(b, n, FOURIER_WIDTH)

def merge_branches(a, f, ga, gf, w_a, w_f, w_o):
    y = jax.nn.sigmoid(ga) * (a @ w_a) + jax.nn.sigmoid(gf) * (f @ w_f)
    return y @ w_o

def setup_inputs(seed: int = 0) -> dict:
    key = jax.random.key(seed)
    ks = jax.random.split(key, 24)
    f32 = jnp.float32

    def dense(k, shape, fan_in, gain=1.0):
        return jax.random.normal(k, shape, f32) * (gain * fan_in ** -0.5)

    def gain_vec(k, shape):
        return 1.0 + 0.05 * jax.random.normal(k, shape, f32)

    return {
        "x": jax.random.normal(ks[0], (BATCH, SEQ, D_MODEL), f32),
        "c": jax.random.normal(ks[1], (BATCH, D_MODEL), f32),
        "ctx": jax.random.normal(ks[2], (BATCH, CTX_LEN, D_MODEL), f32),
        "c_ctx": jax.random.normal(ks[3], (D_MODEL,), f32),
        "w_ada": dense(ks[4], (DEPTH, D_MODEL, N_MOD * D_MODEL), D_MODEL, 0.5),
        "b_ada": 0.02 * jax.random.normal(ks[5], (DEPTH, N_MOD * D_MODEL), f32),
        "g_ffn1": gain_vec(ks[6], (DEPTH, D_MODEL)),
        "w_ffn1_in": dense(ks[7], (DEPTH, D_MODEL, 2 * D_FF), D_MODEL),
        "w_ffn1_out": dense(ks[8], (DEPTH, D_FF, D_MODEL), D_FF),
        "g_mix": gain_vec(ks[9], (DEPTH, D_MODEL)),
        "w_in": dense(ks[10], (DEPTH, D_MODEL, D_IN), D_MODEL),
        "attn_sink": 0.5 * jax.random.normal(ks[11], (DEPTH, N_HEADS), f32),
        "w_attn_branch": dense(ks[12], (DEPTH, ATTN_Q_W, D_MODEL), ATTN_Q_W),
        "w_fourier_branch": dense(ks[13], (DEPTH, FOURIER_WIDTH, D_MODEL), FOURIER_WIDTH),
        "w_out": dense(ks[14], (DEPTH, D_MODEL, D_MODEL), D_MODEL),
        "g_ffn2": gain_vec(ks[15], (DEPTH, D_MODEL)),
        "w_ffn2_in": dense(ks[16], (DEPTH, D_MODEL, 2 * D_FF), D_MODEL),
        "w_ffn2_out": dense(ks[17], (DEPTH, D_FF, D_MODEL), D_FF),
        "g_final": gain_vec(ks[18], (D_MODEL,)),
    }

def reference(x, c, ctx, c_ctx, w_ada, b_ada, g_ffn1, w_ffn1_in, w_ffn1_out, g_mix, w_in,
              attn_sink, w_attn_branch, w_fourier_branch, w_out, g_ffn2, w_ffn2_in, w_ffn2_out,
              g_final):
    b, n = x.shape[:2]
    cos, sin = axial_rope_angles(n)
    cond_lat = jax.nn.silu(c)
    cond_ctx = jax.nn.silu(c_ctx)[None]

    for layer in range(DEPTH):
        last = layer == DEPTH - 1
        mod_lat = (cond_lat @ w_ada[layer] + b_ada[layer]).reshape(b, N_MOD, D_MODEL)
        mod_ctx = (cond_ctx @ w_ada[layer] + b_ada[layer]).reshape(1, N_MOD, D_MODEL)

        x = macaron_ffn(x, mod_lat, 0, g_ffn1[layer], w_ffn1_in[layer], w_ffn1_out[layer])
        ctx = macaron_ffn(ctx, mod_ctx, 0, g_ffn1[layer], w_ffn1_in[layer], w_ffn1_out[layer])

        h_lat = adaln_norm(x, g_mix[layer], mod_lat, 3)
        h_ctx = adaln_norm(ctx, g_mix[layer], mod_ctx, 3)
        w_in_l = w_in[layer]
        sink = attn_sink[layer]
        if last:
            kv_c = h_ctx @ w_in_l[:, K_OFF:U_OFF]
            k_c = kv_c[..., :ATTN_KV_W].reshape(b, -1, N_KV_HEADS, HEAD_DIM)
            v_c = kv_c[..., ATTN_KV_W:].reshape(b, -1, N_KV_HEADS, HEAD_DIM)
        else:
            q_c, k_c, v_c, u_c, ga_c, gf_c = split_projection(h_ctx @ w_in_l)
            a_c = context_attention(q_c, k_c, v_c, sink)
            f_c = fourier_mix(u_c)
            ctx_mixed = ctx + mod_vec(mod_ctx, 5) * merge_branches(
                a_c, f_c, ga_c, gf_c, w_attn_branch[layer], w_fourier_branch[layer], w_out[layer])

        q, k, v, u, ga, gf = split_projection(h_lat @ w_in_l)
        q = apply_rope(q, cos, sin)
        k = apply_rope(k, cos, sin)
        a = windowed_attention_with_context(q, k, v, k_c, v_c, sink)
        f = fourier_mix(u)
        x = x + mod_vec(mod_lat, 5) * merge_branches(
            a, f, ga, gf, w_attn_branch[layer], w_fourier_branch[layer], w_out[layer])

        x = macaron_ffn(x, mod_lat, 6, g_ffn2[layer], w_ffn2_in[layer], w_ffn2_out[layer])
        if not last:
            ctx = macaron_ffn(ctx_mixed, mod_ctx, 6, g_ffn2[layer], w_ffn2_in[layer], w_ffn2_out[layer])

    return rms_norm(x, g_final)


_drawn_inputs = setup_inputs


def setup_inputs(seed=0):
    import zlib

    import numpy as np

    out = dict(_drawn_inputs(seed))
    spreads = {}
    factors = {'ctx': 4.984,
     'b_ada': 3.753,
     'g_ffn1': 7.214,
     'g_mix': 8.0,
     'attn_sink': 8.0,
     'g_ffn2': 7.734}
    for name, (base, spread) in spreads.items():
        noise = np.random.default_rng([zlib.crc32(name.encode()), seed]).standard_normal(out[name].shape)
        drawn = base * np.exp(spread * noise) if base else spread * noise
        out[name] = __import__('jax').numpy.asarray(drawn.astype(out[name].dtype))
    for name, factor in factors.items():
        out[name] = (out[name] * factor).astype(out[name].dtype)
    return out
```

```python
from contextlib import ExitStack

import concourse.bass as bass
from concourse import mybir

ACT = mybir.ActivationFunctionType
ALU = mybir.AluOpType
AX = mybir.AxisListType
F32 = mybir.dt.float32
R32 = mybir.dt.float32r

P = 128
D = 1024
KD = D // P
SEQ, CTX = 1024, 256
NT = 512
FF = 2816
NPAIR = FF // (2 * P)
HEAD = 64
NKV = 4
NB = SEQ // P
NKT = (SEQ + CTX) // P
NG = 4
NMOD = 9
K_OFF, V_OFF, U_OFF, GA_OFF, GF_OFF = 1024, 1280, 1536, 2048, 3072
EPS = 1e-6
NEG = -1e30

ROW_B, ROW_C, ROW_CCTX, ROW_G1, ROW_GM, ROW_G2, ROW_GF = 0, 72, 80, 88, 96, 104, 112
NROW = 120

PAN_FFN1 = 0
PAN_FOU = PAN_FFN1 + 6 * NPAIR
PAN_KV = PAN_FOU + 10 * NG
PAN_ATT = PAN_KV + 4
PAN_MRG = PAN_ATT + 2 * NKV
PAN_OUT = PAN_MRG + 4 * KD
PAN_FFN2 = PAN_OUT + KD
PAN_END = PAN_FFN2 + 6 * NPAIR

FIL_FFN1 = 1
FIL_FOU = FIL_FFN1 + 36 * NPAIR
FIL_KV = FIL_FOU + 18 * NG
FIL_ATT = FIL_KV + 18
FIL_MRG = FIL_ATT + 4 * NKV
FIL_OUT = FIL_MRG + 8 * KD
FIL_FFN2 = FIL_OUT + 2 * KD

KEYS = [[k for k in (b - 1, b, b + 1) if 0 <= k < NB] + [NB, NB + 1] for b in range(NB)]
GROUPS = [-(-2 * len(k) // 4) for k in KEYS]
GROUP0 = [sum(GROUPS[:b]) for b in range(NB)]
NGROUP = sum(GROUPS)


def build(nc, T):
    with ExitStack() as ctx:
        base = 16512

        def at(name, off, shape, dt=F32):
            return nc.alloc_sbuf_tensor_at(name, shape, dt, offset=base + off)

        def sem(name):
            return ctx.enter_context(nc.semaphore(name))

        HH, HL = 0, 32768
        RING = 65536
        CON = RING + 6 * 4096
        POOL = CON + 6272
        Hh = at("Hh", HH, [P, KD, SEQ], R32)
        Hl = at("Hl", HL, [P, KD, SEQ], R32)
        raw = [at(f"raw{s}", RING + s * 4096, [P, D]) for s in range(2)]
        whi = [at(f"whi{s}", RING + (2 + s) * 4096, [P, D], R32) for s in range(2)]
        wlo = [at(f"wlo{s}", RING + (4 + s) * 4096, [P, D], R32) for s in range(2)]
        c = CON
        cols = at("cols", c, [P, NROW]); c += 480
        modT = at("modT", c, [P, NMOD, KD, 2]); c += 576
        gainT = at("gainT", c, [P, 3, KD, 2]); c += 192
        gateT = at("gateT", c, [P, 3, KD, 2]); c += 192
        cond = at("cond", c, [P, KD, 2]); c += 64
        epsT = at("epsT", c, [P, 1]); c += 32
        dummy = at("dummy", c, [P, 32]); c += 128
        ones = at("ones", c, [P, P]); c += 512
        ident = at("ident", c, [P, P]); c += 512
        identR = at("identR", c, [P, P], R32); c += 512
        mask_f = at("mask_f", c, [P, 2, P]); c += 1024
        maskR = at("maskR", c, [P, 2, P], R32); c += 1024
        altR = at("altR", c, [P, 2], R32); c += 32
        alt_f = at("alt_f", c, [P, 2]); c += 32
        sink_f = at("sink_f", c, [P, 16, 2]); c += 128
        sink_r = at("sink_r", c, [P, 16]); c += 64
        sinkH = at("sinkH", c, [P, 16, 2], R32); c += 128
        sinkL = at("sinkL", c, [P, 16, 2], R32); c += 128
        rows = at("rows", c, [NROW, P]); c += 512
        assert c <= POOL, c - POOL
        x_lat = at("x_lat", POOL, [P, KD, SEQ])
        x_ctx = at("x_ctx", POOL + 32768, [P, KD, CTX])
        Ch = at("Ch", POOL + 40960, [P, KD, CTX], R32)
        Cl = at("Cl", POOL + 49152, [P, KD, CTX], R32)
        NRM = POOL + 57344
        sq = [at(f"sq{s}", NRM + 2048 * s, [P, NT]) for s in range(2)]
        tn = [at(f"tn{s}", NRM + 4096 + 2048 * s, [P, NT]) for s in range(2)]
        rms = [at(f"rms{s}", NRM + 8192 + 2048 * s, [P, NT]) for s in range(2)]
        rstd = [at(f"rstd{s}", NRM + 12288 + 2048 * s, [P, NT]) for s in range(2)]
        GB = NRM + 16384
        gH = at("gH", GB, [P, 2, SEQ + CTX], R32)
        gL = at("gL", GB + 10240, [P, 2, SEQ + CTX], R32)
        act_t = at("act_t", GB + 20480, [P, SEQ + CTX])
        x_in = at("x_in", HH, [P, NKT, D])
        ada = [at(f"ada{s}", GB + 4096 * s, [P, D]) for s in range(8)]
        uH = at("uH", POOL, [P, SEQ], R32)
        uL = at("uL", POOL + 4096, [P, SEQ], R32)
        xcH = at("xcH", POOL + 8192, [P, NB, 2 * P], R32)
        xcL = at("xcL", POOL + 16384, [P, NB, 2 * P], R32)
        fB = at("fB", POOL + 24576, [P, NT])
        fT = at("fT", POOL + 26624, [P, SEQ])
        fH = at("fH", POOL + 30720, [P, SEQ], R32)
        fL = at("fL", POOL + 34816, [P, SEQ], R32)
        ROPE = GB
        cosT = at("cosT", ROPE, [P, SEQ])
        sinT = at("sinT", ROPE + 4096, [P, SEQ])
        swp = [at(f"swp{s}", ROPE + 8192 + 2048 * s, [P, NT]) for s in range(2)]
        rot = [at(f"rot{s}", ROPE + 12288 + 2048 * s, [P, NT]) for s in range(2)]
        kH = [at(f"kH{s}", POOL + 2048 * s, [P, NT], R32) for s in range(2)]
        kL = [at(f"kL{s}", POOL + 4096 + 2048 * s, [P, NT], R32) for s in range(2)]
        vT = [at(f"vT{s}", POOL + 8192 + 5120 * s, [P, NKT, P]) for s in range(2)]
        vS = [at(f"vS{s}", POOL + 18432 + 10240 * s, [P, 2, NKT, 2, HEAD], R32) for s in range(2)]
        o = POOL
        keyH = at("keyH", o, [P, SEQ + CTX], R32); o += 5120
        keyL = at("keyL", o, [P, SEQ + CTX], R32); o += 5120
        val = at("val", o, [P, NKT, P], R32); o += 5120
        qS = [at(f"qS{h}", o + 4096 * h, [P, SEQ], R32) for h in range(2)]; o += 8192
        pr = [[at(f"pr{s}{h}", o + (2 * s + h) * 2592, [P, 642]) for h in range(2)] for s in range(2)]
        o += 4 * 2592
        ptH = [at(f"ptH{s}", o + 5120 * s, [P, 5 * 2 * P], R32) for s in range(2)]; o += 10240
        ptL = [at(f"ptL{s}", o + 5120 * s, [P, 5 * 2 * P], R32) for s in range(2)]; o += 10240
        oLow = [at(f"oLow{s}", o + 1024 * s, [HEAD, 2, P]) for s in range(2)]; o += 2048
        aT = at("aT", o, [P, SEQ]); o += 4096
        aH = at("aH", o, [P, SEQ], R32); o += 4096
        aL = at("aL", o, [P, SEQ], R32); o += 4096
        nmax = at("nmax", o, [P, 4]); o += 32
        lsum = at("lsum", o, [P, 4]); o += 32
        rsum = at("rsum", o, [P, 4]); o += 32
        assert o <= ROPE
        mF = [at(f"mF{s}", POOL + 16384 * s, [P, NG, SEQ], R32) for s in range(2)]
        mA = [at(f"mA{s}", POOL + 32768 + 32768 * s, [P, KD, SEQ], R32) for s in range(2)]
        MT = POOL + 98304
        gate_s = at("gate_s", MT, [P, SEQ])
        y = at("y", MT + 4096, [P, SEQ])
        yH = at("yH", MT + 8192, [P, SEQ], R32)
        yL = at("yL", MT + 12288, [P, SEQ], R32)
        assert base + MT + 16384 <= 229368, base + MT + 16384 - 229368
        Yh = at("Yh", HH, [P, KD, SEQ], R32)
        Yl = at("Yl", HL, [P, KD, SEQ], R32)
        oT = at("oT", HH, [P, KD, SEQ])
        orow = [at(f"orow{s}", HL + 4096 * s, [P, D]) for s in range(2)]

        ps = ctx.enter_context(nc.psum_tensor("ps", [P, 8, NT], F32))

        x_scr = nc.dram_tensor("x_scr", [P, KD, SEQ], F32).ap()
        f_scr = nc.dram_tensor("f_scr", [NG, 2, P, SEQ], R32).ap()
        k_scr = nc.dram_tensor("k_scr", [2, 2 * P, SEQ + CTX], R32).ap()
        v_scr = nc.dram_tensor("v_scr", [P, NKV, NKT * P], R32).ap()
        a_scr = nc.dram_tensor("a_scr", [KD, 2, P, SEQ], R32).ap()
        y_scr = nc.dram_tensor("y_scr", [KD, 2, P, SEQ], R32).ap()

        rows_in = sem("rows_in"); const_in = sem("const_in"); sink_in = sem("sink_in")
        x_tile_in = [sem(f"x_tile_in{t}") for t in range(NKT)]
        ones_set = sem("ones_set"); consts_set = sem("consts_set")
        cols_set = sem("cols_set"); cond_set = sem("cond_set")
        x_turned = sem("x_turned"); x_even = sem("x_even"); x_odd = sem("x_odd")
        ada_in = [sem(f"ada_in{s}") for s in range(8)]
        ada_used = sem("ada_used"); mod_set = sem("mod_set"); gain_set = sem("gain_set")
        panel_in = [sem(f"panel_in{s}") for s in range(2)]
        panel_hi = sem("panel_hi"); panel_split = sem("panel_split"); psum_filled = sem("psum_filled")

        def norm_sems(j):
            return {n: sem(f"n{j}_{n}") for n in ("sq", "ss", "rms", "rstd", "t", "hi", "lo")}

        def ffn_sems(j):
            return {n: sem(f"f{j}_{n}") for n in ("silu", "prod", "ghi", "glo", "acc")}

        N1, N2, N3, N4 = (norm_sems(j) for j in range(1, 5))
        F1, F2 = ffn_sems(1), ffn_sems(2)
        x_saved = sem("x_saved")
        u_hi = sem("u_hi"); u_lo = sem("u_lo"); xc_hi = sem("xc_hi"); xc_lo = sem("xc_lo")
        fb_out = sem("fb_out"); f_sum = sem("f_sum"); f_hi = sem("f_hi"); f_lo = sem("f_lo"); f_saved = sem("f_saved"); f_free = sem("f_free")
        rope_in = sem("rope_in"); swapped = sem("swapped"); sin_mul = sem("sin_mul"); rot_set = sem("rot_set")
        k_hi = sem("k_hi"); k_lo = sem("k_lo"); k_saved = [sem(f"k_saved{s}") for s in range(2)]
        v_out = sem("v_out"); v_hi = sem("v_hi"); v_lo = sem("v_lo"); v_saved = sem("v_saved")
        kv_in = sem("kv_in"); q_hi = sem("q_hi"); q_lo = sem("q_lo")
        qk_done = sem("qk_done"); max_set = sem("max_set"); exp_set = sem("exp_set"); rsum_set = sem("rsum_set")
        prob_set = sem("prob_set"); pt_turned = sem("pt_turned"); pt_hi = sem("pt_hi"); pt_lo = sem("pt_lo")
        pv_done = sem("pv_done"); o_low = sem("o_low"); o_out = sem("o_out")
        a_hi = sem("a_hi"); a_lo = sem("a_lo"); a_saved = sem("a_saved"); a_free = sem("a_free")
        merge_in = sem("merge_in"); sgf = sem("sgf"); yf = sem("yf"); sga = sem("sga"); ya = sem("ya"); ysum = sem("ysum")
        y_hi = sem("y_hi"); y_lo = sem("y_lo"); y_saved = sem("y_saved"); y_free = sem("y_free")
        proj_in = sem("proj_in"); x_res = sem("x_res")
        o_turned = sem("o_turned"); o_even = sem("o_even"); o_odd = sem("o_odd"); stored = [sem(f"stored{s}") for s in range(2)]

        CREDIT = [(panel_split, 2), (F1["silu"], 3), (F1["prod"], 3), (F1["glo"], 3), (F1["acc"], 2),
                  (F2["silu"], 2), (F2["prod"], 2), (F2["glo"], 2), (F2["acc"], 2),
                  (xc_lo, 2), (f_sum, 1), (f_lo, 1), (y_lo, 1), (f_free, 1), (exp_set, 2), (pt_lo, 1), (o_out, 1),
                  (a_free, 1), (pv_done, 1), (sgf, 2), (yf, 2), (sga, 2), (ya, 2), (ysum, 1), (y_free, 1), (x_res, 4)]

        w_in = {1: T["w_ffn1_in"], 2: T["w_ffn2_in"]}
        w_out = {1: T["w_ffn1_out"], 2: T["w_ffn2_out"]}
        LAT = [(x_lat, Hh, Hl, 0, NT, 0, 0), (x_lat, Hh, Hl, NT, NT, 0, NT)]
        ALL = LAT + [(x_ctx, Ch, Cl, 0, CTX, 1, SEQ)]

        def chunks(w):
            return w.rearrange("(k p) n -> p k n", p=P)

        def k3(t):
            return t[:, :].rearrange("p (k n) -> p k n", k=KD)

        def panel_wait(eng, p0, per, i, j):
            eng.wait_ge(panel_split, 2 + p0 + j + 1 + per * i if not isinstance(i, int) else 2 + p0 + per * i + j + 1)

        block = ctx.enter_context(nc.Block())

        @block.sync
        def _(sp):
            sp.dma_start(rows[ROW_B:ROW_C, :], T["b_ada"].rearrange("(r n) -> r n", n=P)).then_inc(rows_in, 16)
            for r, name in ((ROW_C, "c"), (ROW_CCTX, "c_ctx"), (ROW_G1, "g_ffn1"), (ROW_GM, "g_mix"),
                            (ROW_G2, "g_ffn2"), (ROW_GF, "g_final")):
                sp.dma_start(rows[r:r + KD, :], T[name].rearrange("(r n) -> r n", n=P)).then_inc(rows_in, 16)
            sp.dma_start(ident[:, :], T["ident"]).then_inc(const_in, 16)
            for t in range(NKT):
                src = T["x"][t * P:(t + 1) * P, :] if t < NB else T["ctx"][(t - NB) * P:(t - NB + 1) * P, :]
                sp.dma_start(x_in[:, t, :], src).then_inc(x_tile_in[t], 16)
            sp.dma_start(mask_f[:, :, :], T["masks"]).then_inc(const_in, 16)
            sp.dma_start(alt_f[:, :], T["alt"]).then_inc(const_in, 16)
            sp.dma_start(sink_r[:, :], T["attn_sink"].partition_broadcast(P)).then_inc(sink_in, 16)

            def ada_load(m, k):
                sp.dma_start(ada[k][:, :], T["w_ada"][k * P:(k + 1) * P, bass.ds(m, D)]).then_inc(ada_in[k], 16)
            for k in range(KD):
                ada_load(0, k)
            with sp.Fori(1, NMOD) as m:
                at_m = sp.snap(m * D)
                for k in range(KD):
                    sp.wait_ge(ada_used, m * KD + (k - KD + 1))
                    ada_load(at_m, k)

            def load(par, n, dst, src, at):
                at = at if isinstance(at, int) else sp.snap(at)
                sp.wait_ge(panel_split, n)
                sp.dma_start(dst, src(at)).then_inc(panel_in[par], 16)

            def ffn_load(j, p0):
                win, wout = chunks(w_in[j]), chunks(w_out[j])
                with sp.Fori(0, NPAIR) as i:
                    for fl in range(2):
                        for half in range(2):
                            s = 2 * fl + half
                            load(s % 2, i * 6 + (p0 + s + 1), k3(raw[s % 2]),
                                 lambda at: win[:, :, bass.ds(at, P)], i * (2 * P) + (half * FF + fl * P))
                    for half in range(2):
                        load(half, i * 6 + (p0 + 4 + half + 1), raw[half][:, :].rearrange("p (f n) -> p f n", f=2),
                             lambda at, half=half: wout[:, bass.ds(at, 2), half * NT:(half + 1) * NT], i * 2)
            ffn_load(1, PAN_FFN1)
            win = chunks(T["w_in"])
            with sp.Fori(0, NG) as g:
                load(0, g * 10 + (PAN_FOU + 1), k3(raw[0]), lambda at: win[:, :, bass.ds(at, P)], g * P + U_OFF)
                load(1, g * 10 + (PAN_FOU + 2), raw[1][:, :], lambda at: T["dft_chan"], 0)
                for n in range(NB):
                    load(n % 2, g * 10 + (PAN_FOU + 3 + n), raw[n % 2][:, :], lambda at, n=n: T["dft_pos"][n * P:(n + 1) * P, :], 0)
            for n in range(4):
                load(n % 2, PAN_KV + n + 1, k3(raw[n % 2]), lambda at, n=n: win[:, :, K_OFF + n * P:K_OFF + (n + 1) * P], 0)
            with sp.Fori(0, NKV) as g:
                for n in range(2):
                    load(n, g * 2 + (PAN_ATT + n + 1), k3(raw[n]), lambda at: win[:, :, bass.ds(at, P)], g * (2 * P) + n * P)
            wf, wa, wo = chunks(T["w_fourier_branch"]), chunks(T["w_attn_branch"]), chunks(T["w_out"])
            with sp.Fori(0, KD) as d:
                load(0, d * 4 + (PAN_MRG + 1), raw[0][:, 0:NG * P].rearrange("p (k n) -> p k n", k=NG), lambda at: wf[:, :, bass.ds(d * P, P)], 0)
                load(1, d * 4 + (PAN_MRG + 2), k3(raw[1]), lambda at: win[:, :, bass.ds(at, P)], d * P + GF_OFF)
                load(0, d * 4 + (PAN_MRG + 3), k3(raw[0]), lambda at: wa[:, :, bass.ds(d * P, P)], 0)
                load(1, d * 4 + (PAN_MRG + 4), k3(raw[1]), lambda at: win[:, :, bass.ds(at, P)], d * P + GA_OFF)
            with sp.Fori(0, KD // 2) as i:
                for n in range(2):
                    load(n, i * 2 + (PAN_OUT + n + 1), k3(raw[n]), lambda at: wo[:, :, bass.ds(at, P)], i * (2 * P) + n * P)
            ffn_load(2, PAN_FFN2)
            for t in range(NB):
                sp.wait_ge(o_even, t + 1)
                sp.wait_ge(o_odd, t + 1)
                sp.dma_start(T["out"][t * P:(t + 1) * P, :], orow[t % 2][:, :]).then_inc(stored[t % 2], 16)
            for s in range(2):
                sp.wait_ge(stored[s], 16 * NB // 2)

        @block.tensor
        def _(pe):
            pe.wait_ge(rows_in, 7 * 16)
            pe.wait_ge(const_in, 3 * 16)
            pe.transpose(ps[:, 6, 0:NROW], rows[:, :], ident[0:NROW, 0:NROW]).then_inc(psum_filled, 1)
            for t in range(NKT):
                pe.wait_ge(x_tile_in[t], 16)
                for half in range(2):
                    if t >= 2:
                        pe.wait_ge(x_odd if half else x_even, t - 1)
                    for k in range(4):
                        kk = half * 4 + k
                        mm = pe.transpose(ps[:, 2 * (t % 2) + half, k * P:(k + 1) * P], x_in[:, t, kk * P:(kk + 1) * P], ident[:, :])
                    mm.then_inc(x_turned, 1)
            pe.wait_ge(cond_set, 2)

            def ada_mm(m):
                for k in range(KD):
                    pe.wait_ge(ada_in[k], 16 * (m + 1) if isinstance(m, int) else m * 16 + 16)
                    if k == 0 and not isinstance(m, int):
                        pe.wait_ge(mod_set, m)
                    for d in range(KD):
                        mm = pe.matmul(ps[:, 7, 2 * d:2 * d + 2], ada[k][:, d * P:(d + 1) * P], cond[:, k, :],
                                       start=(k == 0 and d == 0), stop=(k == KD - 1), skip_group_check=True)
                    mm.then_inc(ada_used, 1)
            ada_mm(0)
            with pe.Fori(1, NMOD) as m:
                ada_mm(m)

            def norm_mm(S, blocks):
                for b, (x, _, _, t0, n, _, _) in enumerate(blocks):
                    if b >= 2:
                        pe.wait_ge(S["rms"], b - 1)
                    for k in range(KD):
                        pe.wait_ge(S["sq"], b * KD + k + 1)
                        pe.matmul(ps[:, 6 + b % 2, 0:n], ones[:, :], sq[k % 2][:, 0:n], start=(k == 0),
                                  stop=(k == KD - 1)).then_inc(S["ss"], 1)

            def three(out, lh, ll, rh, rl, start, stop):
                pe.matmul(out, lh, rh, start=start, stop=False)
                pe.matmul(out, lh, rl, start=False, stop=False)
                return pe.matmul(out, ll, rh, start=False, stop=stop)

            def project(bank, s, hi, lo, t0, n, nk=KD):
                for k in range(nk):
                    mm = three(ps[:, bank, 0:n], whi[s][:, k * P:(k + 1) * P], wlo[s][:, k * P:(k + 1) * P],
                               hi[:, k, t0:t0 + n], lo[:, k, t0:t0 + n], k == 0, k == nk - 1)
                mm.then_inc(psum_filled, 1)

            def ffn_mm(S, blocks, p0, NS):
                nb = len(blocks)
                with pe.Fori(0, NPAIR) as i:
                    for fl in range(2):
                        for half in range(2):
                            s = 2 * fl + half
                            pe.wait_ge(panel_split, i * 6 + (2 + p0 + s + 1))
                            for b, (_, hi, lo, t0, n, _, _) in enumerate(blocks):
                                pe.wait_ge(NS["lo"], KD * (b + 1))
                                pe.wait_ge(S["prod" if half else "silu"], i * (2 * nb) + (fl * nb + b + 1))
                                project(3 * half + b, s % 2, hi, lo, t0, n)
                    for half in range(2):
                        pe.wait_ge(panel_split, i * 6 + (2 + p0 + 4 + half + 1))
                        for b, (_, _, _, _, n, _, g0) in enumerate(blocks):
                            if half == 0:
                                pe.wait_ge(S["glo"], i * (2 * nb) + (nb + nb + b + 1))
                            for d in range(4):
                                pe.wait_ge(S["acc"], i * (8 * nb) + ((half * nb + b) * 4 + d + 1))
                                for fl in range(2):
                                    w = slice(fl * NT + d * P, fl * NT + (d + 1) * P)
                                    mm = three(ps[:, 6 + d % 2, 0:n], whi[half][:, w], wlo[half][:, w],
                                               gH[:, fl, g0:g0 + n], gL[:, fl, g0:g0 + n], fl == 0, fl == 1)
                                mm.then_inc(psum_filled, 1)

            pe.wait_ge(ones_set, 1)
            pe.wait_ge(x_odd, NKT)
            pe.wait_ge(cols_set, 1)
            pe.wait_ge(mod_set, NMOD)
            norm_mm(N1, ALL)
            pe.wait_ge(N1["rms"], 3)
            ffn_mm(F1, ALL, PAN_FFN1, N1)
            pe.wait_ge(F1["acc"], 2 + 24 * NPAIR)
            norm_mm(N2, ALL)

            pe.wait_ge(consts_set, 1)
            pe.wait_ge(N2["rms"], 3)
            with pe.Fori(0, NG) as g:
                pe.wait_ge(panel_split, g * 10 + (2 + PAN_FOU + 1))
                for b, (_, hi, lo, t0, n, _, _) in enumerate(LAT):
                    pe.wait_ge(N2["lo"], KD * (b + 1))
                    project(b, 0, hi, lo, t0, n)
                pe.wait_ge(panel_split, g * 10 + (2 + PAN_FOU + 2))
                for n in range(NB):
                    pe.wait_ge(u_lo, g * 2 + (n // 4 + 1))
                    pe.wait_ge(xc_lo, g * NB + (n + 1))
                    w = slice(n * P, (n + 1) * P)
                    three(ps[:, 2 + n % 2, 0:2 * P], uH[:, w], uL[:, w], whi[1][:, 0:2 * P], wlo[1][:, 0:2 * P],
                          True, True).then_inc(psum_filled, 1)
                pe.wait_ge(f_sum, g + 1)
                for n in range(NB):
                    pe.wait_ge(panel_split, g * 10 + (2 + PAN_FOU + 3 + n))
                    pe.wait_ge(xc_lo, g * NB + (2 + n + 1))
                    st, sp_ = n == 0, n == NB - 1
                    pe.matmul(ps[:, 6, 0:2], xcH[:, n, 0:P], altR[:, :], start=st, stop=False)
                    pe.matmul(ps[:, 6, 0:2], xcL[:, n, 0:P], altR[:, :], start=False, stop=sp_)
                    for z in range(2):
                        mm = three(ps[:, 4 + z, :], xcH[:, n, z * P:(z + 1) * P], xcL[:, n, z * P:(z + 1) * P],
                                   whi[n % 2][:, z * NT:(z + 1) * NT], wlo[n % 2][:, z * NT:(z + 1) * NT], st, sp_)
                    mm.then_inc(psum_filled, 1)

            pe.wait_ge(f_sum, NG + 1)
            for n in range(4):
                pe.wait_ge(panel_split, 2 + PAN_KV + n + 1)
                for b, (_, hi, lo, t0, m, _, _) in enumerate(ALL):
                    pe.wait_ge(N2["lo"], KD * (b + 1))
                    if n >= 2:
                        pe.wait_ge(rot_set, 3 * (n - 2) + b + 1)
                    project(3 * (n % 2) + b, n % 2, hi, lo, t0, m)
            for e in range(6):
                vc, g0 = e // 3, 4 * (e % 3)
                pe.wait_ge(v_out, 3 * vc + e % 3 + 1)
                if e >= 2:
                    pe.wait_ge(v_lo, e - 1)
                for t in range(min(4, NKT - g0)):
                    mm = pe.transpose(ps[:, 6 + e % 2, t * P:(t + 1) * P], vT[vc][:, g0 + t, :], ident[:, :])
                mm.then_inc(psum_filled, 1)

            pe.wait_ge(v_lo, 6)
            with pe.Fori(0, NKV) as g:
                for pl in range(2):
                    pe.wait_ge(panel_split, g * 2 + (2 + PAN_ATT + pl + 1))
                    for b, (_, hi, lo, t0, n, _, _) in enumerate(LAT):
                        pe.wait_ge(pt_lo, g * (2 * NGROUP) + (pl * NGROUP + 1))
                        project(4 + b, pl, hi, lo, t0, n)
                    pe.wait_ge(kv_in, g * 80 + 80)

                    def scores(b):
                        keys = KEYS[b]
                        loc = len(keys) - 2
                        for h in range(2):
                            if h == 0:
                                pe.wait_ge(q_lo, g * 8 + (pl * 4 + (b // 4 + 1) * 2))
                            pe.wait_ge(exp_set, g * (4 * NB) + ((pl * NB + b) * 2 + h + 1))
                            S = ps[:, 2 * h:2 * h + 2, :].rearrange("p a n -> p (a n)")
                            q = qS[h][:, b * P:(b + 1) * P]
                            k0 = keys[0] * P
                            runs = [(0, k0, loc * P)]
                            if loc == 3:
                                runs += [(384, SEQ, P), (512, SEQ + P, P)]
                            else:
                                runs += [(256, SEQ, 2 * P)]
                            for r0, c0, w in runs:
                                pe.matmul(S[:, r0:r0 + w], q, keyH[:, c0:c0 + w], start=(r0 % NT == 0), stop=False, skip_group_check=True)
                                pe.matmul(S[:, r0:r0 + w], q, keyL[:, c0:c0 + w], start=False, stop=True, skip_group_check=True)
                            if b > 0:
                                pe.matmul(S[:, 0:P], identR[:, :], maskR[:, 0, :], start=False, stop=True, skip_group_check=True)
                            if b < NB - 1:
                                r0 = (loc - 1) * P
                                pe.matmul(S[:, r0:r0 + P], identR[:, :], maskR[:, 1, :], start=False, stop=True, skip_group_check=True)
                            r0 = len(keys) * P
                            hd = bass.ds(g * 4 + (2 * pl + h), 1)
                            pe.matmul(S[:, r0:r0 + 2], identR[:, :], sinkH[:, hd, :], start=(r0 % NT == 0), stop=False, skip_group_check=True)
                            pe.matmul(S[:, r0:r0 + 2], identR[:, :], sinkL[:, hd, :], start=False, stop=True,
                                      skip_group_check=True).then_inc(qk_done, 1)

                    def turn(b):
                        pe.wait_ge(prob_set, g * (4 * NB) + ((pl * NB + b) * 2 + 2))
                        tiles = [(t, h) for t in range(len(KEYS[b])) for h in range(2)]
                        for e in range(GROUPS[b]):
                            free = GROUP0[b] if b == 0 or e >= GROUPS[b - 1] else GROUP0[b - 1] + e + 1
                            pe.wait_ge(pt_lo, g * (2 * NGROUP) + (pl * NGROUP + free + 1))
                            for z, (t, h) in enumerate(tiles[4 * e:4 * e + 4]):
                                mm = pe.transpose(ps[:, 4 + e, z * P:(z + 1) * P], pr[b % 2][h][:, t * P:(t + 1) * P], ident[:, :])
                            mm.then_inc(pt_turned, 1)

                    def mix(b):
                        keys = KEYS[b]
                        pe.wait_ge(pt_lo, g * (2 * NGROUP) + (pl * NGROUP + GROUP0[b] + GROUPS[b] + 1))
                        pe.wait_ge(o_out, g * (2 * NB) + (pl * NB + b + 1))
                        for t, kt in enumerate(keys):
                            pe.matmul(ps[:, 7, 0:2 * P], val[:, kt, :], ptH[b % 2][:, t * 2 * P:(t + 1) * 2 * P], start=(t == 0), stop=False)
                            mm = pe.matmul(ps[:, 7, 0:2 * P], val[:, kt, :], ptL[b % 2][:, t * 2 * P:(t + 1) * 2 * P],
                                           start=False, stop=(t == len(keys) - 1))
                        mm.then_inc(pv_done, 1)

                    scores(0)
                    for b in range(NB):
                        if b + 1 < NB:
                            scores(b + 1)
                        turn(b)
                        if b >= 1:
                            mix(b - 1)
                    mix(NB - 1)

            pe.wait_ge(merge_in, 12 * 16 + 12 * 16)
            with pe.Fori(0, KD) as d:
                for j, (S, hi, lo, nk) in enumerate(((yf, mF[0], mF[1], NG), (sgf, Hh, Hl, KD), (ya, mA[0], mA[1], KD), (sga, Hh, Hl, KD))):
                    pe.wait_ge(panel_split, d * 4 + (2 + PAN_MRG + j + 1))
                    for b in range(2):
                        pe.wait_ge(S, d * 2 + (b + 1))
                        project(2 * j + b, j % 2, hi, lo, b * NT, NT, nk)

            pe.wait_ge(proj_in, 16 * 17)
            pe.wait_ge(ya, 2 + 2 * KD)
            with pe.Fori(0, KD // 2) as i:
                for n in range(2):
                    pe.wait_ge(panel_split, i * 2 + (2 + PAN_OUT + n + 1))
                    for b in range(2):
                        pe.wait_ge(x_res, i * 4 + (2 * n + b + 1))
                        project(2 * n + b, n, Yh, Yl, b * NT, NT)
            pe.wait_ge(x_res, 4 + 2 * KD)
            norm_mm(N3, LAT)
            pe.wait_ge(N3["rms"], 2)
            ffn_mm(F2, LAT, PAN_FFN2, N3)
            pe.wait_ge(F2["acc"], 2 + 16 * NPAIR)
            norm_mm(N4, LAT)
            pe.wait_ge(N4["rms"], 2)
            for t in range(NB):
                pe.wait_ge(N4["t"], KD * (t // 4 + 1))
                for half in range(2):
                    if t >= 2:
                        pe.wait_ge(o_odd if half else o_even, t - 1)
                    for k in range(4):
                        kk = half * 4 + k
                        mm = pe.transpose(ps[:, 2 * (t % 2) + half, k * P:(k + 1) * P], oT[:, kk, t * P:(t + 1) * P], ident[:, :])
                    mm.then_inc(o_turned, 1)

        @block.scalar
        def _(act):
            act.wait_ge(cols_set, 1)
            for s, r in ((0, ROW_C), (1, ROW_CCTX)):
                act.activation(cond[:, :, s], cols[:, r:r + KD], ACT.Silu).then_inc(cond_set, 1)
            for t in range(NKT):
                act.wait_ge(x_turned, 2 * t + 1)
                dst = x_lat[:, 0:4, t * P:(t + 1) * P] if t < NB else x_ctx[:, 0:4, (t - NB) * P:(t - NB + 1) * P]
                act.activation(dst, ps[:, 2 * (t % 2), :].rearrange("p (k n) -> p k n", k=4), ACT.Copy).then_inc(x_even, 1)

            def split_hi(s, nth, used):
                act.wait_ge(panel_in[s], nth)
                act.wait_ge(psum_filled, used)
                act.activation(whi[s][:, :], raw[s][:, :], ACT.Copy).then_inc(panel_hi, 1)

            def norm_act(S, blocks, j, last=False):
                for b, (x, _, _, t0, n, _, _) in enumerate(blocks):
                    for k in range(KD):
                        if b * KD + k >= 2:
                            act.wait_ge(S["ss"], b * KD + k - 1)
                        act.activation(sq[k % 2][:, 0:n], x[:, k, t0:t0 + n], ACT.Square).then_inc(S["sq"], 1)
                    act.wait_ge(S["ss"], KD * (b + 1))
                    if b >= 2:
                        act.wait_ge(S["rstd"], b - 1)
                    act.activation(rms[b % 2][:, 0:n], ps[:, 6 + b % 2, 0:n], ACT.Sqrt, bias=epsT[:, 0:1], scale=1.0 / D).then_inc(S["rms"], 1)
                if last:
                    return
                for b, (_, hi, _, t0, n, c, _) in enumerate(blocks):
                    for k in range(KD):
                        act.wait_ge(S["t"], b * KD + k + 1)
                        act.activation(hi[:, k, t0:t0 + n], tn[k % 2][:, 0:n], ACT.Identity,
                                       bias=modT[:, 3 * j, k, c:c + 1]).then_inc(S["hi"], 1)

            def ffn_act(S, blocks, p0, f0, last=False):
                nb = len(blocks)

                def body(i, final=False):
                    filled = [0, nb, 2 * nb, 3 * nb, 4 * nb, 8 * nb]
                    for s in range(6):
                        if not (final and s == 5):
                            split_hi((s + 1) % 2, i * 48 + 16 * ((p0 + s + 1) // 2 + 1), i * (12 * nb) + (f0 + filled[s]))
                        fl = s // 2
                        for b, (_, _, _, _, n, _, g0) in enumerate(blocks):
                            if s in (0, 2):
                                act.wait_ge(psum_filled, i * (12 * nb) + (f0 + filled[s] + b + 1))
                                act.wait_ge(S["glo"], i * (2 * nb) + (fl * nb + b + 1))
                                act.activation(act_t[:, g0:g0 + n], ps[:, b, 0:n], ACT.Silu).then_inc(S["silu"], 1)
                            if s in (1, 3):
                                act.wait_ge(S["prod"], i * (2 * nb) + (nb + fl * nb + b + 1))
                                act.activation(gH[:, fl, g0:g0 + n], act_t[:, g0:g0 + n], ACT.Copy).then_inc(S["ghi"], 1)
                with act.Fori(0, NPAIR - last) as i:
                    body(i)
                if last:
                    body(NPAIR - 1, True)

            split_hi(0, 16, 1)
            act.wait_ge(x_odd, NKT)
            act.wait_ge(x_even, NKT)
            act.wait_ge(gain_set, 1)
            norm_act(N1, ALL, 0)
            ffn_act(F1, ALL, PAN_FFN1, FIL_FFN1)
            act.wait_ge(F1["acc"], 2 + 24 * NPAIR)
            norm_act(N2, ALL, 1)

            act.wait_ge(x_saved, 16)
            act.wait_ge(N2["lo"], 3 * KD)
            with act.Fori(0, NG) as g:
                for s in range(10):
                    done = 0 if s == 0 else 2 if s == 1 else 10 + s - 2
                    split_hi((s + 1) % 2, g * 80 + 16 * ((PAN_FOU + s + 1) // 2 + 1), g * 18 + (FIL_FOU + done))
                    if s == 0:
                        for b in range(2):
                            act.wait_ge(psum_filled, g * 18 + (FIL_FOU + b + 1))
                            act.activation(uH[:, b * NT:(b + 1) * NT], ps[:, b, :], ACT.Copy).then_inc(u_hi, 1)
                    if s == 1:
                        for n in range(NB):
                            act.wait_ge(psum_filled, g * 18 + (FIL_FOU + 2 + n + 1))
                            act.activation(xcH[:, n, :], ps[:, 2 + n % 2, 0:2 * P], ACT.Copy).then_inc(xc_hi, 1)
                act.wait_ge(psum_filled, g * 18 + (FIL_FOU + 18))
                act.activation(fB[:, :], ps[:, 5, :], ACT.Copy).then_inc(fb_out, 1)
                act.wait_ge(f_sum, g + 2)
                act.wait_ge(f_free, g + 1)
                act.activation(fH[:, :], fT[:, :], ACT.Copy).then_inc(f_hi, 1)

            act.wait_ge(f_saved, 32 * NG)
            for n in range(4):
                split_hi((n + 1) % 2, 16 * ((PAN_KV + n + 1) // 2 + 1), FIL_KV + 3 * n)
                for b, (_, _, _, _, m, _, g0) in enumerate(ALL):
                    z = 3 * n + b
                    if n < 2:
                        act.wait_ge(rot_set, z + 1)
                        if z >= 2:
                            act.wait_ge(k_saved[z % 2], 32 * (z // 2))
                        act.activation(kH[z % 2][:, 0:m], rot[z % 2][:, 0:m], ACT.Copy).then_inc(k_hi, 1)
                    else:
                        act.wait_ge(psum_filled, FIL_KV + z + 1)
                        act.activation(vT[n - 2][:, g0 // P:(g0 + m) // P, :], ps[:, 3 * (n % 2) + b, 0:m].rearrange("p (t n) -> p t n", n=P),
                                       ACT.Copy).then_inc(v_out, 1)
            for e in range(6):
                vc, g0 = e // 3, 4 * (e % 3)
                w = min(4, NKT - g0)
                act.wait_ge(psum_filled, FIL_KV + 12 + e + 1)
                act.activation(vS[vc][:, :, g0:g0 + w, 0, :], ps[:, 6 + e % 2, 0:w * P].rearrange("p (t v e) -> p v t e", v=2, e=HEAD),
                               ACT.Copy).then_inc(v_hi, 1)

            act.wait_ge(k_saved[1], 32 * 3)
            act.wait_ge(k_saved[0], 32 * 3)
            act.wait_ge(v_saved, 32)
            with act.Fori(0, NKV) as g:
                for pl in range(2):
                    split_hi((pl + 1) % 2, g * 16 + 16 * ((PAN_ATT + pl + 1) // 2 + 1), g * 4 + (FIL_ATT + 2 * pl))
                    for b in range(2):
                        act.wait_ge(rot_set, g * 4 + (6 + 2 * pl + b + 1))
                        for h in range(2):
                            r = slice(HEAD * h, HEAD * (h + 1))
                            act.activation(qS[h][r, b * NT:(b + 1) * NT], rot[b][r, :], ACT.Copy, scale=HEAD ** -0.5).then_inc(q_hi, 1)

                    def unit(b, h):
                        return g * (4 * NB) + ((pl * NB + b) * 2 + h + 1)

                    def expo(b, h):
                        act.wait_ge(max_set, unit(b, h))
                        n = len(KEYS[b]) * P + 2
                        act.activation(pr[b % 2][h][:, 0:n], ps[:, 2 * h:2 * h + 2, :].rearrange("p a n -> p (a n)")[:, 0:n], ACT.Exp,
                                       bias=nmax[:, 2 * (b % 2) + h:2 * (b % 2) + h + 1],
                                       accum_out=lsum[:, 2 * (b % 2) + h:2 * (b % 2) + h + 1]).then_inc(exp_set, 1)

                    def turned_hi(b, e):
                        w = min(NT, 2 * len(KEYS[b]) * P - NT * e)
                        act.wait_ge(pt_turned, g * (2 * NGROUP) + (pl * NGROUP + GROUP0[b] + e + 1))
                        act.activation(ptH[b % 2][:, NT * e:NT * e + w], ps[:, 4 + e, 0:w], ACT.Copy).then_inc(pt_hi, 1)

                    def low_out(b):
                        act.wait_ge(pv_done, g * (2 * NB) + (1 + pl * NB + b + 1))
                        act.activation(oLow[b % 2][:, :, :], ps[HEAD:P, 7, 0:2 * P].rearrange("p (h n) -> p h n", h=2), ACT.Copy).then_inc(o_low, 1)

                    expo(0, 0)
                    expo(0, 1)
                    for b in range(NB):
                        for e in range(3):
                            if e < GROUPS[b]:
                                turned_hi(b, e)
                            if e < 2 and b + 1 < NB:
                                expo(b + 1, e)
                        if b >= 1:
                            low_out(b - 1)
                    low_out(NB - 1)
                    act.wait_ge(o_out, g * (2 * NB) + ((pl + 1) * NB + 1))
                    act.wait_ge(a_free, g * 2 + (pl + 1))
                    act.activation(aH[:, :], aT[:, :], ACT.Copy).then_inc(a_hi, 1)

            with act.Fori(0, KD) as d:
                for j in range(4):
                    split_hi((j + 1) % 2, d * 32 + 16 * ((PAN_MRG + j + 1) // 2 + 1), d * 8 + (FIL_MRG + 2 * j))
                    if j in (1, 3):
                        for b in range(2):
                            act.wait_ge(psum_filled, d * 8 + (FIL_MRG + 2 * j + b + 1))
                            if j == 1:
                                act.wait_ge(ysum, d + 1)
                            else:
                                act.wait_ge(yf, d * 2 + (2 + b + 1))
                            act.activation(gate_s[:, b * NT:(b + 1) * NT], ps[:, 2 * j + b, :], ACT.Sigmoid).then_inc(sgf if j == 1 else sga, 1)
                act.wait_ge(ysum, d + 2)
                act.wait_ge(y_free, d + 1)
                act.activation(yH[:, :], y[:, :], ACT.Copy).then_inc(y_hi, 1)

            with act.Fori(0, KD // 2) as i:
                for n in range(2):
                    split_hi((n + 1) % 2, i * 16 + 16 * ((PAN_OUT + n + 1) // 2 + 1), i * 4 + (FIL_OUT + 2 * n))
            act.wait_ge(x_res, 4 + 2 * KD)
            norm_act(N3, LAT, 2)
            ffn_act(F2, LAT, PAN_FFN2, FIL_FFN2, last=True)
            act.wait_ge(F2["acc"], 2 + 16 * NPAIR)
            norm_act(N4, LAT, 0, last=True)
            for t in range(NB):
                act.wait_ge(o_turned, 2 * t + 1)
                if t >= 2:
                    act.wait_ge(stored[t % 2], 16 * (t // 2))
                act.activation(orow[t % 2][:, 0:NT], ps[:, 2 * (t % 2), :], ACT.Copy).then_inc(o_even, 1)

        @block.vector
        def _(dve):
            dve.memset(ones[:, :], 1.0).then_inc(ones_set, 1)
            dve.memset(epsT[:, :], EPS)
            dve.wait_ge(psum_filled, 1)
            dve.tensor_copy(cols[:, :], ps[:, 6, 0:NROW]).then_inc(cols_set, 1)
            for t in range(NKT):
                dve.wait_ge(x_turned, 2 * t + 2)
                dst = x_lat[:, 4:8, t * P:(t + 1) * P] if t < NB else x_ctx[:, 4:8, (t - NB) * P:(t - NB + 1) * P]
                dve.tensor_copy(dst, ps[:, 2 * (t % 2) + 1, :].rearrange("p (k n) -> p k n", k=4)).then_inc(x_odd, 1)
            dve.wait_ge(const_in, 3 * 16)
            dve.wait_ge(sink_in, 16)
            dve.tensor_copy(identR[:, :], ident[:, :])
            dve.tensor_copy(maskR[:, :, :], mask_f[:, :, :])
            dve.tensor_copy(altR[:, :], alt_f[:, :]).then_inc(consts_set, 1)
            dve.memset(sink_f[:, :, 1:2], NEG)
            dve.tensor_copy(sink_f[:, :, 0], sink_r[:, :]).then_inc(cols_set, 1)
            dve.wait_ge(cols_set, 2)
            dve.tensor_copy(sinkH[:, :, :], sink_f[:, :, :]).then_inc(cols_set, 1)
            dve.wait_ge(cols_set, 3)
            dve.tensor_tensor(sinkL[:, :, :], sink_f[:, :, :], sinkH[:, :, :].bitcast(F32), ALU.subtract).then_inc(cols_set, 1)

            def mod_add(m):
                dve.wait_ge(ada_used, KD * (m + 1) if isinstance(m, int) else m * KD + KD)
                dve.tensor_tensor(modT[:, bass.ds(m, 1), :, :], ps[:, 7, 0:2 * KD].rearrange("p (a d s) -> p a d s", a=1, s=2),
                                  cols[:, bass.ds(m * KD, KD)].unsqueeze(1).unsqueeze(3).to_broadcast([P, 1, KD, 2]), ALU.add).then_inc(mod_set, 1)
            mod_add(0)
            with dve.Fori(1, NMOD) as m:
                mod_add(m)
            dve.wait_ge(mod_set, NMOD)
            for j, r in enumerate((ROW_G1, ROW_GM, ROW_G2)):
                for s in range(2):
                    dve.scalar_tensor_tensor(gainT[:, j, :, s], modT[:, 3 * j + 1, :, s], 1.0, cols[:, r:r + KD], ALU.add, ALU.mult)
                last = dve.tensor_scalar(gateT[:, j, :, :], modT[:, 3 * j + 2, :, :], 1.0 if j == 1 else 0.5, None, ALU.mult)
            last.then_inc(gain_set, 1)

            def split_lo(s, n):
                dve.wait_ge(panel_hi, n)
                dve.tensor_tensor(wlo[s][:, :], raw[s][:, :], whi[s][:, :].bitcast(F32), ALU.subtract).then_inc(panel_split, 1)

            def norm_dve(S, blocks, j, last=False):
                for b, (x, hi, lo, t0, n, c, _) in enumerate(blocks):
                    dve.wait_ge(S["rms"], b + 1)
                    if b >= 2:
                        dve.wait_ge(S["t"], KD * (b - 1))
                    dve.reciprocal(rstd[b % 2][:, 0:n], rms[b % 2][:, 0:n]).then_inc(S["rstd"], 1)
                    dve.wait_ge(S["rstd"], b + 1)

                    def low(k):
                        dve.wait_ge(S["hi"], b * KD + k + 1)
                        dve.scalar_tensor_tensor(lo[:, k, t0:t0 + n], tn[k % 2][:, 0:n], modT[:, 3 * j, k, c:c + 1],
                                                 hi[:, k, t0:t0 + n].bitcast(F32), ALU.add, ALU.subtract).then_inc(S["lo"], 1)
                    for k in range(KD):
                        gain = cols[:, ROW_GF + k:ROW_GF + k + 1] if last else gainT[:, j, k, c:c + 1]
                        dst = oT[:, k, t0:t0 + n] if last else tn[k % 2][:, 0:n]
                        if not last and b * KD + k >= 2:
                            dve.wait_ge(S["lo"], b * KD + k - 1)
                        dve.scalar_tensor_tensor(dst, x[:, k, t0:t0 + n], gain, rstd[b % 2][:, 0:n], ALU.mult, ALU.mult).then_inc(S["t"], 1)
                        if k >= 1 and not last:
                            low(k - 1)
                    if not last:
                        low(KD - 1)

            def ffn_dve(S, blocks, p0, f0, j, last=False):
                nb = len(blocks)

                def body(i, final=False):
                    filled = [0, nb, 2 * nb, 3 * nb, 4 * nb, 8 * nb]
                    for s in range(6):
                        if not (final and s == 5):
                            split_lo((s + 1) % 2, i * 6 + (p0 + s + 2))
                        fl = s // 2
                        if s in (1, 3):
                            for b, (_, _, _, _, n, _, g0) in enumerate(blocks):
                                dve.wait_ge(psum_filled, i * (12 * nb) + (f0 + filled[s] + b + 1))
                                dve.wait_ge(S["silu"], i * (2 * nb) + (nb + fl * nb + b + 1))
                                dve.tensor_tensor(act_t[:, g0:g0 + n], ps[:, 3 + b, 0:n], act_t[:, g0:g0 + n], ALU.mult).then_inc(S["prod"], 1)
                            for b, (_, _, _, _, n, _, g0) in enumerate(blocks):
                                dve.wait_ge(S["ghi"], i * (2 * nb) + (fl * nb + b + 1))
                                dve.tensor_tensor(gL[:, fl, g0:g0 + n], act_t[:, g0:g0 + n], gH[:, fl, g0:g0 + n].bitcast(F32),
                                                  ALU.subtract).then_inc(S["glo"], 1)
                        if s >= 4:
                            for b, (x, _, _, t0, n, c, _) in enumerate(blocks):
                                for d in range(4):
                                    k = (s - 4) * 4 + d
                                    dve.wait_ge(psum_filled, i * (12 * nb) + (f0 + filled[s] + 4 * b + d + 1))
                                    dve.scalar_tensor_tensor(x[:, k, t0:t0 + n], ps[:, 6 + d % 2, 0:n], gateT[:, j, k, c:c + 1],
                                                             x[:, k, t0:t0 + n], ALU.mult, ALU.add).then_inc(S["acc"], 1)
                with dve.Fori(0, NPAIR - last) as i:
                    body(i)
                if last:
                    body(NPAIR - 1, True)

            split_lo(0, 1)
            dve.wait_ge(x_even, NKT)
            dve.wait_ge(gain_set, 1)
            norm_dve(N1, ALL, 0)
            ffn_dve(F1, ALL, PAN_FFN1, FIL_FFN1, 0)
            dve.wait_ge(F1["acc"], 2 + 24 * NPAIR)
            norm_dve(N2, ALL, 1)

            dve.wait_ge(x_saved, 16)
            with dve.Fori(0, NG) as g:
                for s in range(10):
                    split_lo((s + 1) % 2, g * 10 + (PAN_FOU + s + 2))
                    if s == 0:
                        for b in range(2):
                            dve.wait_ge(u_hi, g * 2 + (b + 1))
                            w = slice(b * NT, (b + 1) * NT)
                            dve.tensor_tensor(uL[:, w], ps[:, b, :], uH[:, w].bitcast(F32), ALU.subtract).then_inc(u_lo, 1)
                    if s == 1:
                        for n in range(NB):
                            dve.wait_ge(xc_hi, g * NB + (n + 1))
                            dve.tensor_tensor(xcL[:, n, :], ps[:, 2 + n % 2, 0:2 * P], xcH[:, n, :].bitcast(F32), ALU.subtract).then_inc(xc_lo, 1)
                dve.wait_ge(fb_out, g + 1)
                dve.wait_ge(f_lo, g + 1)
                dve.tensor_tensor(fT[:, 0:NT], ps[:, 4, :], fB[:, :], ALU.subtract)
                dve.tensor_tensor(fT[:, SEQ - 1:NT:-1], ps[:, 4, 1:NT], fB[:, 1:NT], ALU.add)
                dve.tensor_copy(fT[:, NT:NT + 1], ps[:, 6, 0:1]).then_inc(f_sum, 1)
                dve.wait_ge(f_hi, g + 1)
                dve.tensor_tensor(fL[:, :], fT[:, :], fH[:, :].bitcast(F32), ALU.subtract).then_inc(f_lo, 1)

            def rotate(s, z, t0, n, lat):
                if lat:
                    by_cos = dve.tensor_tensor(rot[z % 2][:, 0:n], ps[:, s, 0:n], cosT[:, t0:t0 + n], ALU.mult).then_inc(cols_set, 1)
                    dve.stream_shuffle(swp[z % 2][:, 0:n], ps[:, s, 0:n], [i ^ 1 for i in range(32)]).then_inc(swapped, 1)
                    return by_cos
                return dve.tensor_copy(rot[z % 2][:, 0:n], ps[:, s, 0:n])

            dve.wait_ge(rope_in, 32)
            for n in range(4):
                split_lo((n + 1) % 2, PAN_KV + n + 2)
                if n >= 2:
                    continue
                for b, (_, _, _, t0, m, _, _) in enumerate(ALL):
                    z = 3 * n + b
                    dve.wait_ge(psum_filled, FIL_KV + z + 1)
                    if z >= 2:
                        dve.wait_ge(k_lo, z - 1)
                    if b < 2:
                        rotate(3 * n + b, z, t0, m, True)
                        dve.wait_ge(cols_set, 4 + 2 * n + b + 1)
                        dve.wait_ge(sin_mul, 2 * n + b + 1)
                        dve.tensor_tensor(rot[z % 2][:, 0:m], rot[z % 2][:, 0:m], swp[z % 2][:, 0:m], ALU.add).then_inc(rot_set, 1)
                    else:
                        rotate(3 * n + b, z, t0, m, False).then_inc(rot_set, 1)
                    dve.wait_ge(k_hi, z + 1)
                    dve.tensor_tensor(kL[z % 2][:, 0:m], rot[z % 2][:, 0:m], kH[z % 2][:, 0:m].bitcast(F32), ALU.subtract).then_inc(k_lo, 1)
            for e in range(6):
                vc, g0 = e // 3, 4 * (e % 3)
                w = min(4, NKT - g0)
                dve.wait_ge(v_hi, e + 1)
                dve.tensor_tensor(vS[vc][:, :, g0:g0 + w, 1, :], ps[:, 6 + e % 2, 0:w * P].rearrange("p (t v e) -> p v t e", v=2, e=HEAD),
                                  vS[vc][:, :, g0:g0 + w, 0, :].bitcast(F32), ALU.subtract).then_inc(v_lo, 1)

            dve.wait_ge(k_saved[1], 32 * 3)
            dve.wait_ge(k_saved[0], 32 * 3)
            dve.wait_ge(v_saved, 32)
            with dve.Fori(0, NKV) as g:
                for pl in range(2):
                    split_lo((pl + 1) % 2, g * 2 + (PAN_ATT + pl + 2))
                    for b in range(2):
                        dve.wait_ge(psum_filled, g * 4 + (FIL_ATT + 2 * pl + b + 1))
                        rotate(4 + b, b, b * NT, NT, True)
                        dve.wait_ge(cols_set, g * 4 + (8 + 2 * pl + b + 1))
                        dve.wait_ge(sin_mul, g * 4 + (4 + 2 * pl + b + 1))
                        dve.tensor_tensor(rot[b][:, :], rot[b][:, :], swp[b][:, :], ALU.add).then_inc(rot_set, 1)
                        for h in range(2):
                            r, o_ = slice(HEAD * h, HEAD * (h + 1)), slice(HEAD * (1 - h), HEAD * (2 - h))
                            w = slice(b * NT, (b + 1) * NT)
                            dve.wait_ge(q_hi, g * 8 + (4 * pl + 2 * b + h + 1))
                            dve.scalar_tensor_tensor(qS[h][o_, w], rot[b][r, :], HEAD ** -0.5, qS[h][r, w].bitcast(F32),
                                                     ALU.mult, ALU.subtract).then_inc(q_lo, 1)

                    def unit(b, h):
                        return g * (4 * NB) + ((pl * NB + b) * 2 + h + 1)

                    def maxi(b, h):
                        dve.wait_ge(qk_done, unit(b, h))
                        n = len(KEYS[b]) * P + 2
                        dve.tensor_reduce(nmax[:, 2 * (b % 2) + h:2 * (b % 2) + h + 1],
                                          ps[:, 2 * h:2 * h + 2, :].rearrange("p a n -> p (a n)")[:, 0:n], AX.X, ALU.max,
                                          negate=True).then_inc(max_set, 1)

                    def recip(b, h):
                        dve.wait_ge(exp_set, g * (4 * NB) + (2 + (pl * NB + b) * 2 + h + 1))
                        z = slice(2 * (b % 2) + h, 2 * (b % 2) + h + 1)
                        dve.reciprocal(rsum[:, z], lsum[:, z]).then_inc(rsum_set, 1)

                    def turned_lo(b, e):
                        w = min(NT, 2 * len(KEYS[b]) * P - NT * e)
                        dve.wait_ge(pt_hi, g * (2 * NGROUP) + (pl * NGROUP + GROUP0[b] + e + 1))
                        dve.tensor_tensor(ptL[b % 2][:, NT * e:NT * e + w], ps[:, 4 + e, 0:w], ptH[b % 2][:, NT * e:NT * e + w].bitcast(F32),
                                          ALU.subtract).then_inc(pt_lo, 1)

                    def out(b):
                        dve.wait_ge(o_low, g * (2 * NB) + (pl * NB + b + 1))
                        for h in range(2):
                            last = dve.tensor_tensor(aT[HEAD * h:HEAD * (h + 1), b * P:(b + 1) * P], ps[0:HEAD, 7, h * P:(h + 1) * P],
                                                     oLow[b % 2][:, h, :], ALU.add)
                        last.then_inc(o_out, 1)

                    maxi(0, 0)
                    maxi(0, 1)
                    recip(0, 0)
                    recip(0, 1)
                    for b in range(NB):
                        if b + 1 < NB:
                            maxi(b + 1, 0)
                            maxi(b + 1, 1)
                        for e in range(3):
                            if e < GROUPS[b]:
                                turned_lo(b, e)
                            if e < 2 and b + 1 < NB:
                                recip(b + 1, e)
                        if b >= 1:
                            out(b - 1)
                    out(NB - 1)
                    dve.wait_ge(a_hi, g * 2 + (pl + 1))
                    dve.tensor_tensor(aL[:, :], aT[:, :], aH[:, :].bitcast(F32), ALU.subtract).then_inc(a_lo, 1)

            with dve.Fori(0, KD) as d:
                for j in range(4):
                    split_lo((j + 1) % 2, d * 4 + (PAN_MRG + j + 2))
                    if j == 1:
                        dve.wait_ge(y_lo, d + 1)
                        for b in range(2):
                            w = slice(b * NT, (b + 1) * NT)
                            dve.wait_ge(sgf, d * 2 + (2 + b + 1))
                            dve.tensor_tensor(y[:, w], ps[:, b, :], gate_s[:, w], ALU.mult).then_inc(yf, 1)
                    if j == 3:
                        for b in range(2):
                            w = slice(b * NT, (b + 1) * NT)
                            dve.wait_ge(sga, d * 2 + (2 + b + 1))
                            dve.tensor_tensor(gate_s[:, w], ps[:, 4 + b, :], gate_s[:, w], ALU.mult).then_inc(ya, 1)
                        dve.wait_ge(ya, d * 2 + 4)
                        dve.tensor_tensor(y[:, :], y[:, :], gate_s[:, :], ALU.add).then_inc(ysum, 1)
                        dve.wait_ge(y_hi, d + 1)
                        dve.tensor_tensor(yL[:, :], y[:, :], yH[:, :].bitcast(F32), ALU.subtract).then_inc(y_lo, 1)

            with dve.Fori(0, KD // 2) as i:
                for n in range(2):
                    split_lo((n + 1) % 2, i * 2 + (PAN_OUT + n + 2))
                    for b in range(2):
                        dve.wait_ge(psum_filled, i * 4 + (FIL_OUT + 2 * n + b + 1))
                        dve.wait_ge(proj_in, 16 * 17)
                        xd = x_lat[:, bass.ds(i * 2 + n, 1), b * NT:(b + 1) * NT].rearrange("p a n -> p (a n)")
                        gt = gateT[:, 1, bass.ds(i * 2 + n, 1), 0:1].rearrange("p a n -> p (a n)")
                        dve.scalar_tensor_tensor(xd, ps[:, 2 * n + b, :], gt, xd, ALU.mult, ALU.add).then_inc(x_res, 1)
            dve.wait_ge(x_res, 4 + 2 * KD)
            norm_dve(N3, LAT, 2)
            ffn_dve(F2, LAT, PAN_FFN2, FIL_FFN2, 2, last=True)
            dve.wait_ge(F2["acc"], 2 + 16 * NPAIR)
            norm_dve(N4, LAT, 0, last=True)
            for t in range(NB):
                dve.wait_ge(o_turned, 2 * t + 2)
                if t >= 2:
                    dve.wait_ge(stored[t % 2], 16 * (t // 2))
                dve.tensor_copy(orow[t % 2][:, NT:D], ps[:, 2 * (t % 2) + 1, :]).then_inc(o_odd, 1)

        @block.gpsimd
        def _(pool):
            for z, (s, n) in enumerate(CREDIT):
                pool.memset(dummy[:, z:z + 1], 0.0).then_inc(s, n)

            def freed(saved, free, i, col):
                pool.wait_ge(saved, i * 32 + 32)
                pool.wait_ge(free, i + 1)
                pool.tensor_tensor(dummy[:, col:col + 1], dummy[:, 0:1], dummy[:, 0:1], ALU.add).then_inc(free, 1)

            pool.wait_ge(F1["acc"], 2 + 24 * NPAIR)
            pool.dma_start(x_scr, x_lat[:, :, :]).then_inc(x_saved, 16)
            pool.dma_start(cosT[:, :], T["rope_cos"]).then_inc(rope_in, 16)
            pool.dma_start(sinT[:, :], T["rope_sin"]).then_inc(rope_in, 16)
            with pool.Fori(0, NG) as g:
                pool.wait_ge(f_lo, g + 2)
                for z, part in enumerate((fH, fL)):
                    pool.dma_start(f_scr[bass.ds(g, 1), z, :, :].rearrange("a p n -> p (a n)"), part[:, :]).then_inc(f_saved, 16)
                freed(f_saved, f_free, g, 29)

            def sine(z, n, t0):
                pool.tensor_tensor(swp[z % 2][:, 0:n], swp[z % 2][:, 0:n], sinT[:, t0:t0 + n], ALU.mult).then_inc(sin_mul, 1)

            pool.wait_ge(rope_in, 32)
            for n in range(2):
                for b, (_, _, _, t0, m, _, g0) in enumerate(ALL):
                    z = 3 * n + b
                    if b < 2:
                        pool.wait_ge(swapped, 2 * n + b + 1)
                        sine(z, m, t0)
                    pool.wait_ge(k_lo, z + 1)
                    for q, part in enumerate((kH, kL)):
                        pool.dma_start(k_scr[q, n * P:(n + 1) * P, g0:g0 + m], part[z % 2][:, 0:m]).then_inc(k_saved[z % 2], 16)
            for vc in range(2):
                pool.wait_ge(v_lo, 3 * vc + 3)
                pool.dma_start(v_scr[:, 2 * vc:2 * vc + 2, :].rearrange("p v n -> p (v n)"),
                               vS[vc][:, :, :, :, :].rearrange("p v t z e -> p (v t z e)")).then_inc(v_saved, 16)

            pool.wait_ge(v_saved, 32)
            for s in range(2):
                pool.wait_ge(k_saved[s], 32 * 3)
            with pool.Fori(0, NKV) as g:
                pool.wait_ge(pv_done, g * (2 * NB) + 1)
                for z, part in enumerate((keyH, keyL)):
                    for h in range(2):
                        pool.dma_start(part[HEAD * h:HEAD * (h + 1), :], k_scr[z, bass.ds(g * HEAD, HEAD), :]).then_inc(kv_in, 16)
                pool.dma_start(val[:, :, :].rearrange("p t n -> p (t n)"), v_scr[:, bass.ds(g, 1), :].rearrange("p a n -> p (a n)")).then_inc(kv_in, 16)
                for pl in range(2):
                    for b in range(2):
                        pool.wait_ge(swapped, g * 4 + (4 + 2 * pl + b + 1))
                        sine(b, NT, b * NT)
                    for b in range(NB):
                        for h in range(2):
                            pool.wait_ge(rsum_set, g * (4 * NB) + ((pl * NB + b) * 2 + h + 1))
                            n = len(KEYS[b]) * P
                            z = slice(2 * (b % 2) + h, 2 * (b % 2) + h + 1)
                            pool.tensor_tensor(pr[b % 2][h][:, 0:n], pr[b % 2][h][:, 0:n], rsum[:, z].to_broadcast([P, n]), ALU.mult).then_inc(prob_set, 1)
                    pool.wait_ge(a_lo, g * 2 + (pl + 1))
                    for z, part in enumerate((aH, aL)):
                        pool.dma_start(a_scr[bass.ds(g * 2 + pl, 1), z, :, :].rearrange("a p n -> p (a n)"), part[:, :]).then_inc(a_saved, 16)
                    freed(a_saved, a_free, g * 2 + pl, 30)

            pool.wait_ge(a_saved, 32 * KD)
            pool.wait_ge(pv_done, 1 + 2 * NB * NKV)
            for z in range(2):
                for g in range(NG):
                    pool.dma_start(mF[z][:, g, :], f_scr[g, z]).then_inc(merge_in, 16)
                for k in range(KD):
                    pool.dma_start(mA[z][:, k, :], a_scr[k, z]).then_inc(merge_in, 16)
            with pool.Fori(0, KD) as d:
                pool.wait_ge(y_lo, d + 2)
                for z, part in enumerate((yH, yL)):
                    pool.dma_start(y_scr[bass.ds(d, 1), z, :, :].rearrange("a p n -> p (a n)"), part[:, :]).then_inc(y_saved, 16)
                freed(y_saved, y_free, d, 31)
            pool.wait_ge(y_saved, 32 * KD)
            pool.wait_ge(psum_filled, FIL_OUT)
            for z, part in enumerate((Yh, Yl)):
                for k in range(KD):
                    pool.dma_start(part[:, k, :], y_scr[k, z]).then_inc(proj_in, 16)
            pool.dma_start(x_lat[:, :, :], x_scr).then_inc(proj_in, 16)


_INS = {"x": (SEQ, D), "c": (D,), "ctx": (CTX, D), "c_ctx": (D,), "w_ada": (D, NMOD * D), "b_ada": (NMOD * D,),
        "g_ffn1": (D,), "w_ffn1_in": (D, 2 * FF), "w_ffn1_out": (FF, D), "g_mix": (D,), "w_in": (D, 4 * D),
        "attn_sink": (16,), "w_attn_branch": (D, D), "w_fourier_branch": (NG * P, D), "w_out": (D, D),
        "g_ffn2": (D,), "w_ffn2_in": (D, 2 * FF), "w_ffn2_out": (FF, D), "g_final": (D,)}


def shape_tables():
    import numpy as np
    i = np.arange(P)
    masks = np.zeros((P, 2, P), np.float32)
    masks[:, 0, :] = np.where(i[None, :] >= i[:, None], 0.0, NEG)
    masks[:, 1, :] = np.where(i[None, :] <= i[:, None], 0.0, NEG)
    alt = np.zeros((P, 2), np.float32)
    alt[:, 0] = 1.0 - 2.0 * (i % 2)
    rows = np.repeat(np.arange(SEQ // 64, dtype=np.float32), 64)
    colm = np.tile(np.arange(64, dtype=np.float32), SEQ // 64)
    inv = np.power(np.float32(10000.0), -np.arange(0, 32, 2, dtype=np.float32) / np.float32(32)).astype(np.float32)
    ang = np.concatenate([rows[:, None] * inv, colm[:, None] * inv], axis=-1).astype(np.float32).astype(np.float64)
    feat = (i % HEAD) // 2
    cos = np.cos(ang).T[feat].astype(np.float32)
    sin = (np.sin(ang).T[feat] * np.where(i % 2 == 0, -1.0, 1.0)[:, None]).astype(np.float32)
    chan = np.zeros((P, D), np.float64)
    a = 2 * np.pi * ((i[:, None] * i[None, :]) % P) / P
    chan[:, 0:P], chan[:, P:2 * P] = np.cos(a), np.sin(a)
    chan /= np.sqrt(float(SEQ * P))
    n, k = np.arange(SEQ), np.arange(NT)
    a = 2 * np.pi * ((n[:, None] * k[None, :]) % SEQ) / SEQ
    pos = np.concatenate([np.cos(a), np.sin(a)], axis=1)
    return {"ident": np.eye(P, dtype=np.float32), "masks": masks, "alt": alt, "rope_cos": cos, "rope_sin": sin,
            "dft_chan": chan.astype(np.float32), "dft_pos": pos.astype(np.float32)}


def kernel(**inputs):
    import numpy as _np
    import concourse.bacc as _bacc
    from concourse import mybir as _mybir
    from concourse.bass_utils import run_bass_kernel_spmd as _run

    nc = _bacc.Bacc("TRN2", target_bir_lowering=False, num_devices=1)
    arrays, T = {}, {}
    tensors = {name: _np.ascontiguousarray(inputs[name]).reshape(shape) for name, shape in _INS.items()}
    tensors.update(shape_tables())
    for name, a in tensors.items():
        arrays[f"in_{name}_dram"] = a
        T[name] = nc.dram_tensor(f"in_{name}_dram", a.shape, _mybir.dt.from_np(a.dtype), kind="ExternalInput").ap()
    T["out"] = nc.dram_tensor("out_0_dram", (SEQ, D), _mybir.dt.float32, kind="ExternalOutput").ap()
    build(nc, T)
    r = _run(nc, [arrays], core_ids=[0])
    return r.results[0]["out_0_dram"].reshape(1, SEQ, D)
```

```python
from contextlib import ExitStack

import concourse.bass as bass
from concourse import mybir

ACT = mybir.ActivationFunctionType
ALU = mybir.AluOpType
AX = mybir.AxisListType
F32 = mybir.dt.float32
R32 = mybir.dt.float32r

P = 128
D = 1024
KD = D // P
SEQ, CTX = 1024, 256
NT = 512
FF = 2816
NPAIR = FF // (2 * P)
HEAD = 64
NKV = 4
NB = SEQ // P
NKT = (SEQ + CTX) // P
NG = 4
NMOD = 9
K_OFF, V_OFF, U_OFF, GA_OFF, GF_OFF = 1024, 1280, 1536, 2048, 3072
EPS = 1e-6
NEG = -1e30

ROW_B, ROW_C, ROW_CCTX, ROW_G1, ROW_GM, ROW_G2, ROW_GF = 0, 72, 80, 88, 96, 104, 112
NROW = 120

PAN_FFN1 = 0
PAN_FOU = PAN_FFN1 + 6 * NPAIR
PAN_KV = PAN_FOU + NG + NB
PAN_ATT = PAN_KV + 4
PAN_MRG = PAN_ATT + 2 * NKV
PAN_OUT = PAN_MRG + 4 * KD
PAN_FFN2 = PAN_OUT + KD
PAN_END = PAN_FFN2 + 6 * NPAIR

FIL_FFN1 = 1
FIL_FOU = FIL_FFN1 + 36 * NPAIR
FIL_KV = FIL_FOU + (2 + NB) * NG + NB - 1 + NG
FIL_ATT = FIL_KV + 18
FIL_MRG = FIL_ATT + 4 * NKV
FIL_OUT = FIL_MRG + 8 * KD
FIL_FFN2 = FIL_OUT + 2 * KD

KEYS = [[k for k in (b - 1, b, b + 1) if 0 <= k < NB] + [NB, NB + 1] for b in range(NB)]
GROUPS = [-(-2 * len(k) // 4) for k in KEYS]
GROUP0 = [sum(GROUPS[:b]) for b in range(NB)]
NGROUP = sum(GROUPS)


def build(nc, T):
    with ExitStack() as ctx:
        base = 16512

        def at(name, off, shape, dt=F32):
            return nc.alloc_sbuf_tensor_at(name, shape, dt, offset=base + off)

        def sem(name):
            return ctx.enter_context(nc.semaphore(name))

        HH, HL = 0, 32768
        RING = 65536
        CON = RING + 6 * 4096
        POOL = CON + 6272
        Hh = at("Hh", HH, [P, KD, SEQ], R32)
        Hl = at("Hl", HL, [P, KD, SEQ], R32)
        raw = [at(f"raw{s}", RING + s * 4096, [P, D]) for s in range(2)]
        whi = [at(f"whi{s}", RING + (2 + s) * 4096, [P, D], R32) for s in range(2)]
        wlo = [at(f"wlo{s}", RING + (4 + s) * 4096, [P, D], R32) for s in range(2)]
        c = CON
        cols = at("cols", c, [P, NROW]); c += 480
        modT = at("modT", c, [P, NMOD, KD, 2]); c += 576
        gainT = at("gainT", c, [P, 3, KD, 2]); c += 192
        gateT = at("gateT", c, [P, 3, KD, 2]); c += 192
        cond = at("cond", c, [P, KD, 2]); c += 64
        epsT = at("epsT", c, [P, 1]); c += 32
        dummy = at("dummy", c, [P, 32]); c += 128
        ones = at("ones", c, [P, P]); c += 512
        ident = at("ident", c, [P, P]); c += 512
        identR = at("identR", c, [P, P], R32); c += 512
        mask_f = at("mask_f", c, [P, 2, P]); c += 1024
        maskR = at("maskR", c, [P, 2, P], R32); c += 1024
        altR = at("altR", c, [P, 2], R32); c += 32
        alt_f = at("alt_f", c, [P, 2]); c += 32
        sink_f = at("sink_f", c, [P, 16, 2]); c += 128
        sink_r = at("sink_r", c, [P, 16]); c += 64
        sinkH = at("sinkH", c, [P, 16, 2], R32); c += 128
        sinkL = at("sinkL", c, [P, 16, 2], R32); c += 128
        rows = at("rows", c, [NROW, P]); c += 512
        assert c <= POOL, c - POOL
        x_lat = at("x_lat", POOL, [P, KD, SEQ])
        x_ctx = at("x_ctx", POOL + 32768, [P, KD, CTX])
        Ch = at("Ch", POOL + 40960, [P, KD, CTX], R32)
        Cl = at("Cl", POOL + 49152, [P, KD, CTX], R32)
        NRM = POOL + 57344
        sq = [at(f"sq{s}", NRM + 2048 * s, [P, NT]) for s in range(2)]
        tn = [at(f"tn{s}", NRM + 4096 + 2048 * s, [P, NT]) for s in range(2)]
        rms = [at(f"rms{s}", NRM + 8192 + 2048 * s, [P, NT]) for s in range(2)]
        GB = NRM + 16384
        gH = at("gH", GB, [P, 2, SEQ + CTX], R32)
        gL = at("gL", GB + 10240, [P, 2, SEQ + CTX], R32)
        act_t = at("act_t", GB + 20480, [P, SEQ + CTX])
        rstd = [at(f"rstd{b}", GB + 32768 + 2048 * b, [P, NT]) for b in range(3)]
        x_in = at("x_in", HH, [P, NKT, D])
        ada = [at(f"ada{s}", GB + 4096 * s, [P, D]) for s in range(8)]
        adaH = whi + [at(f"adaH{s}", HL + 8192 + 4096 * s, [P, D], R32) for s in range(2)]
        adaL = wlo + [at(f"adaL{s}", HL + 16384 + 4096 * s, [P, D], R32) for s in range(2)]
        mod_row = at("mod_row", NRM, [4, D])
        condS = at("condS", NRM + 12288, [P, KD, 4], R32)
        pick = at("pick", NRM + 12544, [4, 2])
        xcH = at("xcH", POOL, [P, NG, NB, 2 * P], R32)
        xcL = at("xcL", GB + 8192, [P, NG, NB, 2 * P], R32)
        chan_f = at("chan_f", POOL + 32768, [P, 2 * P])
        chanH = at("chanH", POOL + 33792, [P, 2 * P], R32)
        chanL = at("chanL", POOL + 34816, [P, 2 * P], R32)
        uH = [at(f"uH{s}", NRM + 8192 * s, [P, SEQ], R32) for s in range(2)]
        uL = [at(f"uL{s}", NRM + 8192 * s + 4096, [P, SEQ], R32) for s in range(2)]
        fT = at("fT", NRM, [P, SEQ])
        fH = at("fH", NRM + 4096, [P, SEQ], R32)
        fL = at("fL", NRM + 8192, [P, SEQ], R32)
        fB = at("fB", NRM + 12288, [P, NT])
        ROPE = GB
        cosT = at("cosT", ROPE, [P, SEQ])
        sinT = at("sinT", ROPE + 4096, [P, SEQ])
        swp = [at(f"swp{s}", ROPE + 8192 + 2048 * s, [P, NT]) for s in range(2)]
        rot = [at(f"rot{s}", ROPE + 12288 + 2048 * s, [P, NT]) for s in range(2)]
        kH = [at(f"kH{s}", POOL + 2048 * s, [P, NT], R32) for s in range(2)]
        kL = [at(f"kL{s}", POOL + 4096 + 2048 * s, [P, NT], R32) for s in range(2)]
        vT = [at(f"vT{s}", POOL + 8192 + 5120 * s, [P, NKT, P]) for s in range(2)]
        vS = [at(f"vS{s}", POOL + 18432 + 10240 * s, [P, 2, NKT, 2, HEAD], R32) for s in range(2)]
        o = POOL
        keyH = at("keyH", o, [P, SEQ + CTX], R32); o += 5120
        keyL = at("keyL", o, [P, SEQ + CTX], R32); o += 5120
        val = at("val", o, [P, NKT, P], R32); o += 5120
        qS = [at(f"qS{h}", o + 4096 * h, [P, SEQ], R32) for h in range(2)]; o += 8192
        pr = [[at(f"pr{s}{h}", o + (2 * s + h) * 2592, [P, 642]) for h in range(2)] for s in range(2)]
        o += 4 * 2592
        ptH = [at(f"ptH{s}", o + 5120 * s, [P, 5 * 2 * P], R32) for s in range(2)]; o += 10240
        ptL = [at(f"ptL{s}", o + 5120 * s, [P, 5 * 2 * P], R32) for s in range(2)]; o += 10240
        oLow = [at(f"oLow{s}", o + 1024 * s, [HEAD, 2, P]) for s in range(2)]; o += 2048
        aT = at("aT", o, [P, SEQ]); o += 4096
        aH = at("aH", o, [P, SEQ], R32); o += 4096
        aL = at("aL", o, [P, SEQ], R32); o += 4096
        dg = [[at(f"dg{s}{h}", o + 1024 * s + 512 * h, [P, P]) for h in range(2)] for s in range(2)]
        o += 2048
        nmax = at("nmax", o, [P, 4]); o += 32
        lsum = at("lsum", o, [P, 4]); o += 32
        rsum = at("rsum", o, [P, 4]); o += 32
        assert o <= ROPE
        qS = [qS, [at(f"qT{h}", ROPE + 16384 + 4096 * h, [P, SEQ], R32) for h in range(2)]]
        y = at("y", POOL, [P, KD, SEQ])
        gate_a = at("gate_a", POOL + 32768, [P, KD, SEQ])
        fouH = at("fouH", POOL + 98304, [P, NG, SEQ], R32)
        fouL = at("fouL", ROPE, [P, NG, SEQ], R32)
        A_AT = [(POOL + 90112, POOL + 94208), (POOL + 65536, POOL + 69632), (POOL + 98304, POOL + 102400), (POOL + 106496, POOL + 110592),
                (ROPE, ROPE + 4096), (ROPE + 8192, ROPE + 12288), (HH + 24576, HL + 24576), (HH + 28672, HL + 28672)]
        attH = [at(f"attH{k}", A_AT[k][0], [P, SEQ], R32) for k in range(KD)]
        attL = [at(f"attL{k}", A_AT[k][1], [P, SEQ], R32) for k in range(KD)]
        assert base + POOL + 114688 <= 229368
        YK = KD - 2
        Yh = at("Yh", HH, [P, YK, SEQ], R32)
        Yl = at("Yl", HL, [P, YK, SEQ], R32)
        mergedH = [Yh[:, k, :] for k in range(YK)] + [at(f"YhE{k}", POOL + 32768 + 8192 * k, [P, SEQ], R32)[:, :] for k in range(2)]
        mergedL = [Yl[:, k, :] for k in range(YK)] + [at(f"YlE{k}", POOL + 36864 + 8192 * k, [P, SEQ], R32)[:, :] for k in range(2)]
        oT = at("oT", HH, [P, KD, SEQ])
        orow = [at(f"orow{s}", HL + 4096 * s, [P, D]) for s in range(2)]

        ps = ctx.enter_context(nc.psum_tensor("ps", [P, 8, NT], F32))

        x_scr = nc.dram_tensor("x_scr", [P, KD, SEQ], F32).ap()
        f_scr = nc.dram_tensor("f_scr", [NG, 2, P, SEQ], R32).ap()
        k_scr = nc.dram_tensor("k_scr", [2, 2 * P, SEQ + CTX], R32).ap()
        v_scr = nc.dram_tensor("v_scr", [P, NKV, NKT * P], R32).ap()
        a_scr = nc.dram_tensor("a_scr", [KD, 2, P, SEQ], R32).ap()

        rows_in = sem("rows_in"); const_in = sem("const_in")
        x_tile_in = [sem(f"x_tile_in{t}") for t in range(NKT)]
        ones_set = sem("ones_set"); consts_set = sem("consts_set")
        cols_set = sem("cols_set"); cond_set = sem("cond_set")
        x_turned = sem("x_turned"); x_even = sem("x_even"); x_odd = sem("x_odd")
        ada_in = [sem(f"ada_in{s}") for s in range(8)]
        ada_used = sem("ada_used"); mod_set = sem("mod_set"); ada_hi = sem("ada_hi"); ada_lo = sem("ada_lo"); row_out = sem("row_out"); mod_turned = sem("mod_turned"); ident_in = sem("ident_in"); gain_set = sem("gain_set")
        panel_in = [sem(f"panel_in{s}") for s in range(2)]
        panel_hi = sem("panel_hi"); panel_split = sem("panel_split"); psum_filled = sem("psum_filled")

        def norm_sems(j):
            return {n: sem(f"n{j}_{n}") for n in ("sq", "ss", "rms", "rstd", "t", "hi", "lo")}

        def ffn_sems(j):
            return {n: sem(f"f{j}_{n}") for n in ("silu", "prod", "ghi", "glo", "acc")}

        N1, N2, N3, N4 = (norm_sems(j) for j in range(1, 5))
        F1, F2 = ffn_sems(1), ffn_sems(2)
        x_saved = sem("x_saved")
        u_hi = sem("u_hi"); u_lo = sem("u_lo"); xc_hi = sem("xc_hi"); xc_lo = sem("xc_lo")
        fb_out = sem("fb_out"); f_sum = sem("f_sum"); f_hi = sem("f_hi"); f_lo = sem("f_lo"); f_saved = sem("f_saved"); chan_in = sem("chan_in"); chan_hi = sem("chan_hi"); chan_lo = sem("chan_lo")
        rope_in = sem("rope_in"); swapped = sem("swapped"); sin_mul = sem("sin_mul"); rot_set = sem("rot_set")
        k_hi = sem("k_hi"); k_lo = sem("k_lo"); k_saved = [sem(f"k_saved{s}") for s in range(2)]
        v_out = sem("v_out"); v_hi = sem("v_hi"); v_lo = sem("v_lo"); v_saved = sem("v_saved"); cos_mul = sem("cos_mul"); a_saved = sem("a_saved")
        key_in = sem("key_in"); val_in = sem("val_in"); q_hi = sem("q_hi"); q_lo = sem("q_lo")
        qk_done = sem("qk_done"); max_set = sem("max_set"); exp_set = sem("exp_set"); rsum_set = sem("rsum_set")
        prob_set = sem("prob_set"); pt_turned = sem("pt_turned"); pt_hi = sem("pt_hi"); pt_lo = sem("pt_lo")
        pv_done = sem("pv_done"); o_low = sem("o_low"); o_out = sem("o_out")
        a_hi = sem("a_hi"); a_lo = sem("a_lo")
        fou_in = sem("fou_in"); att_in = sem("att_in"); att_in_late = sem("att_in_late"); sgf = sem("sgf"); yf = sem("yf"); sga = sem("sga"); ya = sem("ya"); ysum = sem("ysum")
        y_hi = sem("y_hi"); y_lo = sem("y_lo"); x_back = sem("x_back")
        x_res = sem("x_res")
        o_turned = sem("o_turned"); o_even = sem("o_even"); o_odd = sem("o_odd"); stored = [sem(f"stored{s}") for s in range(2)]

        CREDIT = [(panel_split, 2), (F1["silu"], 3), (F1["prod"], 3), (F1["glo"], 3), (F1["acc"], 4),
                  (F2["silu"], 2), (F2["prod"], 2), (F2["glo"], 2), (F2["acc"], 4),
                  (exp_set, 2), (pt_lo, 2), (o_out, 1),
                  (mod_set, 1), (mod_turned, 1), (pv_done, 1), (sgf, 2), (yf, 2), (sga, 4), (ya, 4), (x_res, 4)]

        w_in = {1: T["w_ffn1_in"], 2: T["w_ffn2_in"]}
        w_out = {1: T["w_ffn1_out"], 2: T["w_ffn2_out"]}
        LAT = [(x_lat, Hh, Hl, 0, NT, 0, 0), (x_lat, Hh, Hl, NT, NT, 0, NT)]
        ALL = LAT + [(x_ctx, Ch, Cl, 0, CTX, 1, SEQ)]

        def chunks(w):
            return w.rearrange("(k p) n -> p k n", p=P)

        def k3(t):
            return t[:, :].rearrange("p (k n) -> p k n", k=KD)

        def panel_wait(eng, p0, per, i, j):
            eng.wait_ge(panel_split, 2 + p0 + j + 1 + per * i if not isinstance(i, int) else 2 + p0 + per * i + j + 1)

        block = ctx.enter_context(nc.Block())

        @block.sync
        def _(sp):
            sp.dma_start(rows[ROW_B:ROW_C, :], T["b_ada"].rearrange("(r n) -> r n", n=P)).then_inc(rows_in, 16)
            for r, name in ((ROW_C, "c"), (ROW_CCTX, "c_ctx"), (ROW_G1, "g_ffn1"), (ROW_GM, "g_mix"),
                            (ROW_G2, "g_ffn2"), (ROW_GF, "g_final")):
                sp.dma_start(rows[r:r + KD, :], T[name].rearrange("(r n) -> r n", n=P)).then_inc(rows_in, 16)
            sp.dma_start(ident[:, :], T["ident"]).then_inc(ident_in, 16)
            for t in range(NKT):
                src = T["x"][t * P:(t + 1) * P, :] if t < NB else T["ctx"][(t - NB) * P:(t - NB + 1) * P, :]
                sp.dma_start(x_in[:, t, :], src).then_inc(x_tile_in[t], 16)

            def ada_load(m, k):
                sp.dma_start(ada[k][:, :], T["w_ada"][k * P:(k + 1) * P, bass.ds(m, D)]).then_inc(ada_in[k], 16)
            for k in range(KD):
                ada_load(0, k)
            with sp.Fori(1, NMOD) as m:
                at_m = sp.snap(m * D)
                for k in range(KD):
                    sp.wait_ge(ada_lo, m * KD + (k - KD + 1))
                    ada_load(at_m, k)
            sp.dma_start(mask_f[:, :, :], T["masks"]).then_inc(const_in, 16)
            sp.dma_start(alt_f[:, :], T["alt"]).then_inc(const_in, 16)
            sp.dma_start(sink_r[:, :], T["attn_sink"].partition_broadcast(P)).then_inc(a_saved, 16)

            def load(par, n, dst, src, at):
                at = at if isinstance(at, int) else sp.snap(at)
                sp.wait_ge(panel_split, n)
                sp.dma_start(dst, src(at)).then_inc(panel_in[par], 16)

            def ffn_load(j, p0):
                win, wout = chunks(w_in[j]), chunks(w_out[j])
                with sp.Fori(0, NPAIR) as i:
                    for fl in range(2):
                        for half in range(2):
                            s = 2 * fl + half
                            load(s % 2, i * 6 + (p0 + s + 1), k3(raw[s % 2]),
                                 lambda at: win[:, :, bass.ds(at, P)], i * (2 * P) + (half * FF + fl * P))
                    for half in range(2):
                        load(half, i * 6 + (p0 + 4 + half + 1), raw[half][:, :].rearrange("p (f n) -> p f n", f=2),
                             lambda at, half=half: wout[:, bass.ds(at, 2), half * NT:(half + 1) * NT], i * 2)
            ffn_load(1, PAN_FFN1)
            win = chunks(T["w_in"])
            for g in range(NG):
                load(g % 2, PAN_FOU + g + 1, k3(raw[g % 2]), lambda at, g=g: win[:, :, U_OFF + g * P:U_OFF + (g + 1) * P], 0)
            for n in range(NB):
                load(n % 2, PAN_FOU + NG + n + 1, raw[n % 2][:, :], lambda at, n=n: T["dft_pos"][n * P:(n + 1) * P, :], 0)
            for n in range(4):
                load(n % 2, PAN_KV + n + 1, k3(raw[n % 2]), lambda at, n=n: win[:, :, K_OFF + n * P:K_OFF + (n + 1) * P], 0)
            def att_load(n):
                load(n % 2, PAN_ATT + n + 1, k3(raw[n % 2]), lambda at: win[:, :, n * P:(n + 1) * P], 0)

            def key_load(g):
                for z, part in enumerate((keyH, keyL)):
                    for h in range(2):
                        sp.dma_start(part[HEAD * h:HEAD * (h + 1), :].bitcast(F32), k_scr[z, g * HEAD:(g + 1) * HEAD, :].bitcast(F32)).then_inc(key_in, 16)

            def val_load(g):
                sp.dma_start(val[:, :, :].rearrange("p t n -> p (t n)").bitcast(F32), v_scr[:, g, :].bitcast(F32)).then_inc(val_in, 16)

            att_load(0)
            att_load(1)
            for s in range(2):
                sp.wait_ge(k_saved[s], 32 * 3)
            sp.wait_ge(v_saved, 32)
            sp.wait_ge(v_lo, 6)
            key_load(0)
            val_load(0)
            att_load(2)
            att_load(3)
            wf, wa, wo = chunks(T["w_fourier_branch"]), chunks(T["w_attn_branch"]), chunks(T["w_out"])

            def fou_gate_load(d, z=0):
                load(0, d * 2 + (PAN_MRG + 2 * z + 1), k3(raw[0]), lambda at: win[:, :, bass.ds(at, P)], d * P + (z * P + GF_OFF))

            def fou_load(d, z=0):
                load(1, d * 2 + (PAN_MRG + 2 * z + 2), raw[1][:, 0:NG * P].rearrange("p (k n) -> p k n", k=NG), lambda at: wf[:, :, bass.ds(at, P)], d * P + z * P)
            sp.wait_ge(f_saved, 32 * NG)
            sp.dma_start(fouH[:, :, :].bitcast(F32), f_scr[:, 0, :, :].rearrange("g p n -> p g n").bitcast(F32)).then_inc(fou_in, 16)
            for j in range(2 * NKV):
                if j + 4 < 2 * NKV:
                    att_load(j + 4)
                if j == 2 * NKV - 2:
                    fou_gate_load(0)
                if j == 2 * NKV - 1:
                    fou_load(0)
                    sp.wait_ge(q_lo, 8 * NKV)
                    sp.dma_start(fouL[:, :, :].bitcast(F32), f_scr[:, 1, :, :].rearrange("g p n -> p g n").bitcast(F32)).then_inc(fou_in, 16)
                if j % 2 and j + 1 < 2 * NKV:
                    sp.wait_ge(qk_done, 2 * NB * (j + 1))
                    key_load(j // 2 + 1)
                    sp.wait_ge(pv_done, 1 + NB * (j + 1))
                    val_load(j // 2 + 1)
                sp.wait_ge(a_lo, 2 * j + 2)
                for z, part in enumerate((aH, aL)):
                    sp.dma_start(a_scr[j, z, :, :].bitcast(F32), part[:, :].bitcast(F32)).then_inc(a_saved, 16)
            with sp.Fori(0, KD - 1) as d:
                fou_gate_load(d, 1)
                fou_load(d, 1)
            with sp.Fori(0, KD // 2) as i:
                for n in range(2):
                    load(n, i * 2 + (PAN_MRG + 2 * KD + n + 1), k3(raw[n]), lambda at: win[:, :, bass.ds(at, P)], i * (2 * P) + (GA_OFF + n * P))
            with sp.Fori(0, KD // 2) as i:
                for n in range(2):
                    load(n, i * 2 + (PAN_MRG + 3 * KD + n + 1), k3(raw[n]), lambda at: wa[:, :, bass.ds(at, P)], i * (2 * P) + n * P)
            with sp.Fori(0, KD // 2) as i:
                for n in range(2):
                    load(n, i * 2 + (PAN_OUT + n + 1), k3(raw[n]), lambda at: wo[:, :, bass.ds(at, P)], i * (2 * P) + n * P)
            ffn_load(2, PAN_FFN2)
            for t in range(NB):
                sp.wait_ge(o_even, t + 1)
                sp.wait_ge(o_odd, t + 1)
                sp.dma_start(T["out"][t * P:(t + 1) * P, :], orow[t % 2][:, :]).then_inc(stored[t % 2], 16)
            for s in range(2):
                sp.wait_ge(stored[s], 16 * NB // 2)

        @block.tensor
        def _(pe):
            pe.wait_ge(rows_in, 7 * 16)
            pe.wait_ge(ident_in, 16)
            pe.transpose(ps[:, 6, 0:NROW], rows[:, :], ident[0:NROW, 0:NROW]).then_inc(psum_filled, 1)
            for t in range(NKT):
                pe.wait_ge(x_tile_in[t], 16)
                for half in range(2):
                    if t >= 2:
                        pe.wait_ge(x_odd if half else x_even, t - 1)
                    for k in range(4):
                        kk = half * 4 + k
                        mm = pe.transpose(ps[:, 2 * (t % 2) + half, k * P:(k + 1) * P], x_in[:, t, kk * P:(kk + 1) * P], ident[:, :])
                    mm.then_inc(x_turned, 1)
            def norm_mm(S, blocks):
                for b, (x, _, _, t0, n, _, _) in enumerate(blocks):
                    if b >= 2:
                        pe.wait_ge(S["rms"], b - 1)
                    for k in range(KD):
                        pe.wait_ge(S["sq"], b * KD + k + 1)
                        pe.matmul(ps[:, 6 + b % 2, 0:n], ones[:, :], sq[k % 2][:, 0:n], start=(k == 0),
                                  stop=(k == KD - 1)).then_inc(S["ss"], 1)

            def three(out, lh, ll, rh, rl, start, stop):
                pe.matmul(out, lh, rh, start=start, stop=False)
                pe.matmul(out, lh, rl, start=False, stop=False)
                return pe.matmul(out, ll, rh, start=False, stop=stop)

            def project(bank, s, hi, lo, t0, n, nk=KD, waits={}):
                for k in range(nk):
                    rh, rl = (t[k][:, t0:t0 + n] if isinstance(t, list) else t[:, k, t0:t0 + n] for t in (hi, lo))
                    if k in waits:
                        pe.wait_ge(*waits[k])
                    mm = three(ps[:, bank, 0:n], whi[s][:, k * P:(k + 1) * P], wlo[s][:, k * P:(k + 1) * P],
                               rh, rl, k == 0, k == nk - 1)
                mm.then_inc(psum_filled, 1)

            def ffn_mm(S, blocks, p0, NS):
                nb = len(blocks)
                with pe.Fori(0, NPAIR) as i:
                    for fl in range(2):
                        for half in range(2):
                            s = 2 * fl + half
                            pe.wait_ge(panel_split, i * 6 + (2 + p0 + s + 1))
                            for b, (_, hi, lo, t0, n, _, _) in enumerate(blocks):
                                pe.wait_ge(NS["lo"], KD * (b + 1))
                                pe.wait_ge(S["prod" if half else "silu"], i * (2 * nb) + (fl * nb + b + 1))
                                if half and fl == 0:
                                    pe.wait_ge(S["acc"], i * (8 * nb) + 4)
                                project(3 * half + b, s % 2, hi, lo, t0, n)
                    for half in range(2):
                        pe.wait_ge(panel_split, i * 6 + (2 + p0 + 4 + half + 1))
                        for b, (_, _, _, _, n, _, g0) in enumerate(blocks):
                            if half == 0:
                                pe.wait_ge(S["glo"], i * (2 * nb) + (nb + nb + b + 1))
                            for d in range(4):
                                pe.wait_ge(S["acc"], i * (8 * nb) + ((half * nb + b) * 4 + d + 1))
                                for fl in range(2):
                                    w = slice(fl * NT + d * P, fl * NT + (d + 1) * P)
                                    mm = three(ps[:, 4 + d, 0:n], whi[half][:, w], wlo[half][:, w],
                                               gH[:, fl, g0:g0 + n], gL[:, fl, g0:g0 + n], fl == 0, fl == 1)
                                mm.then_inc(psum_filled, 1)

            pe.wait_ge(ones_set, 1)
            pe.wait_ge(cols_set, 1)
            norm_mm(N1, ALL)

            pe.wait_ge(cond_set, 4)
            pe.wait_ge(N1["rms"], 3)

            def ada_mm(m, k):
                pe.wait_ge(ada_lo, m * KD + (k + 1))
                if k == 0 and not isinstance(m, int):
                    pe.wait_ge(row_out, m * 2)
                for half in range(2):
                    w = slice(half * NT, (half + 1) * NT)
                    pe.matmul(ps[0:4, 4 + half, :], condS[:, k, :], adaH[k % 4][:, w], start=(k == 0), stop=False)
                    mm = pe.matmul(ps[0:4, 4 + half, :], condS[:, k, :], adaL[k % 4][:, w], start=False, stop=(k == KD - 1))
                mm.then_inc(ada_used, 1)

            def ada_turn(m):
                pe.wait_ge(row_out, m * 2)
                pe.wait_ge(mod_set, m)
                for d in range(KD):
                    mm = pe.matmul(ps[:, 7, 2 * d:2 * d + 2], mod_row[:, d * P:(d + 1) * P], pick[:, :],
                                   start=(d == 0), stop=True, skip_group_check=True)
                mm.then_inc(mod_turned, 1)
            for k in range(KD):
                ada_mm(0, k)
            with pe.Fori(1, NMOD) as m:
                for k in range(KD):
                    ada_mm(m, k)
                    if k == 1:
                        ada_turn(m)
            ada_turn(NMOD)
            pe.wait_ge(N1["rms"], 3)
            ffn_mm(F1, ALL, PAN_FFN1, N1)
            pe.wait_ge(F1["acc"], 4 + 24 * NPAIR)
            norm_mm(N2, ALL)

            pe.wait_ge(consts_set, 1)
            pe.wait_ge(N2["rms"], 3)

            def u_project(g):
                pe.wait_ge(panel_split, 2 + PAN_FOU + g + 1)
                for b, (_, hi, lo, t0, n, _, _) in enumerate(LAT):
                    pe.wait_ge(N2["lo"], KD * (b + 1))
                    if g >= 2:
                        pe.wait_ge(u_lo, 2 * (g - 2) + b + 1)
                    project(2 * (g % 2) + b, g % 2, hi, lo, t0, n)

            def u_channels(g):
                for n in range(NB):
                    if n % 4 == 0:
                        pe.wait_ge(u_lo, 2 * g + n // 4 + 1)
                    if g * NB + n >= 4:
                        pe.wait_ge(xc_lo, g * NB + n - 3)
                    w = slice(n * P, (n + 1) * P)
                    three(ps[:, 4 + n % 4, 0:2 * P], uH[g % 2][:, w], uL[g % 2][:, w], chanH[:, :], chanL[:, :],
                          True, True).then_inc(psum_filled, 1)
            u_project(0)
            u_project(1)
            pe.wait_ge(chan_lo, 1)
            u_channels(0)
            u_project(2)
            u_channels(1)
            u_project(3)
            u_channels(2)
            u_channels(3)
            pe.wait_ge(u_lo, 2 * NG)
            for n in range(NB):
                pe.wait_ge(panel_split, 2 + PAN_FOU + NG + n + 1)
                st, sp_ = n == 0, n == NB - 1
                for g in range(NG):
                    if st:
                        pe.wait_ge(xc_lo, NG * NB)
                    def alternating():
                        pe.matmul(ps[:, 2 * g + 1, 0:2], xcH[:, g, n, 0:P], altR[:, :], start=False, stop=False, skip_group_check=True)
                        return pe.matmul(ps[:, 2 * g + 1, 0:2], xcL[:, g, n, 0:P], altR[:, :], start=False, stop=False, skip_group_check=True)
                    if not st:
                        alternating()
                    for z in range(2):
                        mm = three(ps[:, 2 * g + z, :], xcH[:, g, n, z * P:(z + 1) * P], xcL[:, g, n, z * P:(z + 1) * P],
                                   whi[n % 2][:, z * NT:(z + 1) * NT], wlo[n % 2][:, z * NT:(z + 1) * NT], st, sp_)
                    if st:
                        mm = alternating()
                    if sp_ or g == NG - 1:
                        mm.then_inc(psum_filled, 1)

            for n in range(4):
                pe.wait_ge(panel_split, 2 + PAN_KV + n + 1)
                for b, (_, hi, lo, t0, m, _, _) in enumerate(ALL):
                    pe.wait_ge(N2["lo"], KD * (b + 1))
                    bank = 3 * (n % 2) + b
                    if n < 2:
                        pe.wait_ge(f_sum, bank // 2 + 1)
                    else:
                        pe.wait_ge(rot_set, 3 * (n - 2) + b + 1)
                    project(bank, n % 2, hi, lo, t0, m)
            pe.wait_ge(f_sum, NG)
            for e in range(6):
                vc, g0 = e // 3, 4 * (e % 3)
                pe.wait_ge(v_out, 3 * vc + e % 3 + 1)
                if e >= 2:
                    pe.wait_ge(v_lo, e - 1)
                for t in range(min(4, NKT - g0)):
                    mm = pe.transpose(ps[:, 6 + e % 2, t * P:(t + 1) * P], vT[vc][:, g0 + t, :], ident[:, :])
                mm.then_inc(psum_filled, 1)

            pe.wait_ge(v_lo, 6)

            def q_part(pj, b, bank, k0, k1):
                s = pj % 2
                for k in range(k0, k1):
                    mm = three(ps[:, bank, :], whi[s][:, k * P:(k + 1) * P], wlo[s][:, k * P:(k + 1) * P],
                               Hh[:, k, b * NT:(b + 1) * NT], Hl[:, k, b * NT:(b + 1) * NT], k == 0, k == KD - 1)
                if k1 == KD:
                    mm.then_inc(psum_filled, 1)

            def scores(g, pj, b, h):
                keys = KEYS[b]
                loc = len(keys) - 2
                if h == 0:
                    pe.wait_ge(q_lo, g * 8 + (pj * 4 + (b // 4 + 1) * 2))
                pe.wait_ge(exp_set, g * (4 * NB) + ((pj * NB + b) * 2 + h + 1))
                S = ps[:, 2 * h:2 * h + 2, :].rearrange("p a n -> p (a n)")
                q = qS[pj % 2][h][:, b * P:(b + 1) * P]
                k0 = keys[0] * P
                runs = [(0, k0, loc * P)]
                if loc == 3:
                    runs += [(384, SEQ, P), (512, SEQ + P, P)]
                else:
                    runs += [(256, SEQ, 2 * P)]
                for r0, c0, w in runs:
                    pe.matmul(S[:, r0:r0 + w], q, keyH[:, c0:c0 + w], start=(r0 % NT == 0), stop=False, skip_group_check=True)
                    pe.matmul(S[:, r0:r0 + w], q, keyL[:, c0:c0 + w], start=False, stop=True, skip_group_check=True)
                if b > 0:
                    pe.matmul(S[:, 0:P], identR[:, :], maskR[:, 0, :], start=False, stop=True, skip_group_check=True)
                if b < NB - 1:
                    r0 = (loc - 1) * P
                    pe.matmul(S[:, r0:r0 + P], identR[:, :], maskR[:, 1, :], start=False, stop=True, skip_group_check=True)
                r0 = len(keys) * P
                hd = bass.ds(g * 4 + (2 * pj + h), 1)
                pe.matmul(S[:, r0:r0 + 2], identR[:, :], sinkH[:, hd, :], start=(r0 % NT == 0), stop=False, skip_group_check=True)
                pe.matmul(S[:, r0:r0 + 2], identR[:, :], sinkL[:, hd, :], start=False, stop=True,
                          skip_group_check=True).then_inc(qk_done, 1)

            def turn(g, pl, b, e):
                if e >= GROUPS[b]:
                    return
                if e == 0:
                    pe.wait_ge(prob_set, g * (4 * NB) + ((pl * NB + b) * 2 + 2))
                tiles = [(t, h) for t in range(len(KEYS[b])) for h in range(2)]
                pe.wait_ge(pt_lo, g * (2 * NGROUP) + (pl * NGROUP + GROUP0[b] + e + 1))
                for z, (t, h) in enumerate(tiles[4 * e:4 * e + 4]):
                    mm = pe.matmul(ps[:, 4 + (GROUP0[b] + e) % 2, z * P:(z + 1) * P], pr[b % 2][h][:, t * P:(t + 1) * P], dg[b % 2][h][:, :],
                                   start=(z == 0), stop=True, skip_group_check=True)
                mm.then_inc(pt_turned, 1)

            def mix(g, pl, b):
                keys = KEYS[b]
                pe.wait_ge(pt_lo, g * (2 * NGROUP) + (2 + pl * NGROUP + GROUP0[b] + GROUPS[b]))
                pe.wait_ge(o_out, g * (2 * NB) + (pl * NB + b + 1))
                if pl == 0 and b == 0:
                    pe.wait_ge(val_in, g * 16 + 16)
                for t, kt in enumerate(keys):
                    pe.matmul(ps[:, 7, 0:2 * P], val[:, kt, :], ptH[b % 2][:, t * 2 * P:(t + 1) * 2 * P], start=(t == 0), stop=False)
                    mm = pe.matmul(ps[:, 7, 0:2 * P], val[:, kt, :], ptL[b % 2][:, t * 2 * P:(t + 1) * 2 * P],
                                   start=False, stop=(t == len(keys) - 1))
                mm.then_inc(pv_done, 1)

            def pair(g, pl, last):
                fill = {0: (0, 0, 3), 1: (0, 3, 6), 2: (0, 6, 8), 4: (1, 0, 2), 5: (1, 2, 4), 6: (1, 4, 6), 7: (1, 6, 8)}
                for b in range(NB):
                    nxt = (pl, b + 1) if b + 1 < NB else (pl + 1, 0)
                    more = not (last and b == NB - 1)
                    if more and nxt != (2, 0):
                        scores(g, *nxt, 0)
                    turn(g, pl, b, 0)
                    if more and nxt != (2, 0):
                        scores(g, *nxt, 1)
                    turn(g, pl, b, 1)
                    if b >= 1:
                        mix(g, pl, b - 1)
                    if more and nxt == (2, 0):
                        pe.wait_ge(key_in, g * 64 + 128)
                        scores(g, *nxt, 0)
                        scores(g, *nxt, 1)
                    turn(g, pl, b, 2)
                    if b in fill and not last:
                        half, k0, k1 = fill[b]
                        if k0 == 0:
                            if half == 0:
                                pe.wait_ge(panel_split, g * 2 + (2 + PAN_ATT + pl + 2))
                            pe.wait_ge(swapped, g * 4 + (4 + 2 * (pl + 1) + half))
                        q_part(pl + 1, half, 6, k0, k1)
                mix(g, pl, NB - 1)

            pe.wait_ge(panel_split, 2 + PAN_ATT + 1)
            q_part(0, 0, 6, 0, KD)
            q_part(0, 1, 7, 0, KD)
            pe.wait_ge(key_in, 64)
            scores(0, 0, 0, 0)
            scores(0, 0, 0, 1)
            pe.wait_ge(swapped, 6)
            with pe.Fori(0, NKV - 1) as g:
                for pl in range(2):
                    pair(g, pl, False)
            for pl in range(2):
                pair(NKV - 1, pl, pl == 1)

            with pe.Fori(0, KD) as d:
                pe.wait_ge(panel_split, d * 2 + (2 + PAN_MRG + 1))
                for b in range(2):
                    pe.wait_ge(sgf, d * 2 + (b + 1))
                    project(b, 0, Hh, Hl, b * NT, NT)
                pe.wait_ge(panel_split, d * 2 + (2 + PAN_MRG + 2))
                pe.wait_ge(fou_in, 32)
                for b in range(2):
                    pe.wait_ge(yf, d * 2 + (b + 1))
                    project(2 + b, 1, fouH, fouL, b * NT, NT, NG)
            pe.wait_ge(o_out, 1 + 2 * NB * NKV)
            with pe.Fori(0, KD // 2) as i:
                for n in range(2):
                    pe.wait_ge(panel_split, i * 2 + (2 + PAN_MRG + 2 * KD + n + 1))
                    for b in range(2):
                        pe.wait_ge(sga, i * 4 + (2 * n + b + 1))
                        project(4 + 2 * n + b, n, Hh, Hl, b * NT, NT)
            pe.wait_ge(yf, 2 + 2 * KD)
            with pe.Fori(0, KD // 2) as i:
                for n in range(2):
                    pe.wait_ge(panel_split, i * 2 + (2 + PAN_MRG + 3 * KD + n + 1))
                    for b in range(2):
                        pe.wait_ge(ya, i * 4 + (2 * n + b + 1))
                        project(2 * n + b, n, attH, attL, b * NT, NT,
                                waits={0: (att_in, 16 * 12), 6: (att_in_late, 16 * 4)})

            pe.wait_ge(sga, 4 + 2 * KD)
            with pe.Fori(0, KD // 2) as i:
                for n in range(2):
                    pe.wait_ge(panel_split, i * 2 + (2 + PAN_OUT + n + 1))
                    for b in range(2):
                        pe.wait_ge(x_res, i * 4 + (2 * n + b + 1))
                        project(4 + 2 * n + b, n, mergedH, mergedL, b * NT, NT,
                                waits={0: (y_lo, KD - 2), 6: (y_lo, KD - 1), 7: (y_lo, KD)})
            pe.wait_ge(x_res, 4 + 2 * KD)
            norm_mm(N3, LAT)
            pe.wait_ge(N3["rms"], 2)
            ffn_mm(F2, LAT, PAN_FFN2, N3)
            pe.wait_ge(F2["acc"], 4 + 16 * NPAIR)
            norm_mm(N4, LAT)
            pe.wait_ge(N4["rms"], 2)
            for t in range(NB):
                pe.wait_ge(N4["t"], KD * (t // 4 + 1))
                for half in range(2):
                    if t >= 2:
                        pe.wait_ge(o_odd if half else o_even, t - 1)
                    for k in range(4):
                        kk = half * 4 + k
                        mm = pe.transpose(ps[:, 2 * (t % 2) + half, k * P:(k + 1) * P], oT[:, kk, t * P:(t + 1) * P], ident[:, :])
                    mm.then_inc(o_turned, 1)

        @block.scalar
        def _(act):
            act.wait_ge(cols_set, 1)
            for s, r in ((0, ROW_C), (1, ROW_CCTX)):
                act.activation(cond[:, :, s], cols[:, r:r + KD], ACT.Silu).then_inc(cond_set, 1)
            for t in range(NKT):
                act.wait_ge(x_turned, 2 * t + 1)
                dst = x_lat[:, 0:4, t * P:(t + 1) * P] if t < NB else x_ctx[:, 0:4, (t - NB) * P:(t - NB + 1) * P]
                act.activation(dst, ps[:, 2 * (t % 2), :].rearrange("p (k n) -> p k n", k=4), ACT.Copy).then_inc(x_even, 1)

            act.wait_ge(cond_set, 2)
            act.activation(condS[:, :, 0:2], cond[:, :, :], ACT.Copy).then_inc(cond_set, 1)

            def split_hi(s, nth, used):
                act.wait_ge(panel_in[s], nth)
                act.wait_ge(psum_filled, used)
                act.activation(whi[s][:, :], raw[s][:, :], ACT.Copy).then_inc(panel_hi, 1)

            def norm_act_sum(S, blocks):
                for b, (x, _, _, t0, n, _, _) in enumerate(blocks):
                    for k in range(KD):
                        if b * KD + k >= 2:
                            act.wait_ge(S["ss"], b * KD + k - 1)
                        act.activation(sq[k % 2][:, 0:n], x[:, k, t0:t0 + n], ACT.Square).then_inc(S["sq"], 1)
                    act.wait_ge(S["ss"], KD * (b + 1))
                    if b >= 2:
                        act.wait_ge(S["rstd"], b - 1)
                    act.activation(rms[b % 2][:, 0:n], ps[:, 6 + b % 2, 0:n], ACT.Sqrt, bias=epsT[:, 0:1], scale=1.0 / D).then_inc(S["rms"], 1)

            def norm_act(S, blocks, j):
                for b, (_, hi, _, t0, n, c, _) in enumerate(blocks):
                    for k in range(KD):
                        act.wait_ge(S["t"], b * KD + k + 1)
                        act.activation(hi[:, k, t0:t0 + n], tn[k % 2][:, 0:n], ACT.Identity,
                                       bias=modT[:, 3 * j, k, c:c + 1]).then_inc(S["hi"], 1)

            def ffn_act(S, blocks, p0, f0, last=False):
                nb = len(blocks)

                def body(i, final=False):
                    filled = [0, nb, 2 * nb, 3 * nb, 4 * nb, 8 * nb]
                    for s in range(6):
                        if not (final and s == 5):
                            split_hi((s + 1) % 2, i * 48 + 16 * ((p0 + s + 1) // 2 + 1), i * (12 * nb) + (f0 + filled[s]))
                        fl = s // 2
                        for b, (_, _, _, _, n, _, g0) in enumerate(blocks):
                            if s in (0, 2):
                                act.wait_ge(psum_filled, i * (12 * nb) + (f0 + filled[s] + b + 1))
                                act.wait_ge(S["glo"], i * (2 * nb) + (fl * nb + b + 1))
                                act.activation(act_t[:, g0:g0 + n], ps[:, b, 0:n], ACT.Silu).then_inc(S["silu"], 1)
                            if s in (1, 3):
                                act.wait_ge(S["prod"], i * (2 * nb) + (nb + fl * nb + b + 1))
                                act.activation(gH[:, fl, g0:g0 + n], act_t[:, g0:g0 + n], ACT.Copy).then_inc(S["ghi"], 1)
                with act.Fori(0, NPAIR - last) as i:
                    body(i)
                if last:
                    body(NPAIR - 1, True)

            act.wait_ge(x_odd, NKT)
            act.wait_ge(x_even, NKT)
            norm_act_sum(N1, ALL)

            def ada_split(m, k):
                act.wait_ge(ada_in[k], m * 16 + 16)
                if not isinstance(m, int) or k >= 4:
                    act.wait_ge(ada_used, m * KD + (k - 3))
                act.activation(adaH[k % 4][:, :], ada[k][:, :], ACT.Copy).then_inc(ada_hi, 1)

            def row_copy(m):
                act.wait_ge(ada_used, m * KD)
                act.wait_ge(mod_turned, m)
                act.activation(mod_row[:, 0:NT], ps[0:4, 4, :], ACT.Copy).then_inc(row_out, 1)
            for k in range(KD):
                ada_split(0, k)
            with act.Fori(1, NMOD) as m:
                for k in range(KD):
                    ada_split(m, k)
                    if k == 3:
                        row_copy(m)
            act.wait_ge(ada_used, NMOD * KD - 3)
            split_hi(0, 16, 1)
            row_copy(NMOD)
            act.wait_ge(gain_set, 1)
            norm_act(N1, ALL, 0)
            ffn_act(F1, ALL, PAN_FFN1, FIL_FFN1)
            act.wait_ge(F1["acc"], 4 + 24 * NPAIR)
            norm_act_sum(N2, ALL)
            norm_act(N2, ALL, 1)

            act.wait_ge(x_saved, 16)
            act.wait_ge(N2["lo"], 3 * KD)

            def fou_split(p, used):
                split_hi(p % 2, 16 * ((PAN_FOU + p) // 2 + 1), FIL_FOU + used)

            def u_out(g):
                for b in range(2):
                    act.wait_ge(psum_filled, FIL_FOU + (2 + NB) * max(g - 1, 0) + 2 * (g > 0) + b + 1)
                    act.activation(uH[g % 2][:, b * NT:(b + 1) * NT], ps[:, 2 * (g % 2) + b, :], ACT.Copy).then_inc(u_hi, 1)

            def xc_out(g):
                for n in range(NB):
                    act.wait_ge(psum_filled, FIL_FOU + 4 + (2 + NB) * g - 2 * (g == NG - 1) + n + 1)
                    act.activation(xcH[:, g, n, :], ps[:, 4 + n % 4, 0:2 * P], ACT.Copy).then_inc(xc_hi, 1)
            fou_split(1, 0)
            u_out(0)
            act.wait_ge(chan_in, 16)
            act.activation(chanH[:, :], chan_f[:, :], ACT.Copy).then_inc(chan_hi, 1)
            fou_split(2, 2)
            u_out(1)
            xc_out(0)
            fou_split(3, 4)
            u_out(2)
            xc_out(1)
            fou_split(4, 4 + NB + 2)
            u_out(3)
            xc_out(2)
            fou_split(5, 4 + 2 * NB + 4)
            xc_out(3)
            for n in range(NB - 1):
                fou_split(NG + n + 2, (2 + NB) * NG + n + 1)
            for g in range(NG):
                act.wait_ge(psum_filled, FIL_FOU + (2 + NB) * NG + NB - 1 + g + 1)
                if g > 0:
                    act.wait_ge(f_sum, g)
                act.activation(fB[:, :], ps[:, 2 * g + 1, :], ACT.Copy).then_inc(fb_out, 1)
                act.wait_ge(f_sum, g + 1)
                if g > 0:
                    act.wait_ge(f_saved, 32 * g)
                act.activation(fH[:, :], fT[:, :], ACT.Copy).then_inc(f_hi, 1)

            for n in range(4):
                split_hi((n + 1) % 2, 16 * ((PAN_KV + n + 1) // 2 + 1), FIL_KV + 3 * n)
                for b, (_, _, _, _, m, _, g0) in enumerate(ALL):
                    z = 3 * n + b
                    if n < 2:
                        act.wait_ge(rot_set, z + 1)
                        if z >= 2:
                            act.wait_ge(k_saved[z % 2], 32 * (z // 2))
                        act.activation(kH[z % 2][:, 0:m], rot[z % 2][:, 0:m], ACT.Copy).then_inc(k_hi, 1)
                    else:
                        act.wait_ge(psum_filled, FIL_KV + z + 1)
                        act.activation(vT[n - 2][:, g0 // P:(g0 + m) // P, :], ps[:, 3 * (n % 2) + b, 0:m].rearrange("p (t n) -> p t n", n=P),
                                       ACT.Copy).then_inc(v_out, 1)
            for e in range(6):
                vc, g0 = e // 3, 4 * (e % 3)
                w = min(4, NKT - g0)
                act.wait_ge(psum_filled, FIL_KV + 12 + e + 1)
                act.activation(vS[vc][:, :, g0:g0 + w, 0, :], ps[:, 6 + e % 2, 0:w * P].rearrange("p (t v e) -> p v t e", v=2, e=HEAD),
                               ACT.Copy).then_inc(v_hi, 1)

            act.wait_ge(k_saved[1], 32 * 3)
            act.wait_ge(k_saved[0], 32 * 3)
            act.wait_ge(v_saved, 32)

            def queries(g, pj, b):
                act.wait_ge(rot_set, g * 4 + (6 + 2 * pj + b + 1))
                for h in range(2):
                    r = slice(HEAD * h, HEAD * (h + 1))
                    act.activation(qS[pj % 2][h][r, b * NT:(b + 1) * NT], rot[b][r, :], ACT.Copy, scale=HEAD ** -0.5).then_inc(q_hi, 1)

            def expo(g, pj, b, h):
                act.wait_ge(max_set, g * (4 * NB) + ((pj * NB + b) * 2 + h + 1))
                n = len(KEYS[b]) * P + 2
                act.activation(pr[b % 2][h][:, 0:n], ps[:, 2 * h:2 * h + 2, :].rearrange("p a n -> p (a n)")[:, 0:n], ACT.Exp,
                               bias=nmax[:, 2 * (b % 2) + h:2 * (b % 2) + h + 1],
                               accum_out=lsum[:, 2 * (b % 2) + h:2 * (b % 2) + h + 1]).then_inc(exp_set, 1)

            def turned_hi(g, pl, b, e):
                if e >= GROUPS[b]:
                    return
                w = min(NT, 2 * len(KEYS[b]) * P - NT * e)
                act.wait_ge(pt_turned, g * (2 * NGROUP) + (pl * NGROUP + GROUP0[b] + e + 1))
                act.activation(ptH[b % 2][:, NT * e:NT * e + w], ps[:, 4 + (GROUP0[b] + e) % 2, 0:w], ACT.Copy).then_inc(pt_hi, 1)

            def low_out(g, pl, b):
                act.wait_ge(pv_done, g * (2 * NB) + (1 + pl * NB + b + 1))
                act.activation(oLow[b % 2][:, :, :], ps[HEAD:P, 7, 0:2 * P].rearrange("p (h n) -> p h n", h=2), ACT.Copy).then_inc(o_low, 1)

            def out_hi(g, pl, half):
                act.wait_ge(o_out, g * (2 * NB) + (1 + pl * NB + 4 * half + 4))
                act.wait_ge(a_saved, g * 64 + (32 * pl + 16))
                w = slice(half * NT, (half + 1) * NT)
                act.activation(aH[:, w], aT[:, w], ACT.Copy).then_inc(a_hi, 1)

            def pair(g, pl, last):
                for b in range(NB):
                    nxt = (pl, b + 1) if b + 1 < NB else (pl + 1, 0)
                    more = not (last and b == NB - 1)
                    turned_hi(g, pl, b, 0)
                    if more:
                        expo(g, *nxt, 0)
                    turned_hi(g, pl, b, 1)
                    if more:
                        expo(g, *nxt, 1)
                    turned_hi(g, pl, b, 2)
                    if b >= 1:
                        low_out(g, pl, b - 1)
                    if b == 0:
                        queries(g, pl, 1)
                    if b == 4 and not last:
                        queries(g, pl + 1, 0)
                    if b == 5 and not last:
                        split_hi(pl, g * 16 + 16 * ((PAN_ATT + pl + 2) // 2 + 1), g * 4 + (FIL_ATT + 2 * pl + 2))
                    if b == 6:
                        out_hi(g, pl, 0)
                low_out(g, pl, NB - 1)
                out_hi(g, pl, 1)

            split_hi(1, 16 * ((PAN_ATT + 1) // 2 + 1), FIL_ATT)
            queries(0, 0, 0)
            expo(0, 0, 0, 0)
            expo(0, 0, 0, 1)
            with act.Fori(0, NKV - 1) as g:
                for pl in range(2):
                    pair(g, pl, False)
            for pl in range(2):
                pair(NKV - 1, pl, pl == 1)

            def one(t, d, b):
                return t[:, bass.ds(d, 1), b * NT:(b + 1) * NT].rearrange("p a n -> p (a n)")

            with act.Fori(0, KD) as d:
                split_hi(1, d * 16 + 16 * ((PAN_MRG + 1) // 2 + 1), d * 4 + FIL_MRG)
                for b in range(2):
                    act.wait_ge(psum_filled, d * 4 + (FIL_MRG + b + 1))
                    act.activation(one(y, d, b), ps[:, b, :], ACT.Sigmoid).then_inc(sgf, 1)
                split_hi(0, d * 16 + 16 * ((PAN_MRG + 2) // 2 + 1), d * 4 + (FIL_MRG + 2))
            act.wait_ge(a_saved, 16 + 32 * KD)
            with act.Fori(0, KD // 2) as i:
                for n in range(2):
                    split_hi((n + 1) % 2, i * 16 + 16 * ((PAN_MRG + 2 * KD + n + 1) // 2 + 1), i * 4 + (FIL_MRG + 4 * KD + 2 * n))
                    for b in range(2):
                        act.wait_ge(psum_filled, i * 4 + (FIL_MRG + 4 * KD + 2 * n + b + 1))
                        act.activation(one(gate_a, i * 2 + n, b), ps[:, 4 + 2 * n + b, :], ACT.Sigmoid).then_inc(sga, 1)

            def merged_hi(i, n):
                act.wait_ge(ysum, i * 2 + (n + 1))
                if isinstance(i, int):
                    dst, yd = mergedH[2 * i + n], y[:, 2 * i + n, :]
                else:
                    dst, yd = (t[:, bass.ds(i * 2 + n, 1), :].rearrange("p a n -> p (a n)") for t in (Yh, y))
                act.activation(dst, yd, ACT.Copy).then_inc(y_hi, 1)

            def att_split(i, n):
                split_hi((n + 1) % 2, i * 16 + 16 * ((PAN_MRG + 3 * KD + n + 1) // 2 + 1), i * 4 + (FIL_MRG + 6 * KD + 2 * n))
            with act.Fori(0, KD // 2 - 1) as i:
                for n in range(2):
                    att_split(i, n)
                    merged_hi(i, n)
            for n in range(2):
                att_split(KD // 2 - 1, n)
                merged_hi(KD // 2 - 1, n)

            with act.Fori(0, KD // 2) as i:
                for n in range(2):
                    split_hi((n + 1) % 2, i * 16 + 16 * ((PAN_OUT + n + 1) // 2 + 1), i * 4 + (FIL_OUT + 2 * n))
            act.wait_ge(x_res, 4 + 2 * KD)
            norm_act_sum(N3, LAT)
            norm_act(N3, LAT, 2)
            ffn_act(F2, LAT, PAN_FFN2, FIL_FFN2, last=True)
            act.wait_ge(F2["acc"], 4 + 16 * NPAIR)
            norm_act_sum(N4, LAT)
            for t in range(NB):
                act.wait_ge(o_turned, 2 * t + 1)
                if t >= 2:
                    act.wait_ge(stored[t % 2], 16 * (t // 2))
                act.activation(orow[t % 2][:, 0:NT], ps[:, 2 * (t % 2), :], ACT.Copy).then_inc(o_even, 1)

        @block.vector
        def _(dve):
            dve.memset(ones[:, :], 1.0).then_inc(ones_set, 1)
            dve.memset(epsT[:, :], EPS)
            dve.wait_ge(psum_filled, 1)
            dve.tensor_copy(cols[:, :], ps[:, 6, 0:NROW]).then_inc(cols_set, 1)
            for t in range(NKT):
                dve.wait_ge(x_turned, 2 * t + 2)
                dst = x_lat[:, 4:8, t * P:(t + 1) * P] if t < NB else x_ctx[:, 4:8, (t - NB) * P:(t - NB + 1) * P]
                dve.tensor_copy(dst, ps[:, 2 * (t % 2) + 1, :].rearrange("p (k n) -> p k n", k=4)).then_inc(x_odd, 1)
            def split_lo(s, n):
                dve.wait_ge(panel_hi, n)
                dve.tensor_tensor(wlo[s][:, :], raw[s][:, :], whi[s][:, :].bitcast(F32), ALU.subtract).then_inc(panel_split, 1)

            def norm_dve_rstd(S, blocks):
                for b, (_, _, _, _, n, _, _) in enumerate(blocks):
                    dve.wait_ge(S["rms"], b + 1)
                    dve.reciprocal(rstd[b][:, 0:n], rms[b % 2][:, 0:n]).then_inc(S["rstd"], 1)

            def norm_dve(S, blocks, j, last=False):
                for b, (x, hi, lo, t0, n, c, _) in enumerate(blocks):
                    dve.wait_ge(S["rstd"], b + 1)

                    def low(k):
                        dve.wait_ge(S["hi"], b * KD + k + 1)
                        dve.scalar_tensor_tensor(lo[:, k, t0:t0 + n], tn[k % 2][:, 0:n], modT[:, 3 * j, k, c:c + 1],
                                                 hi[:, k, t0:t0 + n].bitcast(F32), ALU.add, ALU.subtract).then_inc(S["lo"], 1)
                    for k in range(KD):
                        gain = cols[:, ROW_GF + k:ROW_GF + k + 1] if last else gainT[:, j, k, c:c + 1]
                        dst = oT[:, k, t0:t0 + n] if last else tn[k % 2][:, 0:n]
                        if not last and b * KD + k >= 2:
                            dve.wait_ge(S["lo"], b * KD + k - 1)
                        dve.scalar_tensor_tensor(dst, x[:, k, t0:t0 + n], gain, rstd[b][:, 0:n], ALU.mult, ALU.mult).then_inc(S["t"], 1)
                        if k >= 1 and not last:
                            low(k - 1)
                    if not last:
                        low(KD - 1)

            def ffn_dve(S, blocks, p0, f0, j, last=False):
                nb = len(blocks)

                def body(i, final=False):
                    filled = [0, nb, 2 * nb, 3 * nb, 4 * nb, 8 * nb]
                    for s in range(6):
                        if not (final and s == 5):
                            split_lo((s + 1) % 2, i * 6 + (p0 + s + 2))
                        fl = s // 2
                        if s in (1, 3):
                            for b, (_, _, _, _, n, _, g0) in enumerate(blocks):
                                dve.wait_ge(psum_filled, i * (12 * nb) + (f0 + filled[s] + b + 1))
                                dve.wait_ge(S["silu"], i * (2 * nb) + (nb + fl * nb + b + 1))
                                dve.tensor_tensor(act_t[:, g0:g0 + n], ps[:, 3 + b, 0:n], act_t[:, g0:g0 + n], ALU.mult).then_inc(S["prod"], 1)
                            for b, (_, _, _, _, n, _, g0) in enumerate(blocks):
                                dve.wait_ge(S["ghi"], i * (2 * nb) + (fl * nb + b + 1))
                                dve.tensor_tensor(gL[:, fl, g0:g0 + n], act_t[:, g0:g0 + n], gH[:, fl, g0:g0 + n].bitcast(F32),
                                                  ALU.subtract).then_inc(S["glo"], 1)
                        if s >= 4:
                            for b, (x, _, _, t0, n, c, _) in enumerate(blocks):
                                for d in range(4):
                                    k = (s - 4) * 4 + d
                                    dve.wait_ge(psum_filled, i * (12 * nb) + (f0 + filled[s] + 4 * b + d + 1))
                                    dve.scalar_tensor_tensor(x[:, k, t0:t0 + n], ps[:, 4 + d, 0:n], gateT[:, j, k, c:c + 1],
                                                             x[:, k, t0:t0 + n], ALU.mult, ALU.add).then_inc(S["acc"], 1)
                with dve.Fori(0, NPAIR - last) as i:
                    body(i)
                if last:
                    body(NPAIR - 1, True)

            dve.wait_ge(cond_set, 3)
            dve.tensor_tensor(condS[:, :, 2:4], cond[:, :, :], condS[:, :, 0:2].bitcast(F32), ALU.subtract)
            dve.wait_ge(ident_in, 16)
            dve.tensor_tensor(pick[:, :], ident[0:4, 0:2], ident[0:4, 2:4], ALU.add).then_inc(cond_set, 1)
            norm_dve_rstd(N1, ALL)

            def ada_split(m, k):
                dve.wait_ge(ada_hi, m * KD + (k + 1))
                dve.tensor_tensor(adaL[k % 4][:, :], ada[k][:, :], adaH[k % 4][:, :].bitcast(F32), ALU.subtract).then_inc(ada_lo, 1)

            def row_copy(m):
                dve.wait_ge(ada_used, m * KD)
                dve.wait_ge(mod_turned, m)
                dve.tensor_copy(mod_row[:, NT:D], ps[0:4, 5, :]).then_inc(row_out, 1)

            def mod_add(m):
                dve.wait_ge(mod_turned, m + 1)
                dve.tensor_tensor(modT[:, bass.ds(m - 1, 1), :, :], ps[:, 7, 0:2 * KD].rearrange("p (a d s) -> p a d s", a=1, s=2),
                                  cols[:, bass.ds((m - 1) * KD, KD)].unsqueeze(1).unsqueeze(3).to_broadcast([P, 1, KD, 2]), ALU.add).then_inc(mod_set, 1)
            for k in range(KD):
                ada_split(0, k)
            with dve.Fori(1, NMOD) as m:
                for k in range(KD):
                    ada_split(m, k)
                    if k == 3:
                        row_copy(m)
                    if k == 6:
                        mod_add(m)
            split_lo(0, 1)
            row_copy(NMOD)
            mod_add(NMOD)
            dve.wait_ge(mod_set, NMOD + 1)
            for j, r in enumerate((ROW_G1, ROW_GM, ROW_G2)):
                for s in range(2):
                    dve.scalar_tensor_tensor(gainT[:, j, :, s], modT[:, 3 * j + 1, :, s], 1.0, cols[:, r:r + KD], ALU.add, ALU.mult)
                last = dve.tensor_scalar(gateT[:, j, :, :], modT[:, 3 * j + 2, :, :], 1.0 if j == 1 else 0.5, None, ALU.mult)
            last.then_inc(gain_set, 1)

            dve.wait_ge(gain_set, 1)
            dve.wait_ge(x_even, NKT)
            norm_dve(N1, ALL, 0)
            dve.wait_ge(const_in, 2 * 16)
            dve.wait_ge(a_saved, 16)
            dve.tensor_copy(identR[:, :], ident[:, :])
            dve.tensor_copy(maskR[:, :, :], mask_f[:, :, :])
            dve.tensor_copy(altR[:, :], alt_f[:, :]).then_inc(consts_set, 1)
            dve.memset(sink_f[:, :, 1:2], NEG)
            dve.tensor_copy(sink_f[:, :, 0], sink_r[:, :]).then_inc(cols_set, 1)
            dve.wait_ge(cols_set, 2)
            dve.tensor_copy(sinkH[:, :, :], sink_f[:, :, :]).then_inc(cols_set, 1)
            dve.wait_ge(cols_set, 3)
            dve.tensor_tensor(sinkL[:, :, :], sink_f[:, :, :], sinkH[:, :, :].bitcast(F32), ALU.subtract).then_inc(cols_set, 1)

            ffn_dve(F1, ALL, PAN_FFN1, FIL_FFN1, 0)
            dve.wait_ge(F1["acc"], 4 + 24 * NPAIR)
            norm_dve_rstd(N2, ALL)
            norm_dve(N2, ALL, 1)

            dve.wait_ge(x_saved, 16)

            def u_low(g):
                for b in range(2):
                    dve.wait_ge(u_hi, g * 2 + b + 1)
                    w = slice(b * NT, (b + 1) * NT)
                    dve.tensor_tensor(uL[g % 2][:, w], ps[:, 2 * (g % 2) + b, :], uH[g % 2][:, w].bitcast(F32), ALU.subtract).then_inc(u_lo, 1)

            def xc_low(g):
                for n in range(NB):
                    dve.wait_ge(xc_hi, g * NB + n + 1)
                    dve.tensor_tensor(xcL[:, g, n, :], ps[:, 4 + n % 4, 0:2 * P], xcH[:, g, n, :].bitcast(F32), ALU.subtract).then_inc(xc_lo, 1)

            def fou_split(p):
                split_lo(p % 2, PAN_FOU + p + 1)
            fou_split(1)
            u_low(0)
            dve.wait_ge(chan_hi, 1)
            dve.tensor_tensor(chanL[:, :], chan_f[:, :], chanH[:, :].bitcast(F32), ALU.subtract).then_inc(chan_lo, 1)
            fou_split(2)
            u_low(1)
            xc_low(0)
            fou_split(3)
            u_low(2)
            xc_low(1)
            fou_split(4)
            u_low(3)
            xc_low(2)
            fou_split(5)
            xc_low(3)
            for n in range(NB - 1):
                fou_split(NG + n + 2)
            for g in range(NG):
                dve.wait_ge(fb_out, g + 1)
                if g > 0:
                    dve.wait_ge(f_lo, g)
                dve.tensor_tensor(fT[:, 1:NT], ps[:, 2 * g, 1:NT], fB[:, 1:NT], ALU.subtract)
                dve.tensor_tensor(fT[:, SEQ - 1:NT:-1], ps[:, 2 * g, 1:NT], fB[:, 1:NT], ALU.add)
                dve.tensor_copy(fT[:, NT:NT + 1], fB[:, 0:1])
                dve.tensor_copy(fT[:, 0:1], ps[:, 2 * g, 0:1]).then_inc(f_sum, 1)
                dve.wait_ge(f_hi, g + 1)
                dve.tensor_tensor(fL[:, :], fT[:, :], fH[:, :].bitcast(F32), ALU.subtract).then_inc(f_lo, 1)

            def rotate(s, z, t0, n, lat):
                if lat:
                    by_cos = dve.tensor_tensor(rot[z % 2][:, 0:n], ps[:, s, 0:n], cosT[:, t0:t0 + n], ALU.mult).then_inc(cos_mul, 1)
                    dve.stream_shuffle(swp[z % 2][:, 0:n], ps[:, s, 0:n], [i ^ 1 for i in range(32)]).then_inc(swapped, 1)
                    return by_cos
                return dve.tensor_copy(rot[z % 2][:, 0:n], ps[:, s, 0:n])

            dve.wait_ge(rope_in, 32)
            for n in range(4):
                split_lo((n + 1) % 2, PAN_KV + n + 2)
                if n >= 2:
                    continue
                for b, (_, _, _, t0, m, _, _) in enumerate(ALL):
                    z = 3 * n + b
                    dve.wait_ge(psum_filled, FIL_KV + z + 1)
                    if z >= 2:
                        dve.wait_ge(k_lo, z - 1)
                    if b < 2:
                        rotate(3 * n + b, z, t0, m, True)
                        dve.wait_ge(cos_mul, 2 * n + b + 1)
                        dve.wait_ge(sin_mul, 2 * n + b + 1)
                        dve.tensor_tensor(rot[z % 2][:, 0:m], rot[z % 2][:, 0:m], swp[z % 2][:, 0:m], ALU.add).then_inc(rot_set, 1)
                    else:
                        rotate(3 * n + b, z, t0, m, False).then_inc(rot_set, 1)
                    dve.wait_ge(k_hi, z + 1)
                    dve.tensor_tensor(kL[z % 2][:, 0:m], rot[z % 2][:, 0:m], kH[z % 2][:, 0:m].bitcast(F32), ALU.subtract).then_inc(k_lo, 1)
            for e in range(6):
                vc, g0 = e // 3, 4 * (e % 3)
                w = min(4, NKT - g0)
                dve.wait_ge(v_hi, e + 1)
                dve.tensor_tensor(vS[vc][:, :, g0:g0 + w, 1, :], ps[:, 6 + e % 2, 0:w * P].rearrange("p (t v e) -> p v t e", v=2, e=HEAD),
                                  vS[vc][:, :, g0:g0 + w, 0, :].bitcast(F32), ALU.subtract).then_inc(v_lo, 1)

            dve.wait_ge(k_saved[1], 32 * 3)
            dve.wait_ge(k_saved[0], 32 * 3)
            dve.wait_ge(v_saved, 32)

            def q_rotate(g, pj, b, bank):
                dve.wait_ge(psum_filled, g * 4 + (FIL_ATT + 2 * pj + b + 1))
                rotate(bank, b, b * NT, NT, True)

            def q_add(g, pj, b):
                dve.wait_ge(cos_mul, g * 4 + (4 + 2 * pj + b + 1))
                dve.wait_ge(sin_mul, g * 4 + (4 + 2 * pj + b + 1))
                dve.tensor_tensor(rot[b][:, :], rot[b][:, :], swp[b][:, :], ALU.add).then_inc(rot_set, 1)

            def q_low(g, pj, b):
                for h in range(2):
                    r, o_ = slice(HEAD * h, HEAD * (h + 1)), slice(HEAD * (1 - h), HEAD * (2 - h))
                    w = slice(b * NT, (b + 1) * NT)
                    dve.wait_ge(q_hi, g * 8 + (4 * pj + 2 * b + h + 1))
                    dve.scalar_tensor_tensor(qS[pj % 2][h][o_, w], rot[b][r, :], HEAD ** -0.5, qS[pj % 2][h][r, w].bitcast(F32),
                                             ALU.mult, ALU.subtract).then_inc(q_lo, 1)

            def maxi(g, pj, b, h):
                dve.wait_ge(qk_done, g * (4 * NB) + ((pj * NB + b) * 2 + h + 1))
                n = len(KEYS[b]) * P + 2
                dve.tensor_reduce(nmax[:, 2 * (b % 2) + h:2 * (b % 2) + h + 1],
                                  ps[:, 2 * h:2 * h + 2, :].rearrange("p a n -> p (a n)")[:, 0:n], AX.X, ALU.max,
                                  negate=True).then_inc(max_set, 1)

            def recip(g, pj, b, h):
                dve.wait_ge(exp_set, g * (4 * NB) + (2 + (pj * NB + b) * 2 + h + 1))
                z = slice(2 * (b % 2) + h, 2 * (b % 2) + h + 1)
                dve.reciprocal(rsum[:, z], lsum[:, z]).then_inc(rsum_set, 1)

            def turned_lo(g, pl, b, e):
                if e >= GROUPS[b]:
                    return
                w = min(NT, 2 * len(KEYS[b]) * P - NT * e)
                dve.wait_ge(pt_hi, g * (2 * NGROUP) + (pl * NGROUP + GROUP0[b] + e + 1))
                dve.tensor_tensor(ptL[b % 2][:, NT * e:NT * e + w], ps[:, 4 + (GROUP0[b] + e) % 2, 0:w],
                                  ptH[b % 2][:, NT * e:NT * e + w].bitcast(F32), ALU.subtract).then_inc(pt_lo, 1)

            def out(g, pl, b):
                dve.wait_ge(o_low, g * (2 * NB) + (pl * NB + b + 1))
                for h in range(2):
                    last = dve.tensor_tensor(aT[HEAD * h:HEAD * (h + 1), b * P:(b + 1) * P], ps[0:HEAD, 7, h * P:(h + 1) * P],
                                             oLow[b % 2][:, h, :], ALU.add)
                last.then_inc(o_out, 1)

            def out_lo(g, pl, half):
                w = slice(half * NT, (half + 1) * NT)
                dve.wait_ge(a_hi, g * 4 + (2 * pl + half + 1))
                dve.tensor_tensor(aL[:, w], aT[:, w], aH[:, w].bitcast(F32), ALU.subtract).then_inc(a_lo, 1)

            def pair(g, pl, last):
                for b in range(NB):
                    nxt = (pl, b + 1) if b + 1 < NB else (pl + 1, 0)
                    more = not (last and b == NB - 1)
                    if b == 0:
                        q_add(g, pl, 1)
                    if b == 4 and not last:
                        q_add(g, pl + 1, 0)
                    if more:
                        maxi(g, *nxt, 0)
                    turned_lo(g, pl, b, 0)
                    if more:
                        maxi(g, *nxt, 1)
                    turned_lo(g, pl, b, 1)
                    if more:
                        recip(g, *nxt, 0)
                    turned_lo(g, pl, b, 2)
                    if more:
                        recip(g, *nxt, 1)
                    if b >= 1:
                        out(g, pl, b - 1)
                    if b == 1:
                        q_low(g, pl, 1)
                    if b == 3 and not last:
                        q_rotate(g, pl + 1, 0, 6)
                    if b == 5 and not last:
                        q_low(g, pl + 1, 0)
                    if b == 6 and not last:
                        split_lo(pl, g * 2 + (PAN_ATT + pl + 3))
                    if b == 7:
                        out_lo(g, pl, 0)
                out(g, pl, NB - 1)
                if not last:
                    q_rotate(g, pl + 1, 1, 6)
                out_lo(g, pl, 1)

            split_lo(1, PAN_ATT + 2)
            q_rotate(0, 0, 0, 6)
            q_add(0, 0, 0)
            q_low(0, 0, 0)
            q_rotate(0, 0, 1, 7)
            maxi(0, 0, 0, 0)
            maxi(0, 0, 0, 1)
            recip(0, 0, 0, 0)
            recip(0, 0, 0, 1)
            with dve.Fori(0, NKV - 1) as g:
                for pl in range(2):
                    pair(g, pl, False)
            for pl in range(2):
                pair(NKV - 1, pl, pl == 1)

            def one(t, d, b):
                return t[:, bass.ds(d, 1), b * NT:(b + 1) * NT].rearrange("p a n -> p (a n)")

            with dve.Fori(0, KD) as d:
                split_lo(1, d * 2 + (PAN_MRG + 2))
                split_lo(0, d * 2 + (PAN_MRG + 3))
                for b in range(2):
                    dve.wait_ge(psum_filled, d * 4 + (FIL_MRG + 2 + b + 1))
                    dve.wait_ge(sgf, d * 2 + (2 + b + 1))
                    dve.tensor_tensor(one(y, d, b), ps[:, 2 + b, :], one(y, d, b), ALU.mult).then_inc(yf, 1)
            with dve.Fori(0, KD // 2) as i:
                for n in range(2):
                    split_lo((n + 1) % 2, i * 2 + (PAN_MRG + 2 * KD + n + 2))

            dve.wait_ge(yf, 2 + 2 * KD)

            def merged(i, n):
                for b in range(2):
                    dve.wait_ge(psum_filled, i * 4 + (FIL_MRG + 6 * KD + 2 * n + b + 1))
                    dve.wait_ge(sga, i * 4 + (4 + 2 * n + b + 1))
                    ga = one(gate_a, i * 2 + n, b)
                    dve.tensor_tensor(ga, ps[:, 2 * n + b, :], ga, ALU.mult).then_inc(ya, 1)
                dve.wait_ge(ya, i * 4 + (4 + 2 * n + 2))
                yd, ga = (t[:, bass.ds(i * 2 + n, 1), :].rearrange("p a n -> p (a n)") for t in (y, gate_a))
                dve.tensor_tensor(yd, yd, ga, ALU.add).then_inc(ysum, 1)
                dve.wait_ge(y_hi, i * 2 + (n + 1))
                if isinstance(i, int):
                    hi, lo = mergedH[2 * i + n], mergedL[2 * i + n]
                else:
                    hi, lo = (t[:, bass.ds(i * 2 + n, 1), :].rearrange("p a n -> p (a n)") for t in (Yh, Yl))
                dve.tensor_tensor(lo, yd, hi.bitcast(F32), ALU.subtract).then_inc(y_lo, 1)

            with dve.Fori(0, KD // 2 - 1) as i:
                for n in range(2):
                    split_lo((n + 1) % 2, i * 2 + (PAN_MRG + 3 * KD + n + 2))
                    merged(i, n)
            for n in range(2):
                split_lo((n + 1) % 2, PAN_MRG + 4 * KD - 2 + n + 2)
                merged(KD // 2 - 1, n)

            with dve.Fori(0, KD // 2) as i:
                for n in range(2):
                    split_lo((n + 1) % 2, i * 2 + (PAN_OUT + n + 2))
                    for b in range(2):
                        dve.wait_ge(psum_filled, i * 4 + (FIL_OUT + 2 * n + b + 1))
                        dve.wait_ge(x_back, 16 * KD)
                        xd = x_lat[:, bass.ds(i * 2 + n, 1), b * NT:(b + 1) * NT].rearrange("p a n -> p (a n)")
                        gt = gateT[:, 1, bass.ds(i * 2 + n, 1), 0:1].rearrange("p a n -> p (a n)")
                        dve.scalar_tensor_tensor(xd, ps[:, 4 + 2 * n + b, :], gt, xd, ALU.mult, ALU.add).then_inc(x_res, 1)
            dve.wait_ge(x_res, 4 + 2 * KD)
            norm_dve_rstd(N3, LAT)
            norm_dve(N3, LAT, 2)
            ffn_dve(F2, LAT, PAN_FFN2, FIL_FFN2, 2, last=True)
            dve.wait_ge(F2["acc"], 4 + 16 * NPAIR)
            norm_dve_rstd(N4, LAT)
            norm_dve(N4, LAT, 0, last=True)
            for t in range(NB):
                dve.wait_ge(o_turned, 2 * t + 2)
                if t >= 2:
                    dve.wait_ge(stored[t % 2], 16 * (t // 2))
                dve.tensor_copy(orow[t % 2][:, NT:D], ps[:, 2 * (t % 2) + 1, :]).then_inc(o_odd, 1)

        @block.gpsimd
        def _(pool):
            for z, (s, n) in enumerate(CREDIT):
                pool.memset(dummy[:, z:z + 1], 0.0).then_inc(s, n)

            def freed(saved, free, i, col):
                pool.wait_ge(saved, i * 32 + 32)
                pool.wait_ge(free, i + 1)
                pool.tensor_tensor(dummy[:, col:col + 1], dummy[:, 0:1], dummy[:, 0:1], ALU.add).then_inc(free, 1)

            pool.wait_ge(F1["acc"], 4 + 24 * NPAIR)
            pool.dma_start(x_scr, x_lat[:, :, :]).then_inc(x_saved, 16)
            pool.dma_start(cosT[:, :], T["rope_cos"]).then_inc(rope_in, 16)
            pool.dma_start(sinT[:, :], T["rope_sin"]).then_inc(rope_in, 16)
            pool.wait_ge(N2["lo"], 3 * KD)
            pool.dma_start(chan_f[:, :], T["dft_chan"]).then_inc(chan_in, 16)
            for g in range(NG):
                pool.wait_ge(f_lo, g + 1)
                for z, part in enumerate((fH, fL)):
                    pool.dma_start(f_scr[g, z, :, :], part[:, :]).then_inc(f_saved, 16)

            def sine(z, n, t0):
                pool.tensor_tensor(swp[z % 2][:, 0:n], swp[z % 2][:, 0:n], sinT[:, t0:t0 + n], ALU.mult).then_inc(sin_mul, 1)

            pool.wait_ge(rope_in, 32)
            for n in range(2):
                for b, (_, _, _, t0, m, _, g0) in enumerate(ALL):
                    z = 3 * n + b
                    if b < 2:
                        pool.wait_ge(swapped, 2 * n + b + 1)
                        sine(z, m, t0)
                    pool.wait_ge(k_lo, z + 1)
                    for q, part in enumerate((kH, kL)):
                        pool.dma_start(k_scr[q, n * P:(n + 1) * P, g0:g0 + m], part[z % 2][:, 0:m]).then_inc(k_saved[z % 2], 16)
            for vc in range(2):
                pool.wait_ge(v_lo, 3 * vc + 3)
                pool.dma_start(v_scr[:, 2 * vc:2 * vc + 2, :].rearrange("p v n -> p (v n)"),
                               vS[vc][:, :, :, :, :].rearrange("p v t z e -> p (v t z e)")).then_inc(v_saved, 16)

            pool.wait_ge(v_saved, 32)
            for s in range(2):
                pool.wait_ge(k_saved[s], 32 * 3)

            def q_sine(g, pj, b):
                pool.wait_ge(swapped, g * 4 + (4 + 2 * pj + b + 1))
                sine(b, NT, b * NT)

            def diagonal(g, pj, b, h):
                pool.wait_ge(rsum_set, g * (4 * NB) + ((pj * NB + b) * 2 + h + 1))
                z = slice(2 * (b % 2) + h, 2 * (b % 2) + h + 1)
                pool.tensor_tensor(dg[b % 2][h][:, :], ident[:, :], rsum[:, z].to_broadcast([P, P]), ALU.mult).then_inc(prob_set, 1)

            def pair(g, pl, last):
                for b in range(NB):
                    nxt = (pl, b + 1) if b + 1 < NB else (pl + 1, 0)
                    if not (last and b == NB - 1):
                        diagonal(g, *nxt, 0)
                        diagonal(g, *nxt, 1)
                    if b == 3 and not last:
                        q_sine(g, pl + 1, 0)
                if not last:
                    q_sine(g, pl + 1, 1)

            q_sine(0, 0, 0)
            q_sine(0, 0, 1)
            diagonal(0, 0, 0, 0)
            diagonal(0, 0, 0, 1)
            with pool.Fori(0, NKV - 1) as g:
                for pl in range(2):
                    pair(g, pl, False)
            for pl in range(2):
                pair(NKV - 1, pl, pl == 1)

            pool.wait_ge(a_saved, 16 + 32 * KD)
            pool.wait_ge(pv_done, 1 + 2 * NB * NKV)

            def att_back(k, loaded):
                for z, part in enumerate((attH, attL)):
                    pool.dma_start(part[k][:, :], a_scr[k, z]).then_inc(loaded, 16)
            for k in range(2):
                att_back(k, att_in)
            pool.wait_ge(psum_filled, FIL_MRG + 4 * KD)
            for k in range(2, 6):
                att_back(k, att_in)
            pool.wait_ge(psum_filled, FIL_MRG + 6 * KD)
            for k in range(6, KD):
                att_back(k, att_in_late)
            for d in range(KD):
                pool.wait_ge(y_lo, d + 1)
                pool.dma_start(x_lat[:, d, :], x_scr[:, d, :]).then_inc(x_back, 16)


_INS = {"x": (SEQ, D), "c": (D,), "ctx": (CTX, D), "c_ctx": (D,), "w_ada": (D, NMOD * D), "b_ada": (NMOD * D,),
        "g_ffn1": (D,), "w_ffn1_in": (D, 2 * FF), "w_ffn1_out": (FF, D), "g_mix": (D,), "w_in": (D, 4 * D),
        "attn_sink": (16,), "w_attn_branch": (D, D), "w_fourier_branch": (NG * P, D), "w_out": (D, D),
        "g_ffn2": (D,), "w_ffn2_in": (D, 2 * FF), "w_ffn2_out": (FF, D), "g_final": (D,)}


def shape_tables():
    import numpy as np
    i = np.arange(P)
    masks = np.zeros((P, 2, P), np.float32)
    masks[:, 0, :] = np.where(i[None, :] >= i[:, None], 0.0, NEG)
    masks[:, 1, :] = np.where(i[None, :] <= i[:, None], 0.0, NEG)
    alt = np.zeros((P, 2), np.float32)
    alt[:, 0] = 1.0 - 2.0 * (i % 2)
    rows = np.repeat(np.arange(SEQ // 64, dtype=np.float32), 64)
    colm = np.tile(np.arange(64, dtype=np.float32), SEQ // 64)
    inv = np.power(np.float32(10000.0), -np.arange(0, 32, 2, dtype=np.float32) / np.float32(32)).astype(np.float32)
    ang = np.concatenate([rows[:, None] * inv, colm[:, None] * inv], axis=-1).astype(np.float32).astype(np.float64)
    feat = (i % HEAD) // 2
    cos = np.cos(ang).T[feat].astype(np.float32)
    sin = (np.sin(ang).T[feat] * np.where(i % 2 == 0, -1.0, 1.0)[:, None]).astype(np.float32)
    chan = np.zeros((P, 2 * P), np.float64)
    a = 2 * np.pi * ((i[:, None] * i[None, :]) % P) / P
    chan[:, 0:P], chan[:, P:2 * P] = np.cos(a), np.sin(a)
    chan /= np.sqrt(float(SEQ * P))
    n, k = np.arange(SEQ), np.arange(NT)
    a = 2 * np.pi * ((n[:, None] * k[None, :]) % SEQ) / SEQ
    pos = np.concatenate([np.cos(a), np.sin(a)], axis=1)
    return {"ident": np.eye(P, dtype=np.float32), "masks": masks, "alt": alt, "rope_cos": cos, "rope_sin": sin,
            "dft_chan": chan.astype(np.float32), "dft_pos": pos.astype(np.float32)}


def kernel(**inputs):
    import numpy as _np
    import concourse.bacc as _bacc
    from concourse import mybir as _mybir
    from concourse.bass_utils import run_bass_kernel_spmd as _run

    nc = _bacc.Bacc("TRN2", target_bir_lowering=False, num_devices=1)
    arrays, T = {}, {}
    tensors = {name: _np.ascontiguousarray(inputs[name]).reshape(shape) for name, shape in _INS.items()}
    tensors.update(shape_tables())
    for name, a in tensors.items():
        arrays[f"in_{name}_dram"] = a
        T[name] = nc.dram_tensor(f"in_{name}_dram", a.shape, _mybir.dt.from_np(a.dtype), kind="ExternalInput").ap()
    T["out"] = nc.dram_tensor("out_0_dram", (SEQ, D), _mybir.dt.float32, kind="ExternalOutput").ap()
    build(nc, T)
    r = _run(nc, [arrays], core_ids=[0])
    return r.results[0]["out_0_dram"].reshape(1, SEQ, D)
```

```python
from contextlib import ExitStack

import concourse.bass as bass
from concourse import mybir

ACT = mybir.ActivationFunctionType
ALU = mybir.AluOpType
AX = mybir.AxisListType
F32 = mybir.dt.float32
R32 = mybir.dt.float32r

P = 128
D = 1024
KD = D // P
SEQ, CTX = 1024, 256
NT = 512
FF = 2816
NPAIR = FF // (2 * P)
HEAD = 64
NKV = 4
NB = SEQ // P
NKT = (SEQ + CTX) // P
NG = 4
NMOD = 9
K_OFF, V_OFF, U_OFF, GA_OFF, GF_OFF = 1024, 1280, 1536, 2048, 3072
EPS = 1e-6
NEG = -1e30

ROW_B, ROW_C, ROW_CCTX, ROW_G1, ROW_GM, ROW_G2, ROW_GF = 0, 72, 80, 88, 96, 104, 112
NROW = 120

PAN_FFN1 = 0
PAN_FOU = PAN_FFN1 + 6 * NPAIR
PAN_KV = PAN_FOU + NG + NB
PAN_ATT = PAN_KV + 4
PAN_MRG = PAN_ATT + 2 * NKV
PAN_OUT = PAN_MRG + 4 * KD
PAN_FFN2 = PAN_OUT + KD
PAN_END = PAN_FFN2 + 6 * NPAIR

FIL_FFN1 = 1
FIL_FOU = FIL_FFN1 + 36 * NPAIR
FIL_KV = FIL_FOU + (2 + NB) * NG + NB - 1 + NG
FIL_ATT = FIL_KV + 18
FIL_MRG = FIL_ATT + 4 * NKV
FIL_OUT = FIL_MRG + 8 * KD
FIL_FFN2 = FIL_OUT + 2 * KD

KEYS = [[b - 1, b + 1, NB, NB + 1, b] if 0 < b < NB - 1 else sorted([b, 1 if b == 0 else b - 1]) + [NB, NB + 1] for b in range(NB)]
GROUPS = [-(-2 * len(k) // 4) for k in KEYS]
GROUP0 = [sum(GROUPS[:b]) for b in range(NB)]
NGROUP = sum(GROUPS)


def build(nc, T):
    with ExitStack() as ctx:
        base = 16512

        def at(name, off, shape, dt=F32):
            return nc.alloc_sbuf_tensor_at(name, shape, dt, offset=base + off)

        def sem(name):
            return ctx.enter_context(nc.semaphore(name))

        HH, HL = 0, 32768
        RING = 65536
        CON = RING + 6 * 4096
        POOL = CON + 6272
        Hh = at("Hh", HH, [P, KD, SEQ], R32)
        Hl = at("Hl", HL, [P, KD, SEQ], R32)
        raw = [at(f"raw{s}", RING + s * 4096, [P, D]) for s in range(2)]
        whi = [at(f"whi{s}", RING + (2 + s) * 4096, [P, D], R32) for s in range(2)]
        wlo = [at(f"wlo{s}", RING + (4 + s) * 4096, [P, D], R32) for s in range(2)]
        c = CON
        cols = at("cols", c, [P, NROW]); c += 480
        modT = at("modT", c, [P, NMOD, KD, 2]); c += 576
        gainT = at("gainT", c, [P, 3, KD, 2]); c += 192
        gateT = at("gateT", c, [P, 3, KD, 2]); c += 192
        cond = at("cond", c, [P, KD, 2]); c += 64
        epsT = at("epsT", c, [P, 1]); c += 32
        dummy = at("dummy", c, [P, 32]); c += 128
        ones = at("ones", c, [P, P]); c += 512
        ident = at("ident", c, [P, P]); c += 512
        identR = at("identR", c, [P, P], R32); c += 512
        mask_f = at("mask_f", c, [P, 2, P]); c += 1024
        maskR = at("maskR", c, [P, 2, P], R32); c += 1024
        altR = at("altR", c, [P, 2], R32); c += 32
        alt_f = at("alt_f", c, [P, 2]); c += 32
        sink_f = at("sink_f", c, [P, 16, 2]); c += 128
        sink_r = at("sink_r", c, [P, 16]); c += 64
        sinkH = at("sinkH", c, [P, 16, 2], R32); c += 128
        sinkL = at("sinkL", c, [P, 16, 2], R32); c += 128
        rows = at("rows", c, [NROW, P]); c += 512
        assert c <= POOL, c - POOL
        x_lat = at("x_lat", POOL, [P, KD, SEQ])
        x_ctx = at("x_ctx", POOL + 32768, [P, KD, CTX])
        Ch = at("Ch", POOL + 40960, [P, KD, CTX], R32)
        Cl = at("Cl", POOL + 49152, [P, KD, CTX], R32)
        NRM = POOL + 57344
        sq = {"pool": [at(f"sqp{s}", NRM + 2048 * s, [P, NT]) for s in range(2)],
              "dve": [at(f"sqd{s}", NRM + 4096 + 2048 * s, [P, NT]) for s in range(2)]}
        sums = {"pool": [at(f"sump{s}", NRM + 8192 + 2048 * s, [P, NT]) for s in range(2)],
                "dve": [at(f"sumd{s}", NRM + 12288 + 2048 * s, [P, NT]) for s in range(2)]}
        tn = [at(f"tn{s}", NRM + 2048 * s, [P, NT]) for s in range(4)]
        GB = NRM + 16384
        sinkR = at("sinkR", GB + 40960, [P, 16, 2], R32)
        onesR = at("onesR", GB + 40960 + 128, [P, P], R32)
        gH = at("gH", GB, [P, 2, SEQ + CTX], R32)
        gL = at("gL", GB + 10240, [P, 2, SEQ + CTX], R32)
        act_t = at("act_t", GB + 20480, [P, SEQ + CTX])
        dgn = at("dgn", GB + 32768, [P, NKT, P])
        sums["pool"].append(at("sump2", GB + 37888, [P, CTX]))
        sums["dve"].append(at("sumd2", GB + 38912, [P, CTX]))
        rms = at("rms", GB + 39936, [P, 2 * NKT])
        rinv = at("rinv", GB + 40032, [P, 2 * NKT])
        RSTD_BANK = [6, 7, 5]
        x_in = at("x_in", HH, [P, NKT, D])
        ada = [at(f"ada{s}", GB + 4096 * s, [P, D]) for s in range(8)]
        adaH = whi + [at(f"adaH{s}", HL + 8192 + 4096 * s, [P, D], R32) for s in range(2)]
        adaL = wlo + [at(f"adaL{s}", HL + 16384 + 4096 * s, [P, D], R32) for s in range(2)]
        mod_row = at("mod_row", NRM, [4, D])
        condS = at("condS", GB + 40128, [P, KD, 4], R32)
        pick = at("pick", GB + 40256, [4, 2])
        xcH = at("xcH", POOL, [P, NG, NB, 2 * P], R32)
        xcL = at("xcL", GB + 8192, [P, NG, NB, 2 * P], R32)
        chan_f = at("chan_f", POOL + 32768, [P, 2 * P])
        chanH = at("chanH", POOL + 33792, [P, 2 * P], R32)
        chanL = at("chanL", POOL + 34816, [P, 2 * P], R32)
        uH = [at(f"uH{s}", NRM + 8192 * s, [P, SEQ], R32) for s in range(2)]
        uL = [at(f"uL{s}", NRM + 8192 * s + 4096, [P, SEQ], R32) for s in range(2)]
        fT = at("fT", NRM, [P, SEQ])
        fH = [at(f"fH{s}", (NRM + 4096, POOL + 32768)[s], [P, SEQ], R32) for s in range(2)]
        fL = [at(f"fL{s}", (NRM + 8192, POOL + 36864)[s], [P, SEQ], R32) for s in range(2)]
        fB = at("fB", NRM + 12288, [P, NT])
        ROPE = GB
        cosT = at("cosT", ROPE, [P, SEQ])
        sinT = at("sinT", ROPE + 4096, [P, SEQ])
        swp = [at(f"swp{s}", ROPE + 8192 + 2048 * s, [P, NT]) for s in range(2)]
        rot = [at(f"rot{s}", ROPE + 12288 + 2048 * s, [P, NT]) for s in range(2)]
        kH = [at(f"kH{s}", POOL + 2048 * s, [P, NT], R32) for s in range(2)]
        kL = [at(f"kL{s}", POOL + 4096 + 2048 * s, [P, NT], R32) for s in range(2)]
        vT = [at(f"vT{s}", POOL + 8192 + 5120 * s, [P, NKT, P]) for s in range(2)]
        vS = [at(f"vS{s}", POOL + 18432 + 10240 * s, [P, 2, NKT, 2, HEAD], R32) for s in range(2)]
        o = POOL
        keyH = at("keyH", o, [P, SEQ + CTX], R32); o += 5120
        keyL = at("keyL", o, [P, SEQ + CTX], R32); o += 5120
        val = at("val", o, [P, NKT, P], R32); o += 5120
        qS = [at(f"qS{h}", o + 4096 * h, [P, SEQ], R32) for h in range(2)]; o += 8192
        pr = [[at(f"pr{s}{h}", o + (2 * s + h) * 2592, [P, 642]) for h in range(2)] for s in range(2)]
        o += 4 * 2592
        ptH = [at(f"ptH{s}", o + 5120 * s, [P, 5 * 2 * P], R32) for s in range(2)]; o += 10240
        ptL = [at(f"ptL{s}", o + 5120 * s, [P, 5 * 2 * P], R32) for s in range(2)]; o += 10240
        oLow = [at(f"oLow{s}", o + 1024 * s, [HEAD, 2, P]) for s in range(2)]; o += 2048
        aT = at("aT", o, [P, SEQ]); o += 4096
        aH = at("aH", o, [P, SEQ], R32); o += 4096
        aL = at("aL", o, [P, SEQ], R32); o += 4096
        dg = [[at(f"dg{s}{h}", o + 1024 * s + 512 * h, [P, P]) for h in range(2)] for s in range(2)]
        o += 2048
        nmax = at("nmax", o, [P, 4]); o += 32
        lsum = at("lsum", o, [P, 4]); o += 32
        rsum = at("rsum", o, [P, 4]); o += 32
        assert o <= ROPE
        qS = [qS, [at(f"qT{h}", ROPE + 16384 + 4096 * h, [P, SEQ], R32) for h in range(2)]]
        y = at("y", POOL, [P, KD, SEQ])
        gate_a = at("gate_a", POOL + 32768, [P, KD, SEQ])
        fouH = at("fouH", POOL + 98304, [P, NG, SEQ], R32)
        fouL = at("fouL", ROPE, [P, NG, SEQ], R32)
        A_AT = [(POOL + 90112, POOL + 94208), (POOL + 65536, POOL + 69632), (POOL + 98304, POOL + 102400), (POOL + 106496, POOL + 110592),
                (ROPE, ROPE + 4096), (ROPE + 8192, ROPE + 12288), (HH + 24576, HL + 24576), (HH + 28672, HL + 28672)]
        attH = [at(f"attH{k}", A_AT[k][0], [P, SEQ], R32) for k in range(KD)]
        attL = [at(f"attL{k}", A_AT[k][1], [P, SEQ], R32) for k in range(KD)]
        assert base + POOL + 114688 <= 229368
        YK = KD - 2
        Yh = at("Yh", HH, [P, YK, SEQ], R32)
        Yl = at("Yl", HL, [P, YK, SEQ], R32)
        mergedH = [Yh[:, k, :] for k in range(YK)] + [at(f"YhE{k}", POOL + 32768 + 8192 * k, [P, SEQ], R32)[:, :] for k in range(2)]
        mergedL = [Yl[:, k, :] for k in range(YK)] + [at(f"YlE{k}", POOL + 36864 + 8192 * k, [P, SEQ], R32)[:, :] for k in range(2)]
        gdiag = at("gdiag", GB + 25600, [P, KD, P])
        orow = [at(f"orow{s}", HL + 4096 * s, [P, D]) for s in range(2)]

        ps = ctx.enter_context(nc.psum_tensor("ps", [P, 8, NT], F32))

        x_scr = nc.dram_tensor("x_scr", [P, KD, SEQ], F32).ap()
        f_scr = nc.dram_tensor("f_scr", [NG, 2, P, SEQ], R32).ap()
        k_scr = nc.dram_tensor("k_scr", [2, 2 * P, SEQ + CTX], R32).ap()
        v_scr = nc.dram_tensor("v_scr", [P, NKV, NKT * P], R32).ap()
        a_scr = nc.dram_tensor("a_scr", [KD, 2, P, SEQ], R32).ap()

        rows_in = sem("rows_in"); const_in = sem("const_in")
        x_tile_in = [sem(f"x_tile_in{t}") for t in range(NKT)]
        ones_set = sem("ones_set"); consts_set = sem("consts_set")
        cols_set = sem("cols_set"); cond_set = sem("cond_set")
        x_turned = sem("x_turned"); x_even = sem("x_even"); x_odd = sem("x_odd")
        ada_in = [sem(f"ada_in{s}") for s in range(8)]
        ada_used = sem("ada_used"); mod_set = sem("mod_set"); ada_hi = sem("ada_hi"); ada_lo = sem("ada_lo"); row_out = sem("row_out"); mod_turned = sem("mod_turned"); ident_in = sem("ident_in"); gain_set = sem("gain_set")
        panel_in = [sem(f"panel_in{s}") for s in range(2)]
        panel_hi = sem("panel_hi"); panel_split = sem("panel_split"); psum_filled = sem("psum_filled")

        def norm_sems(j):
            return {n: sem(f"n{j}_{n}") for n in ("sq", "pool_add", "dve_add", "ss", "rms", "inv", "dg") + (("rstd", "t", "hi", "lo", "pool_lo") if j < 4 else ())}

        def ffn_sems(j):
            return {n: sem(f"f{j}_{n}") for n in ("silu", "prod", "ghi", "glo", "acc")}

        N1, N2, N3, N4 = (norm_sems(j) for j in range(1, 5))
        F1, F2 = ffn_sems(1), ffn_sems(2)
        x_saved = sem("x_saved")
        u_hi = sem("u_hi"); u_lo = sem("u_lo"); xc_hi = sem("xc_hi"); xc_lo = sem("xc_lo")
        fb_out = sem("fb_out"); f_sum = sem("f_sum"); f_hi = sem("f_hi"); f_lo = sem("f_lo"); f_saved = [sem(f"f_saved{s}") for s in range(2)]; chan_in = sem("chan_in"); chan_hi = sem("chan_hi"); chan_lo = sem("chan_lo")
        rope_in = sem("rope_in"); swapped = sem("swapped"); sin_mul = sem("sin_mul"); rot_set = sem("rot_set")
        k_hi = sem("k_hi"); k_lo = sem("k_lo"); k_saved = [sem(f"k_saved{s}") for s in range(2)]
        v_out = sem("v_out"); v_hi = sem("v_hi"); v_lo = sem("v_lo"); v_saved = sem("v_saved"); cos_mul = sem("cos_mul"); a_saved = sem("a_saved")
        key_in = sem("key_in"); key_rest = sem("key_rest"); val_in = sem("val_in"); q_hi = sem("q_hi"); q_lo = sem("q_lo")
        qk_done = sem("qk_done"); max_set = sem("max_set"); exp_set = sem("exp_set"); rsum_set = sem("rsum_set")
        prob_set = sem("prob_set"); pt_turned = sem("pt_turned"); pt_hi = sem("pt_hi"); pt_lo = sem("pt_lo")
        pv_done = sem("pv_done"); o_low = sem("o_low"); o_out = sem("o_out")
        a_hi = sem("a_hi"); a_lo = sem("a_lo")
        fou_in = sem("fou_in"); att_in = sem("att_in"); att_in_late = sem("att_in_late"); sgf = sem("sgf"); yf = sem("yf"); sga = sem("sga"); ya = sem("ya"); ysum = sem("ysum")
        y_hi = sem("y_hi"); y_lo = sem("y_lo"); x_back = sem("x_back")
        x_res = sem("x_res")
        o_turned = sem("o_turned"); o_even = sem("o_even"); o_odd = sem("o_odd"); stored = [sem(f"stored{s}") for s in range(2)]

        CREDIT = [(panel_split, 2), (F1["silu"], 3), (F1["prod"], 3), (F1["glo"], 3), (F1["acc"], 4),
                  (F2["silu"], 2), (F2["prod"], 2), (F2["glo"], 2), (F2["acc"], 4),
                  (exp_set, 2), (pt_lo, 2), (o_out, 1),
                  (mod_set, 1), (mod_turned, 1), (pv_done, 1), (sgf, 2), (yf, 2), (sga, 4), (ya, 4), (x_res, 4)]

        w_in = {1: T["w_ffn1_in"], 2: T["w_ffn2_in"]}
        w_out = {1: T["w_ffn1_out"], 2: T["w_ffn2_out"]}
        LAT = [(x_lat, Hh, Hl, 0, NT, 0, 0), (x_lat, Hh, Hl, NT, NT, 0, NT)]
        ALL = LAT + [(x_ctx, Ch, Cl, 0, CTX, 1, SEQ)]

        def chunks(w):
            return w.rearrange("(k p) n -> p k n", p=P)

        def ffn_done(S, nb, b, k):
            return S["acc"], 4 + 8 * nb * (NPAIR - 1) + (k // 4 * nb + b) * 4 + k % 4 + 1

        def after_ffn(S, nb):
            return [(b, k, "pool" if k < 4 or b == 2 else "dve", ffn_done(S, nb, b, k))
                    for half in range(2) for b in range(nb) for k in range(4 * half, 4 * half + 4)]
        ORDER = {"n1": [(b, k, "pool" if k in (1, 4, 7) else "dve", None) for b in range(3) for k in range(KD)],
                 "n2": after_ffn(F1, 3),
                 "n3": [(b, k, "dve" if k >= 5 else "pool", (x_res, 4 + 2 * k + b + 1)) for k in range(KD) for b in range(2)],
                 "n4": after_ffn(F2, 2)}

        def low_part(S, b, k):
            return S["pool_lo" if k % 2 else "lo"], b * (KD // 2) + k // 2 + 1

        def low_parts(eng, S, b):
            for k in (KD - 2, KD - 1):
                eng.wait_ge(*low_part(S, b, k))

        def low_of(eng, S, blocks, j, b, k):
            _, hi, lo, t0, n, c, _ = blocks[b]
            eng.wait_ge(S["hi"], (b * KD + k) // 2 * 3 + (3 if k % 2 else 1))
            if k % 2:
                eng.tensor_tensor(lo[:, k, t0:t0 + n], tn[k % 4][:, 0:n], hi[:, k, t0:t0 + n].bitcast(F32),
                                  ALU.subtract).then_inc(S["pool_lo"], 1)
                return
            eng.scalar_tensor_tensor(lo[:, k, t0:t0 + n], tn[k % 4][:, 0:n], modT[:, 3 * j, k, c:c + 1],
                                     hi[:, k, t0:t0 + n].bitcast(F32), ALU.add, ALU.subtract).then_inc(S["lo"], 1)

        def adds(eng, engine, S, order, blocks):
            r, seen = 0, set()
            for u, (b, k, who, _) in enumerate(order):
                if who != engine:
                    continue
                if b not in seen:
                    seen.add(b)
                    continue
                n = blocks[b][4]
                eng.wait_ge(S["sq"], u + 1)
                if r > 0:
                    eng.wait_ge(S[engine + "_add"], r)
                eng.tensor_tensor(sums[engine][b][:, 0:n], sums[engine][b][:, 0:n], sq[engine][r % 2][:, 0:n], ALU.add).then_inc(S[engine + "_add"], 1)
                r += 1

        def added(order, engine, b):
            r, seen, last = 0, set(), 0
            for ob, _, who, _ in order:
                if who == engine:
                    r += ob in seen
                    seen.add(ob)
                    last = r if ob == b else last
            return last

        def k3(t):
            return t[:, :].rearrange("p (k n) -> p k n", k=KD)

        block = ctx.enter_context(nc.Block())

        @block.sync
        def _(sp):
            sp.dma_start(rows[ROW_B:ROW_C, :], T["b_ada"].rearrange("(r n) -> r n", n=P)).then_inc(rows_in, 16)
            for r, name in ((ROW_C, "c"), (ROW_CCTX, "c_ctx"), (ROW_G1, "g_ffn1"), (ROW_GM, "g_mix"),
                            (ROW_G2, "g_ffn2"), (ROW_GF, "g_final")):
                sp.dma_start(rows[r:r + KD, :], T[name].rearrange("(r n) -> r n", n=P)).then_inc(rows_in, 16)
            sp.dma_start(ident[:, :], T["ident"]).then_inc(ident_in, 16)
            for t in range(NKT):
                src = T["x"][t * P:(t + 1) * P, :] if t < NB else T["ctx"][(t - NB) * P:(t - NB + 1) * P, :]
                sp.dma_start(x_in[:, t, :], src).then_inc(x_tile_in[t], 16)

            def ada_load(m, k):
                sp.dma_start(ada[k][:, :], T["w_ada"][k * P:(k + 1) * P, bass.ds(m, D)]).then_inc(ada_in[k], 16)
            for k in range(KD):
                ada_load(0, k)
            with sp.Fori(1, NMOD) as m:
                at_m = sp.snap(m * D)
                for k in range(KD):
                    sp.wait_ge(ada_lo, m * KD + (k - KD + 1))
                    ada_load(at_m, k)
            sp.dma_start(mask_f[:, :, :], T["masks"]).then_inc(const_in, 16)
            sp.dma_start(alt_f[:, :], T["alt"]).then_inc(const_in, 16)
            sp.dma_start(sink_r[:, :], T["attn_sink"].partition_broadcast(P)).then_inc(a_saved, 16)

            def load(par, n, dst, src, at):
                at = at if isinstance(at, int) else sp.snap(at)
                sp.wait_ge(panel_split, n)
                sp.dma_start(dst, src(at)).then_inc(panel_in[par], 16)

            def ffn_load(j, p0):
                win, wout = chunks(w_in[j]), chunks(w_out[j])
                with sp.Fori(0, NPAIR) as i:
                    for fl in range(2):
                        for half in range(2):
                            s = 2 * fl + half
                            load(s % 2, i * 6 + (p0 + s + 1), k3(raw[s % 2]),
                                 lambda at: win[:, :, bass.ds(at, P)], i * (2 * P) + (half * FF + fl * P))
                    for half in range(2):
                        load(half, i * 6 + (p0 + 4 + half + 1), raw[half][:, :].rearrange("p (f n) -> p f n", f=2),
                             lambda at, half=half: wout[:, bass.ds(at, 2), half * NT:(half + 1) * NT], i * 2)
            ffn_load(1, PAN_FFN1)
            win = chunks(T["w_in"])
            for g in range(NG):
                load(g % 2, PAN_FOU + g + 1, k3(raw[g % 2]), lambda at, g=g: win[:, :, U_OFF + g * P:U_OFF + (g + 1) * P], 0)
            for n in range(NB):
                load(n % 2, PAN_FOU + NG + n + 1, raw[n % 2][:, :], lambda at, n=n: T["dft_pos"][n * P:(n + 1) * P, :], 0)
            for n in range(4):
                load(n % 2, PAN_KV + n + 1, k3(raw[n % 2]), lambda at, n=n: win[:, :, K_OFF + n * P:K_OFF + (n + 1) * P], 0)
            def att_load(n):
                load(n % 2, PAN_ATT + n + 1, k3(raw[n % 2]), lambda at: win[:, :, n * P:(n + 1) * P], 0)

            def key_load(g):
                for ends in (True, False):
                    for z, part in enumerate((keyH, keyL)):
                        for h in range(2):
                            dst = part[HEAD * h:HEAD * (h + 1), :].bitcast(F32)
                            of = k_scr[z, g * HEAD:(g + 1) * HEAD, :].bitcast(F32)
                            if ends:
                                dst, of = (t.rearrange("p (a n) -> p a n", n=2 * P)[:, 0:5:4, :] for t in (dst, of))
                            else:
                                dst, of = dst[:, 2 * P:SEQ], of[:, 2 * P:SEQ]
                            sp.dma_start(dst, of).then_inc(key_in if ends else key_rest, 16)

            def val_load(g):
                sp.dma_start(val[:, :, :].rearrange("p t n -> p (t n)").bitcast(F32), v_scr[:, g, :].bitcast(F32)).then_inc(val_in, 16)

            att_load(0)
            att_load(1)
            for s in range(2):
                sp.wait_ge(k_saved[s], 32 * 3)
            sp.wait_ge(v_saved, 32)
            sp.wait_ge(v_lo, 6)
            key_load(0)
            val_load(0)
            att_load(2)
            att_load(3)
            wf, wa, wo = chunks(T["w_fourier_branch"]), chunks(T["w_attn_branch"]), chunks(T["w_out"])

            def fou_gate_load(d, z=0):
                load(0, d * 2 + (PAN_MRG + 2 * z + 1), k3(raw[0]), lambda at: win[:, :, bass.ds(at, P)], d * P + (z * P + GF_OFF))

            def fou_load(d, z=0):
                load(1, d * 2 + (PAN_MRG + 2 * z + 2), raw[1][:, 0:NG * P].rearrange("p (k n) -> p k n", k=NG), lambda at: wf[:, :, bass.ds(at, P)], d * P + z * P)
            for s in range(2):
                sp.wait_ge(f_saved[s], 32 * NG // 2)
            sp.dma_start(fouH[:, :, :].bitcast(F32), f_scr[:, 0, :, :].rearrange("g p n -> p g n").bitcast(F32)).then_inc(fou_in, 16)
            for j in range(2 * NKV):
                if j + 4 < 2 * NKV:
                    att_load(j + 4)
                if j == 2 * NKV - 2:
                    fou_gate_load(0)
                if j == 2 * NKV - 1:
                    fou_load(0)
                    sp.wait_ge(q_lo, 8 * NKV)
                    sp.dma_start(fouL[:, :, :].bitcast(F32), f_scr[:, 1, :, :].rearrange("g p n -> p g n").bitcast(F32)).then_inc(fou_in, 16)
                if j % 2 and j + 1 < 2 * NKV:
                    sp.wait_ge(qk_done, 2 * NB * (j + 1))
                    key_load(j // 2 + 1)
                    sp.wait_ge(pv_done, 1 + NB * (j + 1))
                    val_load(j // 2 + 1)
                sp.wait_ge(a_lo, 2 * j + 2)
                for z, part in enumerate((aH, aL)):
                    sp.dma_start(a_scr[j, z, :, :].bitcast(F32), part[:, :].bitcast(F32)).then_inc(a_saved, 16)
            with sp.Fori(0, KD - 1) as d:
                fou_gate_load(d, 1)
                fou_load(d, 1)
            with sp.Fori(0, KD // 2) as i:
                for n in range(2):
                    load(n, i * 2 + (PAN_MRG + 2 * KD + n + 1), k3(raw[n]), lambda at: win[:, :, bass.ds(at, P)], i * (2 * P) + (GA_OFF + n * P))
            with sp.Fori(0, KD // 2) as i:
                for n in range(2):
                    load(n, i * 2 + (PAN_MRG + 3 * KD + n + 1), k3(raw[n]), lambda at: wa[:, :, bass.ds(at, P)], i * (2 * P) + n * P)
            with sp.Fori(0, KD // 2) as i:
                for n in range(2):
                    load(n, i * 2 + (PAN_OUT + n + 1), k3(raw[n]), lambda at: wo[:, :, bass.ds(at, P)], i * (2 * P) + n * P)
            ffn_load(2, PAN_FFN2)
            for t in range(NB):
                sp.wait_ge(o_even, t + 1)
                sp.wait_ge(o_odd, t + 1)
                sp.dma_start(T["out"][t * P:(t + 1) * P, :], orow[t % 2][:, :]).then_inc(stored[t % 2], 16)
            for s in range(2):
                sp.wait_ge(stored[s], 16 * NB // 2)

        @block.tensor
        def _(pe):
            pe.wait_ge(rows_in, 7 * 16)
            pe.wait_ge(ident_in, 16)
            pe.transpose(ps[:, 6, 0:NROW], rows[:, :], ident[0:NROW, 0:NROW]).then_inc(psum_filled, 1)
            for t in range(NKT):
                pe.wait_ge(x_tile_in[t], 16)
                for half in range(2):
                    if t >= 2:
                        pe.wait_ge(x_odd if half else x_even, t - 1)
                    for k in range(4):
                        kk = half * 4 + k
                        mm = pe.transpose(ps[:, 2 * (t % 2) + half, k * P:(k + 1) * P], x_in[:, t, kk * P:(kk + 1) * P], ident[:, :])
                    mm.then_inc(x_turned, 1)
            def norm_mm(S, blocks, order):
                norm_sums(S, blocks, order)
                tiles = 0
                for b, (_, _, _, _, n, _, _) in enumerate(blocks):
                    pe.wait_ge(S["dg"], tiles + n // P)
                    for t in range(n // P):
                        mm = pe.matmul(ps[:, RSTD_BANK[b], t * P:(t + 1) * P], ones[:, :], dgn[:, tiles + t, :],
                                       start=(t == 0), stop=True, skip_group_check=True)
                    mm.then_inc(S["rstd"], 1)
                    tiles += n // P

            def norm_sums(S, blocks, order):
                tiles = 0
                for b, (_, _, _, _, n, _, _) in enumerate(blocks):
                    for e, engine in enumerate(("pool", "dve")):
                        if not any(o[0] == b and o[2] == engine for o in order):
                            continue
                        pe.wait_ge(S["sq"], 1 + max(u for u, o in enumerate(order) if o[0] == b and o[2] == engine))
                        if added(order, engine, b):
                            pe.wait_ge(S[engine + "_add"], added(order, engine, b))
                        for t in range(n // P):
                            z = 2 * (tiles + t)
                            mm = pe.matmul(ps[:, 4, z:z + 2], sums[engine][b][:, t * P:(t + 1) * P], ones[:, 0:2],
                                           start=(z == 0 and e == 0), stop=True, skip_group_check=True)
                    mm.then_inc(S["ss"], 1)
                    tiles += n // P

            def three(out, lh, ll, rh, rl, start, stop):
                pe.matmul(out, lh, rh, start=start, stop=False)
                pe.matmul(out, lh, rl, start=False, stop=False)
                return pe.matmul(out, ll, rh, start=False, stop=stop)

            def project(bank, s, hi, lo, t0, n, nk=KD, waits={}):
                for k in range(nk):
                    rh, rl = (t[k][:, t0:t0 + n] if isinstance(t, list) else t[:, k, t0:t0 + n] for t in (hi, lo))
                    if k in waits:
                        pe.wait_ge(*waits[k])
                    mm = three(ps[:, bank, 0:n], whi[s][:, k * P:(k + 1) * P], wlo[s][:, k * P:(k + 1) * P],
                               rh, rl, k == 0, k == nk - 1)
                mm.then_inc(psum_filled, 1)

            def ffn_mm(S, blocks, p0, NS):
                nb = len(blocks)
                with pe.Fori(0, NPAIR) as i:
                    for fl in range(2):
                        for half in range(2):
                            s = 2 * fl + half
                            pe.wait_ge(panel_split, i * 6 + (2 + p0 + s + 1))
                            for b, (_, hi, lo, t0, n, _, _) in enumerate(blocks):
                                early = half == 0 and fl == 0
                                if not early:
                                    low_parts(pe, NS, b)
                                pe.wait_ge(S["prod" if half else "silu"], i * (2 * nb) + (fl * nb + b + 1))
                                if half and fl == 0:
                                    pe.wait_ge(S["acc"], i * (8 * nb) + 4)
                                project(3 * half + b, s % 2, hi, lo, t0, n,
                                        waits={k: low_part(NS, b, k) for k in range(KD)} if early else {})
                    for half in range(2):
                        pe.wait_ge(panel_split, i * 6 + (2 + p0 + 4 + half + 1))
                        for b, (_, _, _, _, n, _, g0) in enumerate(blocks):
                            if half == 0:
                                pe.wait_ge(S["glo"], i * (2 * nb) + (nb + nb + b + 1))
                            for d in range(4):
                                if half == 0 and b == 0 and d >= 2 and d - 1 < nb:
                                    pe.wait_ge(S["prod"], i * (2 * nb) + (nb + nb + d - 1 + 1))
                                pe.wait_ge(S["acc"], i * (8 * nb) + ((half * nb + b) * 4 + d + 1))
                                for fl in range(2):
                                    w = slice(fl * NT + d * P, fl * NT + (d + 1) * P)
                                    mm = three(ps[:, 4 + (d + 2) % 4, 0:n], whi[half][:, w], wlo[half][:, w],
                                               gH[:, fl, g0:g0 + n], gL[:, fl, g0:g0 + n], fl == 0, fl == 1)
                                mm.then_inc(psum_filled, 1)

            pe.wait_ge(ones_set, 1)
            pe.wait_ge(cols_set, 1)

            pe.wait_ge(cond_set, 4)

            def ada_mm(m, k):
                pe.wait_ge(ada_lo, m * KD + (k + 1))
                if k == 0 and not isinstance(m, int):
                    pe.wait_ge(row_out, m * 2)
                for half in range(2):
                    w = slice(half * NT, (half + 1) * NT)
                    pe.matmul(ps[0:4, half, :], condS[:, k, :], adaH[k % 4][:, w], start=(k == 0), stop=False)
                    mm = pe.matmul(ps[0:4, half, :], condS[:, k, :], adaL[k % 4][:, w], start=False, stop=(k == KD - 1))
                mm.then_inc(ada_used, 1)

            def ada_turn(m):
                pe.wait_ge(row_out, m * 2)
                pe.wait_ge(mod_set, m)
                for d in range(KD):
                    mm = pe.matmul(ps[:, 2, 2 * d:2 * d + 2], mod_row[:, d * P:(d + 1) * P], pick[:, :],
                                   start=(d == 0), stop=True, skip_group_check=True)
                mm.then_inc(mod_turned, 1)
            for k in range(KD):
                ada_mm(0, k)
            norm_mm(N1, ALL, ORDER["n1"])
            with pe.Fori(1, NMOD) as m:
                for k in range(KD):
                    ada_mm(m, k)
                    if k == 1:
                        ada_turn(m)
            ada_turn(NMOD)
            ffn_mm(F1, ALL, PAN_FFN1, N1)
            pe.wait_ge(F1["acc"], 4 + 24 * NPAIR)
            norm_mm(N2, ALL, ORDER["n2"])

            pe.wait_ge(consts_set, 1)

            def u_project(g):
                pe.wait_ge(panel_split, 2 + PAN_FOU + g + 1)
                for b, (_, hi, lo, t0, n, _, _) in enumerate(LAT):
                    if g >= 2:
                        pe.wait_ge(u_lo, 2 * (g - 2) + b + 1)
                    project(2 * (g % 2) + b, g % 2, hi, lo, t0, n,
                            waits={k: low_part(N2, b, k) for k in range(KD)} if g == 0 else {})

            def u_channels(g):
                for n in range(NB):
                    if n % 4 == 0:
                        pe.wait_ge(u_lo, 2 * g + n // 4 + 1)
                    if g * NB + n >= 4:
                        pe.wait_ge(xc_lo, g * NB + n - 3)
                    w = slice(n * P, (n + 1) * P)
                    three(ps[:, 4 + n % 4, 0:2 * P], uH[g % 2][:, w], uL[g % 2][:, w], chanH[:, :], chanL[:, :],
                          True, True).then_inc(psum_filled, 1)
            u_project(0)
            u_project(1)
            pe.wait_ge(chan_lo, 1)
            low_parts(pe, N2, 2)
            u_channels(0)
            u_project(2)
            u_channels(1)
            u_project(3)
            u_channels(2)
            u_channels(3)
            pe.wait_ge(u_lo, 2 * NG)
            for n in range(NB):
                pe.wait_ge(panel_split, 2 + PAN_FOU + NG + n + 1)
                st, sp_ = n == 0, n == NB - 1
                for g in range(NG):
                    if st:
                        pe.wait_ge(xc_lo, NG * NB)
                    def alternating():
                        pe.matmul(ps[:, 2 * g + 1, 0:2], xcH[:, g, n, 0:P], altR[:, :], start=False, stop=False, skip_group_check=True)
                        return pe.matmul(ps[:, 2 * g + 1, 0:2], xcL[:, g, n, 0:P], altR[:, :], start=False, stop=False, skip_group_check=True)
                    if not st:
                        alternating()
                    for z in range(2):
                        mm = three(ps[:, 2 * g + z, :], xcH[:, g, n, z * P:(z + 1) * P], xcL[:, g, n, z * P:(z + 1) * P],
                                   whi[n % 2][:, z * NT:(z + 1) * NT], wlo[n % 2][:, z * NT:(z + 1) * NT], st, sp_)
                    if st:
                        mm = alternating()
                    if sp_ or g == NG - 1:
                        mm.then_inc(psum_filled, 1)

            for n in range(4):
                pe.wait_ge(panel_split, 2 + PAN_KV + n + 1)
                for b, (_, hi, lo, t0, m, _, _) in enumerate(ALL):
                    low_parts(pe, N2, b)
                    bank = 3 * (n % 2) + b
                    if n < 2:
                        pe.wait_ge(f_sum, bank // 2 + 1)
                    else:
                        pe.wait_ge(rot_set, 3 * (n - 2) + b + 1)
                    project(bank, n % 2, hi, lo, t0, m)
            pe.wait_ge(f_sum, NG)
            for e in range(6):
                vc, g0 = e // 3, 4 * (e % 3)
                pe.wait_ge(v_out, 3 * vc + e % 3 + 1)
                if e >= 2:
                    pe.wait_ge(v_lo, e - 1)
                for t in range(min(4, NKT - g0)):
                    mm = pe.transpose(ps[:, 6 + e % 2, t * P:(t + 1) * P], vT[vc][:, g0 + t, :], ident[:, :])
                mm.then_inc(psum_filled, 1)

            pe.wait_ge(v_lo, 6)

            def q_part(pj, b, bank, k0, k1):
                s = pj % 2
                for k in range(k0, k1):
                    mm = three(ps[:, bank, :], whi[s][:, k * P:(k + 1) * P], wlo[s][:, k * P:(k + 1) * P],
                               Hh[:, k, b * NT:(b + 1) * NT], Hl[:, k, b * NT:(b + 1) * NT], k == 0, k == KD - 1)
                if k1 == KD:
                    mm.then_inc(psum_filled, 1)

            def scores(g, pj, b, h):
                keys = KEYS[b]
                loc = len(keys) - 2
                if h == 0:
                    pe.wait_ge(q_lo, g * 8 + (pj * 4 + (b // 4 + 1) * 2))
                pe.wait_ge(exp_set, g * (4 * NB) + ((pj * NB + b) * 2 + h + 1))
                S = ps[:, 2 * h:2 * h + 2, :].rearrange("p a n -> p (a n)")
                q = qS[pj % 2][h][:, b * P:(b + 1) * P]
                k0 = keys[0] * P
                inner = len(keys) == 5

                def near(part):
                    if inner:
                        return part[:, k0:k0 + 4 * P].rearrange("p (a n) -> p a n", a=2)[:, :, 0:P]
                    return part[:, k0:k0 + 2 * P]
                runs = [(0, near), (2 * P, lambda part: part[:, SEQ:SEQ + 2 * P])]
                if inner:
                    runs += [(4 * P, lambda part: part[:, b * P:(b + 1) * P])]
                for r0, of in runs:
                    w = P if r0 == 4 * P else 2 * P
                    pe.matmul(S[:, r0:r0 + w], q, of(keyH), start=(r0 % NT == 0), stop=False, skip_group_check=True)
                    pe.matmul(S[:, r0:r0 + w], q, of(keyL), start=False, stop=True, skip_group_check=True)
                if inner:
                    pe.matmul(S[:, 0:2 * P], identR[:, :], maskR[:, :, :], start=False, stop=True, skip_group_check=True)
                elif b == 0:
                    pe.matmul(S[:, P:2 * P], identR[:, :], maskR[:, 1, :], start=False, stop=True, skip_group_check=True)
                else:
                    pe.matmul(S[:, 0:P], identR[:, :], maskR[:, 0, :], start=False, stop=True, skip_group_check=True)
                r0 = len(keys) * P
                hd = bass.ds(g * 4 + (2 * pj + h), 1)
                pe.matmul(S[:, r0:r0 + 2], onesR[:, :], sinkR[:, hd, :], start=(r0 % NT == 0), stop=True,
                          skip_group_check=True).then_inc(qk_done, 1)

            def turn(g, pl, b, e):
                if e >= GROUPS[b]:
                    return
                if e == 0:
                    pe.wait_ge(prob_set, g * (4 * NB) + ((pl * NB + b) * 2 + 2))
                tiles = [(t, h) for t in range(len(KEYS[b])) for h in range(2)]
                pe.wait_ge(pt_lo, g * (2 * NGROUP) + (pl * NGROUP + GROUP0[b] + e + 1))
                for z, (t, h) in enumerate(tiles[4 * e:4 * e + 4]):
                    mm = pe.matmul(ps[:, 4 + (GROUP0[b] + e) % 2, z * P:(z + 1) * P], pr[b % 2][h][:, t * P:(t + 1) * P], dg[b % 2][h][:, :],
                                   start=(z == 0), stop=True, skip_group_check=True)
                mm.then_inc(pt_turned, 1)

            def mix(g, pl, b):
                keys = KEYS[b]
                pe.wait_ge(pt_lo, g * (2 * NGROUP) + (2 + pl * NGROUP + GROUP0[b] + GROUPS[b]))
                pe.wait_ge(o_out, g * (2 * NB) + (pl * NB + b + 1))
                if pl == 0 and b == 0:
                    pe.wait_ge(val_in, g * 16 + 16)
                for t, kt in enumerate(keys):
                    pe.matmul(ps[:, 7, 0:2 * P], val[:, kt, :], ptH[b % 2][:, t * 2 * P:(t + 1) * 2 * P], start=(t == 0), stop=False)
                    mm = pe.matmul(ps[:, 7, 0:2 * P], val[:, kt, :], ptL[b % 2][:, t * 2 * P:(t + 1) * 2 * P],
                                   start=False, stop=(t == len(keys) - 1))
                mm.then_inc(pv_done, 1)

            def pair(g, pl, last):
                fill = {0: (0, 0, 3), 1: (0, 3, 6), 2: (0, 6, 8), 4: (1, 0, 2), 5: (1, 2, 4), 6: (1, 4, 6), 7: (1, 6, 8)}
                for b in range(NB):
                    nxt = (pl, b + 1) if b + 1 < NB else (pl + 1, 0)
                    more = not (last and b == NB - 1)
                    if b == 0 and pl == 0:
                        pe.wait_ge(key_rest, g * 64 + 64)
                    if more and nxt != (2, 0):
                        scores(g, *nxt, 0)
                    turn(g, pl, b, 0)
                    if more and nxt != (2, 0):
                        scores(g, *nxt, 1)
                    turn(g, pl, b, 1)
                    if b >= 1:
                        mix(g, pl, b - 1)
                    turn(g, pl, b, 2)
                    if b in fill and not last:
                        half, k0, k1 = fill[b]
                        if k0 == 0:
                            if half == 0:
                                pe.wait_ge(panel_split, g * 2 + (2 + PAN_ATT + pl + 2))
                            pe.wait_ge(swapped, g * 4 + (4 + 2 * (pl + 1) + half))
                        q_part(pl + 1, half, 6, k0, k1)
                mix(g, pl, NB - 1)
                if pl == 1 and not last:
                    pe.wait_ge(key_in, g * 64 + 128)
                    scores(g, 2, 0, 0)
                    scores(g, 2, 0, 1)

            pe.wait_ge(panel_split, 2 + PAN_ATT + 1)
            q_part(0, 0, 6, 0, KD)
            q_part(0, 1, 7, 0, KD)
            pe.wait_ge(key_in, 64)
            scores(0, 0, 0, 0)
            scores(0, 0, 0, 1)
            pe.wait_ge(swapped, 6)
            with pe.Fori(0, NKV - 1) as g:
                for pl in range(2):
                    pair(g, pl, False)
            for pl in range(2):
                pair(NKV - 1, pl, pl == 1)

            with pe.Fori(0, KD) as d:
                pe.wait_ge(panel_split, d * 2 + (2 + PAN_MRG + 1))
                for b in range(2):
                    pe.wait_ge(sgf, d * 2 + (b + 1))
                    project(b, 0, Hh, Hl, b * NT, NT)
                pe.wait_ge(panel_split, d * 2 + (2 + PAN_MRG + 2))
                pe.wait_ge(fou_in, 32)
                for b in range(2):
                    pe.wait_ge(yf, d * 2 + (b + 1))
                    project(2 + b, 1, fouH, fouL, b * NT, NT, NG)
            pe.wait_ge(o_out, 1 + 2 * NB * NKV)
            with pe.Fori(0, KD // 2) as i:
                for n in range(2):
                    pe.wait_ge(panel_split, i * 2 + (2 + PAN_MRG + 2 * KD + n + 1))
                    for b in range(2):
                        pe.wait_ge(sga, i * 4 + (2 * n + b + 1))
                        project(4 + 2 * n + b, n, Hh, Hl, b * NT, NT)
            pe.wait_ge(yf, 2 + 2 * KD)
            with pe.Fori(0, KD // 2) as i:
                for n in range(2):
                    pe.wait_ge(panel_split, i * 2 + (2 + PAN_MRG + 3 * KD + n + 1))
                    for b in range(2):
                        pe.wait_ge(ya, i * 4 + (2 * n + b + 1))
                        project(2 * n + b, n, attH, attL, b * NT, NT,
                                waits={0: (att_in, 16 * 12), 6: (att_in_late, 16 * 4)})

            pe.wait_ge(sga, 4 + 2 * KD)
            with pe.Fori(0, KD // 2) as i:
                for n in range(2):
                    pe.wait_ge(panel_split, i * 2 + (2 + PAN_OUT + n + 1))
                    for b in range(2):
                        pe.wait_ge(x_res, i * 4 + (2 * n + b + 1))
                        project(4 + 2 * n + b, n, mergedH, mergedL, b * NT, NT,
                                waits={0: (y_lo, KD - 2), 6: (y_lo, KD - 1), 7: (y_lo, KD)})
            pe.wait_ge(x_res, 4 + 2 * KD)
            norm_mm(N3, LAT, ORDER["n3"])
            ffn_mm(F2, LAT, PAN_FFN2, N3)
            pe.wait_ge(F2["acc"], 4 + 16 * NPAIR)
            pe.wait_ge(N4["dg"], KD)
            for t in range(NB):
                if t == 2:
                    norm_sums(N4, LAT, ORDER["n4"])
                for half in range(2):
                    if t >= 2:
                        pe.wait_ge(o_odd if half else o_even, t - 1)
                    for k in range(4):
                        kk = half * 4 + k
                        mm = pe.matmul(ps[:, 2 * (t % 2) + half, k * P:(k + 1) * P], x_lat[:, kk, t * P:(t + 1) * P], gdiag[:, kk, :],
                                       start=(k == 0), stop=True, skip_group_check=True)
                    mm.then_inc(o_turned, 1)

        @block.scalar
        def _(act):
            act.wait_ge(cols_set, 1)
            for s, r in ((0, ROW_C), (1, ROW_CCTX)):
                act.activation(cond[:, :, s], cols[:, r:r + KD], ACT.Silu).then_inc(cond_set, 1)
            for t in range(NKT):
                act.wait_ge(x_turned, 2 * t + 1)
                dst = x_lat[:, 0:4, t * P:(t + 1) * P] if t < NB else x_ctx[:, 0:4, (t - NB) * P:(t - NB + 1) * P]
                act.activation(dst, ps[:, 2 * (t % 2), :].rearrange("p (k n) -> p k n", k=4), ACT.Copy).then_inc(x_even, 1)

            act.wait_ge(cond_set, 2)
            act.activation(condS[:, :, 0:2], cond[:, :, :], ACT.Copy).then_inc(cond_set, 1)

            def split_hi(s, nth, used):
                act.wait_ge(panel_in[s], nth)
                act.wait_ge(psum_filled, used)
                act.activation(whi[s][:, :], raw[s][:, :], ACT.Copy).then_inc(panel_hi, 1)

            def norm_act_sum(S, blocks, order):
                count, seen = {"pool": 0, "dve": 0}, set()
                for b, k, engine, ready in order:
                    x, t0, n = blocks[b][0], blocks[b][3], blocks[b][4]
                    if ready:
                        act.wait_ge(*ready)
                    if (engine, b) in seen:
                        r = count[engine]
                        count[engine] += 1
                        if r >= 2:
                            act.wait_ge(S[engine + "_add"], r - 1)
                        dst = sq[engine][r % 2]
                    else:
                        seen.add((engine, b))
                        dst = sums[engine][b]
                    act.activation(dst[:, 0:n], x[:, k, t0:t0 + n], ACT.Square).then_inc(S["sq"], 1)
                act.wait_ge(S["ss"], len(blocks))
                w = 2 * sum(blk[4] for blk in blocks) // P
                act.activation(rms[:, 0:w], ps[:, 4, 0:w], ACT.Sqrt, bias=epsT[:, 0:1], scale=1.0 / D).then_inc(S["rms"], 1)

            def norm_act(S, blocks, j, between=None):
                for b, (_, hi, _, t0, n, c, _) in enumerate(blocks):
                    for k in range(KD):
                        if b == 1 and k == 0 and between:
                            between()
                        act.wait_ge(S["t"], b * KD + k + 1)
                        act.activation(hi[:, k, t0:t0 + n], tn[k % 4][:, 0:n], ACT.Identity,
                                       bias=modT[:, 3 * j, k, c:c + 1]).then_inc(S["hi"], 1)
                        if k % 2:
                            act.activation(tn[k % 4][:, 0:n], tn[k % 4][:, 0:n], ACT.Identity,
                                           bias=modT[:, 3 * j, k, c:c + 1]).then_inc(S["hi"], 1)

            def ffn_act(S, blocks, p0, f0, last=False):
                nb = len(blocks)

                def body(i, final=False):
                    filled = [0, nb, 2 * nb, 3 * nb, 4 * nb, 8 * nb]
                    for s in range(6):
                        if not (final and s == 5):
                            split_hi((s + 1) % 2, i * 48 + 16 * ((p0 + s + 1) // 2 + 1), i * (12 * nb) + (f0 + filled[s]))
                        fl = s // 2
                        for b, (_, _, _, _, n, _, g0) in enumerate(blocks):
                            if s in (0, 2):
                                act.wait_ge(psum_filled, i * (12 * nb) + (f0 + filled[s] + b + 1))
                                act.wait_ge(S["glo"], i * (2 * nb) + (fl * nb + b + 1))
                                act.activation(act_t[:, g0:g0 + n], ps[:, b, 0:n], ACT.Silu).then_inc(S["silu"], 1)
                            if s in (1, 3):
                                act.wait_ge(S["prod"], i * (2 * nb) + (nb + fl * nb + b + 1))
                                act.activation(gH[:, fl, g0:g0 + n], act_t[:, g0:g0 + n], ACT.Copy).then_inc(S["ghi"], 1)
                with act.Fori(0, NPAIR - last) as i:
                    body(i)
                if last:
                    body(NPAIR - 1, True)

            act.wait_ge(x_odd, NKT)
            act.wait_ge(x_even, NKT)

            def ada_split(m, k):
                act.wait_ge(ada_in[k], m * 16 + 16)
                if not isinstance(m, int) or k >= 4:
                    act.wait_ge(ada_used, m * KD + (k - 3))
                act.activation(adaH[k % 4][:, :], ada[k][:, :], ACT.Copy).then_inc(ada_hi, 1)

            def row_copy(m):
                act.wait_ge(ada_used, m * KD)
                act.wait_ge(mod_turned, m)
                act.activation(mod_row[:, 0:NT], ps[0:4, 0, :], ACT.Copy).then_inc(row_out, 1)
            for k in range(KD):
                ada_split(0, k)
            norm_act_sum(N1, ALL, ORDER["n1"])
            with act.Fori(1, NMOD) as m:
                for k in range(KD):
                    ada_split(m, k)
                    if k == 1:
                        row_copy(m)
            act.wait_ge(ada_used, NMOD * KD - 3)
            split_hi(0, 16, 1)
            row_copy(NMOD)
            act.wait_ge(gain_set, 1)
            norm_act(N1, ALL, 0)
            ffn_act(F1, ALL, PAN_FFN1, FIL_FFN1)
            norm_act_sum(N2, ALL, ORDER["n2"])
            norm_act(N2, ALL, 1, lambda: split_hi(1, 16 * ((PAN_FOU + 1) // 2 + 1), FIL_FOU))

            act.wait_ge(x_saved, 16)
            low_parts(act, N2, 2)

            def fou_split(p, used):
                split_hi(p % 2, 16 * ((PAN_FOU + p) // 2 + 1), FIL_FOU + used)

            def u_out(g):
                for b in range(2):
                    act.wait_ge(psum_filled, FIL_FOU + (2 + NB) * max(g - 1, 0) + 2 * (g > 0) + b + 1)
                    act.activation(uH[g % 2][:, b * NT:(b + 1) * NT], ps[:, 2 * (g % 2) + b, :], ACT.Copy).then_inc(u_hi, 1)

            def xc_out(g):
                for n in range(NB):
                    act.wait_ge(psum_filled, FIL_FOU + 4 + (2 + NB) * g - 2 * (g == NG - 1) + n + 1)
                    act.activation(xcH[:, g, n, :], ps[:, 4 + n % 4, 0:2 * P], ACT.Copy).then_inc(xc_hi, 1)
            u_out(0)
            act.wait_ge(chan_in, 16)
            act.activation(chanH[:, :], chan_f[:, :], ACT.Copy).then_inc(chan_hi, 1)
            fou_split(2, 2)
            u_out(1)
            xc_out(0)
            fou_split(3, 4)
            u_out(2)
            xc_out(1)
            fou_split(4, 4 + NB + 2)
            u_out(3)
            xc_out(2)
            fou_split(5, 4 + 2 * NB + 4)
            xc_out(3)
            for n in range(NB - 1):
                fou_split(NG + n + 2, (2 + NB) * NG + n + 1)
            for g in range(NG):
                act.wait_ge(psum_filled, FIL_FOU + (2 + NB) * NG + NB - 1 + g + 1)
                if g > 0:
                    act.wait_ge(f_sum, g)
                act.activation(fB[:, :], ps[:, 2 * g + 1, :], ACT.Copy).then_inc(fb_out, 1)
                act.wait_ge(f_sum, g + 1)
                if g > 1:
                    act.wait_ge(f_saved[g % 2], 32 * (g // 2))
                act.activation(fH[g % 2][:, :], fT[:, :], ACT.Copy).then_inc(f_hi, 1)

            for n in range(4):
                split_hi((n + 1) % 2, 16 * ((PAN_KV + n + 1) // 2 + 1), FIL_KV + 3 * n)
                for b, (_, _, _, _, m, _, g0) in enumerate(ALL):
                    z = 3 * n + b
                    if n < 2:
                        act.wait_ge(rot_set, z + 1)
                        if z >= 2:
                            act.wait_ge(k_saved[z % 2], 32 * (z // 2))
                        act.activation(kH[z % 2][:, 0:m], rot[z % 2][:, 0:m], ACT.Copy).then_inc(k_hi, 1)
                    else:
                        act.wait_ge(psum_filled, FIL_KV + z + 1)
                        act.activation(vT[n - 2][:, g0 // P:(g0 + m) // P, :], ps[:, 3 * (n % 2) + b, 0:m].rearrange("p (t n) -> p t n", n=P),
                                       ACT.Copy).then_inc(v_out, 1)
            for e in range(6):
                vc, g0 = e // 3, 4 * (e % 3)
                w = min(4, NKT - g0)
                act.wait_ge(psum_filled, FIL_KV + 12 + e + 1)
                act.activation(vS[vc][:, :, g0:g0 + w, 0, :], ps[:, 6 + e % 2, 0:w * P].rearrange("p (t v e) -> p v t e", v=2, e=HEAD),
                               ACT.Copy).then_inc(v_hi, 1)

            act.wait_ge(k_saved[1], 32 * 3)
            act.wait_ge(k_saved[0], 32 * 3)
            act.wait_ge(v_saved, 32)

            def queries(g, pj, b):
                act.wait_ge(rot_set, g * 4 + (6 + 2 * pj + b + 1))
                for h in range(2):
                    r = slice(HEAD * h, HEAD * (h + 1))
                    act.activation(qS[pj % 2][h][r, b * NT:(b + 1) * NT], rot[b][r, :], ACT.Copy, scale=HEAD ** -0.5).then_inc(q_hi, 1)

            def expo(g, pj, b, h):
                act.wait_ge(max_set, g * (4 * NB) + ((pj * NB + b) * 2 + h + 1))
                n = len(KEYS[b]) * P + 2
                act.activation(pr[b % 2][h][:, 0:n], ps[:, 2 * h:2 * h + 2, :].rearrange("p a n -> p (a n)")[:, 0:n], ACT.Exp,
                               bias=nmax[:, 2 * (b % 2) + h:2 * (b % 2) + h + 1],
                               accum_out=lsum[:, 2 * (b % 2) + h:2 * (b % 2) + h + 1]).then_inc(exp_set, 1)

            def turned_hi(g, pl, b, e):
                if e >= GROUPS[b]:
                    return
                w = min(NT, 2 * len(KEYS[b]) * P - NT * e)
                act.wait_ge(pt_turned, g * (2 * NGROUP) + (pl * NGROUP + GROUP0[b] + e + 1))
                act.activation(ptH[b % 2][:, NT * e:NT * e + w], ps[:, 4 + (GROUP0[b] + e) % 2, 0:w], ACT.Copy).then_inc(pt_hi, 1)

            def low_out(g, pl, b):
                act.wait_ge(pv_done, g * (2 * NB) + (1 + pl * NB + b + 1))
                act.activation(oLow[b % 2][:, :, :], ps[HEAD:P, 7, 0:2 * P].rearrange("p (h n) -> p h n", h=2), ACT.Copy).then_inc(o_low, 1)

            def out_hi(g, pl, half):
                act.wait_ge(o_out, g * (2 * NB) + (1 + pl * NB + 4 * half + 4))
                act.wait_ge(a_saved, g * 64 + (32 * pl + 16))
                w = slice(half * NT, (half + 1) * NT)
                act.activation(aH[:, w], aT[:, w], ACT.Copy).then_inc(a_hi, 1)

            def pair(g, pl, last):
                for b in range(NB):
                    nxt = (pl, b + 1) if b + 1 < NB else (pl + 1, 0)
                    more = not (last and b == NB - 1)
                    more = more and nxt != (2, 0)
                    turned_hi(g, pl, b, 0)
                    if more:
                        expo(g, *nxt, 0)
                    turned_hi(g, pl, b, 1)
                    if more:
                        expo(g, *nxt, 1)
                    turned_hi(g, pl, b, 2)
                    if b >= 1:
                        low_out(g, pl, b - 1)
                    if b == 0:
                        queries(g, pl, 1)
                    if b == 4 and not last:
                        queries(g, pl + 1, 0)
                    if b == 5 and not last:
                        split_hi(pl, g * 16 + 16 * ((PAN_ATT + pl + 2) // 2 + 1), g * 4 + (FIL_ATT + 2 * pl + 2))
                    if b == 6:
                        out_hi(g, pl, 0)
                low_out(g, pl, NB - 1)
                if pl == 1 and not last:
                    expo(g, 2, 0, 0)
                    expo(g, 2, 0, 1)
                out_hi(g, pl, 1)

            split_hi(1, 16 * ((PAN_ATT + 1) // 2 + 1), FIL_ATT)
            queries(0, 0, 0)
            expo(0, 0, 0, 0)
            expo(0, 0, 0, 1)
            with act.Fori(0, NKV - 1) as g:
                for pl in range(2):
                    pair(g, pl, False)
            for pl in range(2):
                pair(NKV - 1, pl, pl == 1)

            def one(t, d, b):
                return t[:, bass.ds(d, 1), b * NT:(b + 1) * NT].rearrange("p a n -> p (a n)")

            with act.Fori(0, KD) as d:
                split_hi(1, d * 16 + 16 * ((PAN_MRG + 1) // 2 + 1), d * 4 + FIL_MRG)
                for b in range(2):
                    act.wait_ge(psum_filled, d * 4 + (FIL_MRG + b + 1))
                    act.activation(one(y, d, b), ps[:, b, :], ACT.Sigmoid).then_inc(sgf, 1)
                split_hi(0, d * 16 + 16 * ((PAN_MRG + 2) // 2 + 1), d * 4 + (FIL_MRG + 2))
            act.wait_ge(a_saved, 16 + 32 * KD)
            with act.Fori(0, KD // 2) as i:
                for n in range(2):
                    split_hi((n + 1) % 2, i * 16 + 16 * ((PAN_MRG + 2 * KD + n + 1) // 2 + 1), i * 4 + (FIL_MRG + 4 * KD + 2 * n))
                    for b in range(2):
                        act.wait_ge(psum_filled, i * 4 + (FIL_MRG + 4 * KD + 2 * n + b + 1))
                        act.activation(one(gate_a, i * 2 + n, b), ps[:, 4 + 2 * n + b, :], ACT.Sigmoid).then_inc(sga, 1)

            def merged_hi(i, n):
                act.wait_ge(ysum, i * 2 + (n + 1))
                if isinstance(i, int):
                    dst, yd = mergedH[2 * i + n], y[:, 2 * i + n, :]
                else:
                    dst, yd = (t[:, bass.ds(i * 2 + n, 1), :].rearrange("p a n -> p (a n)") for t in (Yh, y))
                act.activation(dst, yd, ACT.Copy).then_inc(y_hi, 1)

            def att_split(i, n):
                split_hi((n + 1) % 2, i * 16 + 16 * ((PAN_MRG + 3 * KD + n + 1) // 2 + 1), i * 4 + (FIL_MRG + 6 * KD + 2 * n))
            with act.Fori(0, KD // 2 - 1) as i:
                for n in range(2):
                    att_split(i, n)
                    merged_hi(i, n)
            for n in range(2):
                att_split(KD // 2 - 1, n)
                merged_hi(KD // 2 - 1, n)

            with act.Fori(0, KD // 2) as i:
                for n in range(2):
                    split_hi((n + 1) % 2, i * 16 + 16 * ((PAN_OUT + n + 1) // 2 + 1), i * 4 + (FIL_OUT + 2 * n))
            norm_act_sum(N3, LAT, ORDER["n3"])
            norm_act(N3, LAT, 2)
            ffn_act(F2, LAT, PAN_FFN2, FIL_FFN2, last=True)
            norm_act_sum(N4, LAT, ORDER["n4"])
            act.wait_ge(N4["inv"], 1)
            for t in range(NB):
                act.wait_ge(o_turned, 2 * t + 1)
                if t >= 2:
                    act.wait_ge(stored[t % 2], 16 * (t // 2))
                act.activation(orow[t % 2][:, 0:NT], ps[:, 2 * (t % 2), :], ACT.Copy, scale=rinv[:, 2 * t:2 * t + 1]).then_inc(o_even, 1)

        @block.vector
        def _(dve):
            dve.memset(ones[:, :], 1.0).then_inc(ones_set, 1)
            dve.memset(epsT[:, :], EPS)
            dve.wait_ge(psum_filled, 1)
            dve.tensor_copy(cols[:, :], ps[:, 6, 0:NROW]).then_inc(cols_set, 1)
            for t in range(NKT):
                dve.wait_ge(x_turned, 2 * t + 2)
                dst = x_lat[:, 4:8, t * P:(t + 1) * P] if t < NB else x_ctx[:, 4:8, (t - NB) * P:(t - NB + 1) * P]
                dve.tensor_copy(dst, ps[:, 2 * (t % 2) + 1, :].rearrange("p (k n) -> p k n", k=4)).then_inc(x_odd, 1)
            def split_lo(s, n):
                dve.wait_ge(panel_hi, n)
                dve.tensor_tensor(wlo[s][:, :], raw[s][:, :], whi[s][:, :].bitcast(F32), ALU.subtract).then_inc(panel_split, 1)

            def norm_dve_rstd(S, blocks, order, last=False):
                adds(dve, "dve", S, order, blocks)
                tiles = sum(blk[4] for blk in blocks) // P
                dve.wait_ge(S["rms"], 1)
                dve.reciprocal(rinv[:, 0:2 * tiles], rms[:, 0:2 * tiles]).then_inc(S["inv"], 1)
                dve.wait_ge(S["inv"], 1)
                for t in range(0 if last else tiles):
                    dve.tensor_scalar(dgn[:, t, :], ident[:, :], rinv[:, 2 * t:2 * t + 1], None, ALU.mult).then_inc(S["dg"], 1)

            def norm_dve(S, blocks, j, between=None):
                for b, (x, _, _, t0, n, c, _) in enumerate(blocks):
                    dve.wait_ge(S["rstd"], b + 1)
                    if b == 1 and between:
                        between()
                    for k in range(KD):
                        if b * KD + k >= 4:
                            dve.wait_ge(*low_part(S, b - (k < 4), (k - 4) % KD))
                        dve.scalar_tensor_tensor(tn[k % 4][:, 0:n], x[:, k, t0:t0 + n], gainT[:, j, k, c:c + 1],
                                                 ps[:, RSTD_BANK[b], 0:n], ALU.mult, ALU.mult).then_inc(S["t"], 1)
                        if k % 2:
                            low_of(dve, S, blocks, j, b, k - 1)

            def ffn_dve(S, blocks, p0, f0, j, last=False):
                nb = len(blocks)

                def body(i, final=False):
                    filled = [0, nb, 2 * nb, 3 * nb, 4 * nb, 8 * nb]
                    for s in range(6):
                        if not (final and s == 5):
                            split_lo((s + 1) % 2, i * 6 + (p0 + s + 2))
                        fl = s // 2
                        if s in (1, 3):
                            for b, (_, _, _, _, n, _, g0) in enumerate(blocks):
                                dve.wait_ge(psum_filled, i * (12 * nb) + (f0 + filled[s] + b + 1))
                                dve.wait_ge(S["silu"], i * (2 * nb) + (nb + fl * nb + b + 1))
                                dve.tensor_tensor(act_t[:, g0:g0 + n], ps[:, 3 + b, 0:n], act_t[:, g0:g0 + n], ALU.mult).then_inc(S["prod"], 1)
                                dve.wait_ge(S["ghi"], i * (2 * nb) + (fl * nb + b + 1))
                                dve.tensor_tensor(gL[:, fl, g0:g0 + n], act_t[:, g0:g0 + n], gH[:, fl, g0:g0 + n].bitcast(F32),
                                                  ALU.subtract).then_inc(S["glo"], 1)
                        if s >= 4:
                            for b, (x, _, _, t0, n, c, _) in enumerate(blocks):
                                for d in range(4):
                                    k = (s - 4) * 4 + d
                                    dve.wait_ge(psum_filled, i * (12 * nb) + (f0 + filled[s] + 4 * b + d + 1))
                                    dve.scalar_tensor_tensor(x[:, k, t0:t0 + n], ps[:, 4 + (d + 2) % 4, 0:n], gateT[:, j, k, c:c + 1],
                                                             x[:, k, t0:t0 + n], ALU.mult, ALU.add).then_inc(S["acc"], 1)
                with dve.Fori(0, NPAIR - last) as i:
                    body(i)
                if last:
                    body(NPAIR - 1, True)

            dve.wait_ge(cond_set, 3)
            dve.tensor_tensor(condS[:, :, 2:4], cond[:, :, :], condS[:, :, 0:2].bitcast(F32), ALU.subtract)
            dve.wait_ge(ident_in, 16)
            dve.tensor_tensor(pick[:, :], ident[0:4, 0:2], ident[0:4, 2:4], ALU.add).then_inc(cond_set, 1)

            def ada_split(m, k):
                dve.wait_ge(ada_hi, m * KD + (k + 1))
                dve.tensor_tensor(adaL[k % 4][:, :], ada[k][:, :], adaH[k % 4][:, :].bitcast(F32), ALU.subtract).then_inc(ada_lo, 1)

            def row_copy(m):
                dve.wait_ge(ada_used, m * KD)
                dve.wait_ge(mod_turned, m)
                dve.tensor_copy(mod_row[:, NT:D], ps[0:4, 1, :]).then_inc(row_out, 1)

            def mod_add(m):
                dve.wait_ge(mod_turned, m + 1)
                dve.tensor_tensor(modT[:, bass.ds(m - 1, 1), :, :], ps[:, 2, 0:2 * KD].rearrange("p (a d s) -> p a d s", a=1, s=2),
                                  cols[:, bass.ds((m - 1) * KD, KD)].unsqueeze(1).unsqueeze(3).to_broadcast([P, 1, KD, 2]), ALU.add).then_inc(mod_set, 1)
            for k in range(KD):
                ada_split(0, k)
            norm_dve_rstd(N1, ALL, ORDER["n1"])
            with dve.Fori(1, NMOD) as m:
                for k in range(KD):
                    ada_split(m, k)
                    if k == 1:
                        row_copy(m)
                    if k == 6:
                        mod_add(m)
            split_lo(0, 1)
            row_copy(NMOD)
            mod_add(NMOD)
            dve.wait_ge(mod_set, NMOD + 1)
            for j, r in enumerate((ROW_G1, ROW_GM, ROW_G2)):
                for s in range(2):
                    dve.scalar_tensor_tensor(gainT[:, j, :, s], modT[:, 3 * j + 1, :, s], 1.0, cols[:, r:r + KD], ALU.add, ALU.mult)
                last = dve.tensor_scalar(gateT[:, j, :, :], modT[:, 3 * j + 2, :, :], 1.0 if j == 1 else 0.5, None, ALU.mult)
            last.then_inc(gain_set, 1)

            dve.wait_ge(gain_set, 1)
            dve.wait_ge(x_even, NKT)
            norm_dve(N1, ALL, 0)
            dve.wait_ge(const_in, 2 * 16)
            dve.wait_ge(a_saved, 16)
            dve.tensor_copy(identR[:, :], ident[:, :])
            dve.tensor_copy(maskR[:, :, :], mask_f[:, :, :])
            dve.tensor_copy(altR[:, :], alt_f[:, :]).then_inc(consts_set, 1)
            dve.memset(sink_f[:, :, 1:2], NEG)
            dve.tensor_copy(sink_f[:, :, 0], sink_r[:, :]).then_inc(cols_set, 1)
            dve.wait_ge(cols_set, 2)
            dve.tensor_copy(sinkH[:, :, :], sink_f[:, :, :]).then_inc(cols_set, 1)
            dve.wait_ge(cols_set, 3)
            dve.tensor_tensor(sinkL[:, :, :], sink_f[:, :, :], sinkH[:, :, :].bitcast(F32), ALU.subtract).then_inc(cols_set, 1)
            dve.tensor_copy(onesR[:, :], ones[:, :])
            dve.wait_ge(cols_set, 4)
            dve.tensor_scalar(sink_f[:, :, :], sinkH[:, :, :].bitcast(F32), ident[:, 0:1], None, ALU.mult).then_inc(cols_set, 1)
            dve.wait_ge(cols_set, 5)
            dve.scalar_tensor_tensor(sinkR[:, :, :], sinkL[:, :, :].bitcast(F32), ident[:, 1:2], sink_f[:, :, :], ALU.mult, ALU.add).then_inc(cols_set, 1)

            ffn_dve(F1, ALL, PAN_FFN1, FIL_FFN1, 0)
            dve.wait_ge(F1["acc"], 4 + 24 * NPAIR)
            norm_dve_rstd(N2, ALL, ORDER["n2"])
            norm_dve(N2, ALL, 1, between=lambda: split_lo(1, PAN_FOU + 2))

            dve.wait_ge(x_saved, 16)

            def u_low(g):
                for b in range(2):
                    dve.wait_ge(u_hi, g * 2 + b + 1)
                    w = slice(b * NT, (b + 1) * NT)
                    dve.tensor_tensor(uL[g % 2][:, w], ps[:, 2 * (g % 2) + b, :], uH[g % 2][:, w].bitcast(F32), ALU.subtract).then_inc(u_lo, 1)

            def xc_low(g):
                for n in range(NB):
                    dve.wait_ge(xc_hi, g * NB + n + 1)
                    dve.tensor_tensor(xcL[:, g, n, :], ps[:, 4 + n % 4, 0:2 * P], xcH[:, g, n, :].bitcast(F32), ALU.subtract).then_inc(xc_lo, 1)

            def fou_split(p):
                split_lo(p % 2, PAN_FOU + p + 1)
            u_low(0)
            dve.wait_ge(chan_hi, 1)
            dve.tensor_tensor(chanL[:, :], chan_f[:, :], chanH[:, :].bitcast(F32), ALU.subtract).then_inc(chan_lo, 1)
            fou_split(2)
            u_low(1)
            xc_low(0)
            fou_split(3)
            u_low(2)
            xc_low(1)
            fou_split(4)
            u_low(3)
            xc_low(2)
            fou_split(5)
            xc_low(3)
            for n in range(NB - 1):
                fou_split(NG + n + 2)
            for g in range(NG):
                dve.wait_ge(fb_out, g + 1)
                if g > 0:
                    dve.wait_ge(f_lo, g)
                dve.tensor_tensor(fT[:, 1:NT], ps[:, 2 * g, 1:NT], fB[:, 1:NT], ALU.subtract)
                dve.tensor_tensor(fT[:, SEQ - 1:NT:-1], ps[:, 2 * g, 1:NT], fB[:, 1:NT], ALU.add)
                dve.tensor_copy(fT[:, NT:NT + 1], fB[:, 0:1])
                dve.tensor_copy(fT[:, 0:1], ps[:, 2 * g, 0:1]).then_inc(f_sum, 1)
                dve.wait_ge(f_hi, g + 1)
                dve.tensor_tensor(fL[g % 2][:, :], fT[:, :], fH[g % 2][:, :].bitcast(F32), ALU.subtract).then_inc(f_lo, 1)

            def rotate(s, z, t0, n, lat):
                if lat:
                    by_cos = dve.tensor_tensor(rot[z % 2][:, 0:n], ps[:, s, 0:n], cosT[:, t0:t0 + n], ALU.mult).then_inc(cos_mul, 1)
                    dve.stream_shuffle(swp[z % 2][:, 0:n], ps[:, s, 0:n], [i ^ 1 for i in range(32)]).then_inc(swapped, 1)
                    return by_cos
                return dve.tensor_copy(rot[z % 2][:, 0:n], ps[:, s, 0:n])

            dve.wait_ge(rope_in, 32)
            for n in range(4):
                split_lo((n + 1) % 2, PAN_KV + n + 2)
                if n >= 2:
                    continue
                for b, (_, _, _, t0, m, _, _) in enumerate(ALL):
                    z = 3 * n + b
                    dve.wait_ge(psum_filled, FIL_KV + z + 1)
                    if z >= 2:
                        dve.wait_ge(k_lo, z - 1)
                    if b < 2:
                        rotate(3 * n + b, z, t0, m, True)
                        dve.wait_ge(cos_mul, 2 * n + b + 1)
                        dve.wait_ge(sin_mul, 2 * n + b + 1)
                        dve.tensor_tensor(rot[z % 2][:, 0:m], rot[z % 2][:, 0:m], swp[z % 2][:, 0:m], ALU.add).then_inc(rot_set, 1)
                    else:
                        rotate(3 * n + b, z, t0, m, False).then_inc(rot_set, 1)
                    dve.wait_ge(k_hi, z + 1)
                    dve.tensor_tensor(kL[z % 2][:, 0:m], rot[z % 2][:, 0:m], kH[z % 2][:, 0:m].bitcast(F32), ALU.subtract).then_inc(k_lo, 1)
            for e in range(6):
                vc, g0 = e // 3, 4 * (e % 3)
                w = min(4, NKT - g0)
                dve.wait_ge(v_hi, e + 1)
                dve.tensor_tensor(vS[vc][:, :, g0:g0 + w, 1, :], ps[:, 6 + e % 2, 0:w * P].rearrange("p (t v e) -> p v t e", v=2, e=HEAD),
                                  vS[vc][:, :, g0:g0 + w, 0, :].bitcast(F32), ALU.subtract).then_inc(v_lo, 1)

            dve.wait_ge(k_saved[1], 32 * 3)
            dve.wait_ge(k_saved[0], 32 * 3)
            dve.wait_ge(v_saved, 32)

            def q_rotate(g, pj, b, bank):
                dve.wait_ge(psum_filled, g * 4 + (FIL_ATT + 2 * pj + b + 1))
                rotate(bank, b, b * NT, NT, True)

            def q_add(g, pj, b):
                dve.wait_ge(cos_mul, g * 4 + (4 + 2 * pj + b + 1))
                dve.wait_ge(sin_mul, g * 4 + (4 + 2 * pj + b + 1))
                dve.tensor_tensor(rot[b][:, :], rot[b][:, :], swp[b][:, :], ALU.add).then_inc(rot_set, 1)

            def q_low(g, pj, b):
                for h in range(2):
                    r, o_ = slice(HEAD * h, HEAD * (h + 1)), slice(HEAD * (1 - h), HEAD * (2 - h))
                    w = slice(b * NT, (b + 1) * NT)
                    dve.wait_ge(q_hi, g * 8 + (4 * pj + 2 * b + h + 1))
                    dve.scalar_tensor_tensor(qS[pj % 2][h][o_, w], rot[b][r, :], HEAD ** -0.5, qS[pj % 2][h][r, w].bitcast(F32),
                                             ALU.mult, ALU.subtract).then_inc(q_lo, 1)

            def maxi(g, pj, b, h):
                dve.wait_ge(qk_done, g * (4 * NB) + ((pj * NB + b) * 2 + h + 1))
                n = len(KEYS[b]) * P + 2
                dve.tensor_reduce(nmax[:, 2 * (b % 2) + h:2 * (b % 2) + h + 1],
                                  ps[:, 2 * h:2 * h + 2, :].rearrange("p a n -> p (a n)")[:, 0:n], AX.X, ALU.max,
                                  negate=True).then_inc(max_set, 1)

            def recip(g, pj, b, h):
                dve.wait_ge(exp_set, g * (4 * NB) + (2 + (pj * NB + b) * 2 + h + 1))
                z = slice(2 * (b % 2) + h, 2 * (b % 2) + h + 1)
                dve.reciprocal(rsum[:, z], lsum[:, z]).then_inc(rsum_set, 1)

            def turned_lo(g, pl, b, e):
                if e >= GROUPS[b]:
                    return
                w = min(NT, 2 * len(KEYS[b]) * P - NT * e)
                dve.wait_ge(pt_hi, g * (2 * NGROUP) + (pl * NGROUP + GROUP0[b] + e + 1))
                dve.tensor_tensor(ptL[b % 2][:, NT * e:NT * e + w], ps[:, 4 + (GROUP0[b] + e) % 2, 0:w],
                                  ptH[b % 2][:, NT * e:NT * e + w].bitcast(F32), ALU.subtract).then_inc(pt_lo, 1)

            def out(g, pl, b):
                dve.wait_ge(o_low, g * (2 * NB) + (pl * NB + b + 1))
                for h in range(2):
                    last = dve.tensor_tensor(aT[HEAD * h:HEAD * (h + 1), b * P:(b + 1) * P], ps[0:HEAD, 7, h * P:(h + 1) * P],
                                             oLow[b % 2][:, h, :], ALU.add)
                last.then_inc(o_out, 1)

            def out_lo(g, pl, half):
                w = slice(half * NT, (half + 1) * NT)
                dve.wait_ge(a_hi, g * 4 + (2 * pl + half + 1))
                dve.tensor_tensor(aL[:, w], aT[:, w], aH[:, w].bitcast(F32), ALU.subtract).then_inc(a_lo, 1)

            def pair(g, pl, last):
                for b in range(NB):
                    nxt = (pl, b + 1) if b + 1 < NB else (pl + 1, 0)
                    more = not (last and b == NB - 1)
                    more = more and nxt != (2, 0)
                    if b == 0:
                        q_add(g, pl, 1)
                    if b == 4 and not last:
                        q_add(g, pl + 1, 0)
                    if more:
                        maxi(g, *nxt, 0)
                    turned_lo(g, pl, b, 0)
                    if more:
                        maxi(g, *nxt, 1)
                    turned_lo(g, pl, b, 1)
                    if more:
                        recip(g, *nxt, 0)
                    turned_lo(g, pl, b, 2)
                    if more:
                        recip(g, *nxt, 1)
                    if b >= 1:
                        out(g, pl, b - 1)
                    if b == 1:
                        q_low(g, pl, 1)
                    if b == 3 and not last:
                        q_rotate(g, pl + 1, 0, 6)
                    if b == 5 and not last:
                        q_low(g, pl + 1, 0)
                    if b == 6 and not last:
                        split_lo(pl, g * 2 + (PAN_ATT + pl + 3))
                    if b == 7:
                        out_lo(g, pl, 0)
                out(g, pl, NB - 1)
                if pl == 1 and not last:
                    for h in range(2):
                        maxi(g, 2, 0, h)
                    for h in range(2):
                        recip(g, 2, 0, h)
                if not last:
                    q_rotate(g, pl + 1, 1, 6)
                out_lo(g, pl, 1)

            split_lo(1, PAN_ATT + 2)
            q_rotate(0, 0, 0, 6)
            q_add(0, 0, 0)
            q_low(0, 0, 0)
            q_rotate(0, 0, 1, 7)
            maxi(0, 0, 0, 0)
            maxi(0, 0, 0, 1)
            recip(0, 0, 0, 0)
            recip(0, 0, 0, 1)
            with dve.Fori(0, NKV - 1) as g:
                for pl in range(2):
                    pair(g, pl, False)
            for pl in range(2):
                pair(NKV - 1, pl, pl == 1)

            def one(t, d, b):
                return t[:, bass.ds(d, 1), b * NT:(b + 1) * NT].rearrange("p a n -> p (a n)")

            with dve.Fori(0, KD) as d:
                split_lo(1, d * 2 + (PAN_MRG + 2))
                split_lo(0, d * 2 + (PAN_MRG + 3))
                for b in range(2):
                    dve.wait_ge(psum_filled, d * 4 + (FIL_MRG + 2 + b + 1))
                    dve.wait_ge(sgf, d * 2 + (2 + b + 1))
                    dve.tensor_tensor(one(y, d, b), ps[:, 2 + b, :], one(y, d, b), ALU.mult).then_inc(yf, 1)
            with dve.Fori(0, KD // 2) as i:
                for n in range(2):
                    split_lo((n + 1) % 2, i * 2 + (PAN_MRG + 2 * KD + n + 2))

            dve.wait_ge(yf, 2 + 2 * KD)

            def merged(i, n):
                for b in range(2):
                    dve.wait_ge(psum_filled, i * 4 + (FIL_MRG + 6 * KD + 2 * n + b + 1))
                    dve.wait_ge(sga, i * 4 + (4 + 2 * n + b + 1))
                    ga = one(gate_a, i * 2 + n, b)
                    dve.tensor_tensor(ga, ps[:, 2 * n + b, :], ga, ALU.mult).then_inc(ya, 1)
                dve.wait_ge(ya, i * 4 + (4 + 2 * n + 2))
                yd, ga = (t[:, bass.ds(i * 2 + n, 1), :].rearrange("p a n -> p (a n)") for t in (y, gate_a))
                dve.tensor_tensor(yd, yd, ga, ALU.add).then_inc(ysum, 1)
                dve.wait_ge(y_hi, i * 2 + (n + 1))
                if isinstance(i, int):
                    hi, lo = mergedH[2 * i + n], mergedL[2 * i + n]
                else:
                    hi, lo = (t[:, bass.ds(i * 2 + n, 1), :].rearrange("p a n -> p (a n)") for t in (Yh, Yl))
                dve.tensor_tensor(lo, yd, hi.bitcast(F32), ALU.subtract).then_inc(y_lo, 1)

            with dve.Fori(0, KD // 2 - 1) as i:
                for n in range(2):
                    split_lo((n + 1) % 2, i * 2 + (PAN_MRG + 3 * KD + n + 2))
                    merged(i, n)
            for n in range(2):
                split_lo((n + 1) % 2, PAN_MRG + 4 * KD - 2 + n + 2)
                merged(KD // 2 - 1, n)

            for k in range(KD):
                dve.tensor_scalar(gdiag[:, k, :], ident[:, :], cols[:, ROW_GF + k:ROW_GF + k + 1], None, ALU.mult).then_inc(N4["dg"], 1)
            with dve.Fori(0, KD // 2) as i:
                for n in range(2):
                    split_lo((n + 1) % 2, i * 2 + (PAN_OUT + n + 2))
                    for b in range(2):
                        dve.wait_ge(psum_filled, i * 4 + (FIL_OUT + 2 * n + b + 1))
                        dve.wait_ge(x_back, 16 * KD)
                        xd = x_lat[:, bass.ds(i * 2 + n, 1), b * NT:(b + 1) * NT].rearrange("p a n -> p (a n)")
                        gt = gateT[:, 1, bass.ds(i * 2 + n, 1), 0:1].rearrange("p a n -> p (a n)")
                        dve.scalar_tensor_tensor(xd, ps[:, 4 + 2 * n + b, :], gt, xd, ALU.mult, ALU.add).then_inc(x_res, 1)
            dve.wait_ge(x_res, 4 + 2 * KD)
            norm_dve_rstd(N3, LAT, ORDER["n3"])
            norm_dve(N3, LAT, 2)
            ffn_dve(F2, LAT, PAN_FFN2, FIL_FFN2, 2, last=True)
            dve.wait_ge(F2["acc"], 4 + 16 * NPAIR)
            norm_dve_rstd(N4, LAT, ORDER["n4"], last=True)
            for t in range(NB):
                dve.wait_ge(o_turned, 2 * t + 2)
                if t >= 2:
                    dve.wait_ge(stored[t % 2], 16 * (t // 2))
                dve.tensor_scalar(orow[t % 2][:, NT:D], ps[:, 2 * (t % 2) + 1, :], rinv[:, 2 * t:2 * t + 1], None, ALU.mult).then_inc(o_odd, 1)

        @block.gpsimd
        def _(pool):
            for z, (s, n) in enumerate(CREDIT):
                pool.memset(dummy[:, z:z + 1], 0.0).then_inc(s, n)

            def norm_pool(S, blocks, j):
                for b in range(len(blocks)):
                    for k in range(1, KD, 2):
                        low_of(pool, S, blocks, j, b, k)

            adds(pool, "pool", N1, ORDER["n1"], ALL)
            norm_pool(N1, ALL, 0)
            adds(pool, "pool", N2, ORDER["n2"], ALL)
            pool.wait_ge(F1["acc"], 4 + 24 * NPAIR)
            pool.dma_start(x_scr, x_lat[:, :, :]).then_inc(x_saved, 16)
            pool.dma_start(cosT[:, :], T["rope_cos"]).then_inc(rope_in, 16)
            pool.dma_start(sinT[:, :], T["rope_sin"]).then_inc(rope_in, 16)
            norm_pool(N2, ALL, 1)
            low_parts(pool, N2, 2)
            pool.dma_start(chan_f[:, :], T["dft_chan"]).then_inc(chan_in, 16)
            for g in range(NG):
                pool.wait_ge(f_lo, g + 1)
                for z, part in enumerate((fH, fL)):
                    pool.dma_start(f_scr[g, z, :, :], part[g % 2][:, :]).then_inc(f_saved[g % 2], 16)

            def sine(z, n, t0):
                pool.tensor_tensor(swp[z % 2][:, 0:n], swp[z % 2][:, 0:n], sinT[:, t0:t0 + n], ALU.mult).then_inc(sin_mul, 1)

            pool.wait_ge(rope_in, 32)
            for n in range(2):
                for b, (_, _, _, t0, m, _, g0) in enumerate(ALL):
                    z = 3 * n + b
                    if b < 2:
                        pool.wait_ge(swapped, 2 * n + b + 1)
                        sine(z, m, t0)
                    pool.wait_ge(k_lo, z + 1)
                    for q, part in enumerate((kH, kL)):
                        pool.dma_start(k_scr[q, n * P:(n + 1) * P, g0:g0 + m], part[z % 2][:, 0:m]).then_inc(k_saved[z % 2], 16)
            for vc in range(2):
                pool.wait_ge(v_lo, 3 * vc + 3)
                pool.dma_start(v_scr[:, 2 * vc:2 * vc + 2, :].rearrange("p v n -> p (v n)"),
                               vS[vc][:, :, :, :, :].rearrange("p v t z e -> p (v t z e)")).then_inc(v_saved, 16)

            pool.wait_ge(v_saved, 32)
            for s in range(2):
                pool.wait_ge(k_saved[s], 32 * 3)

            def q_sine(g, pj, b):
                pool.wait_ge(swapped, g * 4 + (4 + 2 * pj + b + 1))
                sine(b, NT, b * NT)

            def diagonal(g, pj, b, h):
                pool.wait_ge(rsum_set, g * (4 * NB) + ((pj * NB + b) * 2 + h + 1))
                z = slice(2 * (b % 2) + h, 2 * (b % 2) + h + 1)
                pool.tensor_tensor(dg[b % 2][h][:, :], ident[:, :], rsum[:, z].to_broadcast([P, P]), ALU.mult).then_inc(prob_set, 1)

            def pair(g, pl, last):
                for b in range(NB):
                    nxt = (pl, b + 1) if b + 1 < NB else (pl + 1, 0)
                    if not (last and b == NB - 1):
                        diagonal(g, *nxt, 0)
                        diagonal(g, *nxt, 1)
                    if b == 3 and not last:
                        q_sine(g, pl + 1, 0)
                if not last:
                    q_sine(g, pl + 1, 1)

            q_sine(0, 0, 0)
            q_sine(0, 0, 1)
            diagonal(0, 0, 0, 0)
            diagonal(0, 0, 0, 1)
            with pool.Fori(0, NKV - 1) as g:
                for pl in range(2):
                    pair(g, pl, False)
            for pl in range(2):
                pair(NKV - 1, pl, pl == 1)

            pool.wait_ge(a_saved, 16 + 32 * KD)
            pool.wait_ge(pv_done, 1 + 2 * NB * NKV)

            def att_back(k, loaded):
                for z, part in enumerate((attH, attL)):
                    pool.dma_start(part[k][:, :], a_scr[k, z]).then_inc(loaded, 16)
            for k in range(2):
                att_back(k, att_in)
            pool.wait_ge(psum_filled, FIL_MRG + 4 * KD)
            for k in range(2, 6):
                att_back(k, att_in)
            pool.wait_ge(psum_filled, FIL_MRG + 6 * KD)
            for k in range(6, KD):
                att_back(k, att_in_late)
            for d in range(KD):
                pool.wait_ge(y_lo, d + 1)
                pool.dma_start(x_lat[:, d, :], x_scr[:, d, :]).then_inc(x_back, 16)
            adds(pool, "pool", N3, ORDER["n3"], LAT)
            norm_pool(N3, LAT, 2)
            adds(pool, "pool", N4, ORDER["n4"], LAT)


_INS = {"x": (SEQ, D), "c": (D,), "ctx": (CTX, D), "c_ctx": (D,), "w_ada": (D, NMOD * D), "b_ada": (NMOD * D,),
        "g_ffn1": (D,), "w_ffn1_in": (D, 2 * FF), "w_ffn1_out": (FF, D), "g_mix": (D,), "w_in": (D, 4 * D),
        "attn_sink": (16,), "w_attn_branch": (D, D), "w_fourier_branch": (NG * P, D), "w_out": (D, D),
        "g_ffn2": (D,), "w_ffn2_in": (D, 2 * FF), "w_ffn2_out": (FF, D), "g_final": (D,)}


def shape_tables():
    import numpy as np
    i = np.arange(P)
    masks = np.zeros((P, 2, P), np.float32)
    masks[:, 0, :] = np.where(i[None, :] >= i[:, None], 0.0, NEG)
    masks[:, 1, :] = np.where(i[None, :] <= i[:, None], 0.0, NEG)
    alt = np.zeros((P, 2), np.float32)
    alt[:, 0] = 1.0 - 2.0 * (i % 2)
    rows = np.repeat(np.arange(SEQ // 64, dtype=np.float32), 64)
    colm = np.tile(np.arange(64, dtype=np.float32), SEQ // 64)
    inv = np.power(np.float32(10000.0), -np.arange(0, 32, 2, dtype=np.float32) / np.float32(32)).astype(np.float32)
    ang = np.concatenate([rows[:, None] * inv, colm[:, None] * inv], axis=-1).astype(np.float32).astype(np.float64)
    feat = (i % HEAD) // 2
    cos = np.cos(ang).T[feat].astype(np.float32)
    sin = (np.sin(ang).T[feat] * np.where(i % 2 == 0, -1.0, 1.0)[:, None]).astype(np.float32)
    chan = np.zeros((P, 2 * P), np.float64)
    a = 2 * np.pi * ((i[:, None] * i[None, :]) % P) / P
    chan[:, 0:P], chan[:, P:2 * P] = np.cos(a), np.sin(a)
    chan /= np.sqrt(float(SEQ * P))
    n, k = np.arange(SEQ), np.arange(NT)
    a = 2 * np.pi * ((n[:, None] * k[None, :]) % SEQ) / SEQ
    pos = np.concatenate([np.cos(a), np.sin(a)], axis=1)
    return {"ident": np.eye(P, dtype=np.float32), "masks": masks, "alt": alt, "rope_cos": cos, "rope_sin": sin,
            "dft_chan": chan.astype(np.float32), "dft_pos": pos.astype(np.float32)}


def kernel(**inputs):
    import numpy as _np
    import concourse.bacc as _bacc
    from concourse import mybir as _mybir
    from concourse.bass_utils import run_bass_kernel_spmd as _run

    nc = _bacc.Bacc("TRN2", target_bir_lowering=False, num_devices=1)
    arrays, T = {}, {}
    tensors = {name: _np.ascontiguousarray(inputs[name]).reshape(shape) for name, shape in _INS.items()}
    tensors.update(shape_tables())
    for name, a in tensors.items():
        arrays[f"in_{name}_dram"] = a
        T[name] = nc.dram_tensor(f"in_{name}_dram", a.shape, _mybir.dt.from_np(a.dtype), kind="ExternalInput").ap()
    T["out"] = nc.dram_tensor("out_0_dram", (SEQ, D), _mybir.dt.float32, kind="ExternalOutput").ap()
    build(nc, T)
    r = _run(nc, [arrays], core_ids=[0])
    return r.results[0]["out_0_dram"].reshape(1, SEQ, D)
```
